# Optimizing a Trainium2 kernel written in Bass

```python
import math, functools
import jax, jax.numpy as jnp
from jax import lax
import numpy as np

D_MODEL = 1024
BATCH = 1
SEQ = 512
DEPTH = 2

CHUNK = 64
N_MIXERS = 4
HEAD_DIM = 64
ROT_DIM = HEAD_DIM // 4
ROPE_THETA = 500000.0
NORM_EPS = 1e-6
QBLK = 128
NEG_INF = -1e30

A_HEADS = D_MODEL // HEAD_DIM
A_KV_HEADS = 4
WINDOW = 128
WIN_CHUNKS = WINDOW // CHUNK
B_HEADS = D_MODEL // (2 * HEAD_DIM)
C_HEADS = D_MODEL // HEAD_DIM
C_LOOKBACK = 8
MAX_REL = 256
D_HEADS = D_MODEL // HEAD_DIM
D_KV_HEADS = 4
IDX_HEADS = 8
IDX_DIM = 64
TOPK_MAX = 256
D_FF = 2816
CONV_W = 3

A_IN = (A_HEADS + 2 * A_KV_HEADS) * HEAD_DIM
B_IN = 3 * B_HEADS * 2 * HEAD_DIM
C_IN = 3 * C_HEADS * HEAD_DIM
D_IN = (D_HEADS + 2 * D_KV_HEADS) * HEAD_DIM + IDX_HEADS * IDX_DIM + IDX_DIM + IDX_HEADS

kernel_name = 'hybrid_chunk_causal_interleaved_trunk'

def rms_norm(x, gain):
    xf = x.astype(jnp.float32)
    y = xf * lax.rsqrt(jnp.mean(xf * xf, axis=-1, keepdims=True) + NORM_EPS)
    return (y * gain.astype(jnp.float32)).astype(x.dtype)

def rope_tables(positions):
    inv_freq = jnp.power(ROPE_THETA, -jnp.arange(0, ROT_DIM, 2, dtype=jnp.float32) / ROT_DIM)
    ang = positions.astype(jnp.float32)[..., None] * inv_freq
    return jnp.cos(ang)[:, :, None, :], jnp.sin(ang)[:, :, None, :]

def apply_partial_rope(x, cos, sin):
    half = ROT_DIM // 2
    xr = x[..., :ROT_DIM].astype(jnp.float32)
    x1, x2 = xr[..., :half], xr[..., half:]
    rot = jnp.concatenate([x1 * cos - x2 * sin, x2 * cos + x1 * sin], axis=-1)
    return jnp.concatenate([rot.astype(x.dtype), x[..., ROT_DIM:]], axis=-1)

def chunk_band(x, n_chunks):
    nc = x.shape[0] // CHUNK
    xc = x.reshape((nc, CHUNK) + x.shape[1:])
    xp = jnp.pad(xc, [(n_chunks - 1, 0)] + [(0, 0)] * (xc.ndim - 1))
    idx = jnp.arange(nc)[:, None] + jnp.arange(n_chunks)[None, :]
    return xp[idx].reshape((nc, n_chunks * CHUNK) + x.shape[1:])

def band_valid(nc, n_chunks):
    src = jnp.arange(nc)[:, None] - (n_chunks - 1) + jnp.arange(n_chunks)[None, :]
    return jnp.repeat(src >= 0, CHUNK, axis=1)

def to_blocks(x):
    b, s = x.shape[:2]
    return jnp.moveaxis(x.reshape((b, s // QBLK, QBLK) + x.shape[2:]), 1, 0)

def from_blocks(y):
    nb, b, q = y.shape[:3]
    return jnp.moveaxis(y, 0, 1).reshape((b, nb * q) + y.shape[3:])

def sliding_sink_attention(h, w_in, sinks, w_out, cos, sin):
    b, s, _ = h.shape
    nc = s // CHUNK
    g = A_HEADS // A_KV_HEADS
    q, k, v = jnp.split(h @ w_in, [A_HEADS * HEAD_DIM, (A_HEADS + A_KV_HEADS) * HEAD_DIM], axis=-1)
    q = apply_partial_rope(q.reshape(b, s, A_HEADS, HEAD_DIM), cos, sin)
    k = apply_partial_rope(k.reshape(b, s, A_KV_HEADS, HEAD_DIM), cos, sin)
    v = v.reshape(b, s, A_KV_HEADS, HEAD_DIM)
    qc = q.reshape(b, nc, CHUNK, A_KV_HEADS, g, HEAD_DIM)
    band = functools.partial(chunk_band, n_chunks=WIN_CHUNKS)
    kb = jax.vmap(band)(k)
    vb = jax.vmap(band)(v)
    sc = jnp.einsum('bcqhgd,bckhd->bchgqk', qc, kb, preferred_element_type=jnp.float32) * HEAD_DIM ** -0.5
    valid = band_valid(nc, WIN_CHUNKS)[None, :, None, None, None, :]
    sc = jnp.where(valid, sc, NEG_INF)
    sink = jnp.broadcast_to(sinks.astype(jnp.float32).reshape(1, 1, A_KV_HEADS, g, 1, 1), sc.shape[:-1] + (1,))
    p = jax.nn.softmax(jnp.concatenate([sc, sink], axis=-1), axis=-1)[..., :-1]
    o = jnp.einsum('bchgqk,bckhd->bcqhgd', p.astype(v.dtype), vb)
    return o.reshape(b, s, A_HEADS * HEAD_DIM) @ w_out

def differential_attention(h, w_in, lam_q1, lam_k1, lam_q2, lam_k2, subln, w_out, cos, sin, lambda_init):
    b, s, _ = h.shape
    q, k, v = jnp.split(h @ w_in, 3, axis=-1)
    q = apply_partial_rope(q.reshape(b, s, B_HEADS * 2, HEAD_DIM), cos, sin).reshape(b, s, B_HEADS, 2, HEAD_DIM)
    k = apply_partial_rope(k.reshape(b, s, B_HEADS * 2, HEAD_DIM), cos, sin).reshape(b, s, B_HEADS, 2, HEAD_DIM)
    v = v.reshape(b, s, B_HEADS, 2 * HEAD_DIM)
    f32 = jnp.float32
    lam = (jnp.exp(jnp.sum(lam_q1.astype(f32) * lam_k1.astype(f32)))
           - jnp.exp(jnp.sum(lam_q2.astype(f32) * lam_k2.astype(f32))) + lambda_init)
    kchunk = jnp.arange(s) // CHUNK
    scale = HEAD_DIM ** -0.5

    def block(args):
        qb, n = args
        sc = jnp.einsum('bqhmd,bkhmd->bhmqk', qb, k, preferred_element_type=f32) * scale
        qchunk = (n * QBLK + jnp.arange(QBLK)) // CHUNK
        sc = jnp.where(kchunk[None, :] <= qchunk[:, None], sc, NEG_INF)
        p = jax.nn.softmax(sc, axis=-1)
        a = p[:, :, 0] - lam * p[:, :, 1]
        return jnp.einsum('bhqk,bkhe->bqhe', a.astype(v.dtype), v)

    o = from_blocks(lax.map(block, (to_blocks(q), jnp.arange(s // QBLK))))
    o = rms_norm(o, subln) * (1.0 - lambda_init)
    return o.reshape(b, s, B_HEADS * 2 * HEAD_DIM) @ w_out

def chunked_relpos_attention(h, w_in, rel_bias, w_out):
    b, s, _ = h.shape
    nc = s // CHUNK
    nband = C_LOOKBACK + 1
    q, k, v = [t.reshape(b, s, C_HEADS, HEAD_DIM) for t in jnp.split(h @ w_in, 3, axis=-1)]
    qpos = jnp.arange(CHUNK)[:, None]
    kpos = jnp.arange(nband * CHUNK)[None, :]
    rel = jnp.clip(C_LOOKBACK * CHUNK + qpos - kpos, -MAX_REL, MAX_REL) + MAX_REL
    bias = rel_bias.astype(jnp.float32)[:, rel]
    valid = band_valid(nc, nband)[:, None, None, :]
    scale = HEAD_DIM ** -0.5

    def one_sequence(args):
        qs, ks, vs = args
        qc = qs.reshape(nc, CHUNK, C_HEADS, HEAD_DIM)
        kb = chunk_band(ks, nband)
        vb = chunk_band(vs, nband)
        sc = jnp.einsum('cqhd,ckhd->chqk', qc, kb, preferred_element_type=jnp.float32) * scale + bias
        sc = jnp.where(valid, sc, NEG_INF)
        p = jax.nn.softmax(sc, axis=-1)
        o = jnp.einsum('chqk,ckhd->cqhd', p.astype(vs.dtype), vb)
        return o.reshape(s, C_HEADS * HEAD_DIM)

    o = lax.map(one_sequence, (q, k, v))
    return o @ w_out

def dsa_attention(h, w_in, idx_knorm, w_out, cos, sin):
    b, s, _ = h.shape
    g = D_HEADS // D_KV_HEADS
    topk = min(TOPK_MAX, s // 4)
    o1 = D_HEADS * HEAD_DIM
    o2 = o1 + D_KV_HEADS * HEAD_DIM
    o3 = o2 + D_KV_HEADS * HEAD_DIM
    o4 = o3 + IDX_HEADS * IDX_DIM
    o5 = o4 + IDX_DIM
    q, k, v, iq, ik, iw = jnp.split(h @ w_in, [o1, o2, o3, o4, o5], axis=-1)
    q = apply_partial_rope(q.reshape(b, s, D_HEADS, HEAD_DIM), cos, sin).reshape(b, s, D_KV_HEADS, g, HEAD_DIM)
    k = apply_partial_rope(k.reshape(b, s, D_KV_HEADS, HEAD_DIM), cos, sin)
    v = v.reshape(b, s, D_KV_HEADS, HEAD_DIM)
    iq = apply_partial_rope(iq.reshape(b, s, IDX_HEADS, IDX_DIM), cos, sin)
    ik = apply_partial_rope(rms_norm(ik, idx_knorm).reshape(b, s, 1, IDX_DIM), cos, sin)[:, :, 0]
    iw = iw.astype(jnp.float32) * IDX_HEADS ** -0.5
    kchunk = jnp.arange(s) // CHUNK
    gather = jax.vmap(lambda t, i: t[i])
    scale = HEAD_DIM ** -0.5

    def block(args):
        qb, iqb, iwb, n = args
        qchunk = (n * QBLK + jnp.arange(QBLK)) // CHUNK
        logits = jnp.einsum('bqhd,bkd->bqhk', iqb, ik, preferred_element_type=jnp.float32) * IDX_DIM ** -0.5
        score = jnp.einsum('bqh,bqhk->bqk', iwb, jax.nn.relu(logits))
        score = jnp.where(kchunk[None, None, :] <= qchunk[None, :, None], score, NEG_INF)
        _, sel = lax.top_k(score, topk)
        sel_valid = (sel // CHUNK) <= qchunk[None, :, None]
        ks = gather(k, sel)
        vs = gather(v, sel)
        sc = jnp.einsum('bqhgd,bqkhd->bhgqk', qb, ks, preferred_element_type=jnp.float32) * scale
        sc = jnp.where(sel_valid[:, None, None], sc, NEG_INF)
        p = jax.nn.softmax(sc, axis=-1)
        return jnp.einsum('bhgqk,bqkhd->bqhgd', p.astype(vs.dtype), vs)

    o = from_blocks(lax.map(block, (to_blocks(q), to_blocks(iq), to_blocks(iw), jnp.arange(s // QBLK))))
    return o.reshape(b, s, D_HEADS * HEAD_DIM) @ w_out

def conv_ffn(h, w_up, conv_w, conv_b, w_down):
    a, gate = jnp.split(h @ w_up, 2, axis=-1)
    a = lax.conv_general_dilated(a, conv_w[:, None, :], window_strides=(1,), padding=[(CONV_W - 1, 0)],
                                 dimension_numbers=('NWC', 'WIO', 'NWC'), feature_group_count=D_FF) + conv_b
    return (jax.nn.silu(a) * gate) @ w_down

def _n_layers_of(kind):
    return len(range(kind, DEPTH, N_MIXERS))

def setup_inputs(seed: int = 0) -> dict:
    key = jax.random.key(seed)
    ks = iter(jax.random.split(key, 32))
    f32 = jnp.float32

    def w(shape, fan_in):
        return jax.random.normal(next(ks), shape, f32) * fan_in ** -0.5

    def gain(shape):
        return 1.0 + 0.02 * jax.random.normal(next(ks), shape, f32)

    def small(shape, sc):
        return sc * jax.random.normal(next(ks), shape, f32)

    na, nb, nc, nd = (_n_layers_of(i) for i in range(N_MIXERS))
    x = jax.random.normal(next(ks), (BATCH, SEQ, D_MODEL), f32)
    offset = jax.random.randint(next(ks), (BATCH, 1), 0, 4096, dtype=jnp.int32)
    positions = (offset + jnp.arange(SEQ, dtype=jnp.int32)[None, :]).astype(jnp.int32)
    return {
        'x': x,
        'positions': positions,
        'attn_norm': gain((DEPTH, D_MODEL)),
        'ffn_norm': gain((DEPTH, D_MODEL)),
        'ffn_w_up': w((DEPTH, D_MODEL, 2 * D_FF), D_MODEL),
        'ffn_conv_w': w((DEPTH, CONV_W, D_FF), CONV_W),
        'ffn_conv_b': small((DEPTH, D_FF), 0.02),
        'ffn_w_down': w((DEPTH, D_FF, D_MODEL), D_FF),
        'a_w_in': w((na, D_MODEL, A_IN), D_MODEL),
        'a_sinks': small((na, A_HEADS), 0.5),
        'a_w_out': w((na, A_HEADS * HEAD_DIM, D_MODEL), A_HEADS * HEAD_DIM),
        'b_w_in': w((nb, D_MODEL, B_IN), D_MODEL),
        'b_lam_q1': small((nb, HEAD_DIM), 0.1),
        'b_lam_k1': small((nb, HEAD_DIM), 0.1),
        'b_lam_q2': small((nb, HEAD_DIM), 0.1),
        'b_lam_k2': small((nb, HEAD_DIM), 0.1),
        'b_subln': gain((nb, 2 * HEAD_DIM)),
        'b_w_out': w((nb, B_HEADS * 2 * HEAD_DIM, D_MODEL), B_HEADS * 2 * HEAD_DIM),
        'c_w_in': w((nc, D_MODEL, C_IN), D_MODEL),
        'c_rel_bias': small((nc, C_HEADS, 2 * MAX_REL + 1), 0.1),
        'c_w_out': w((nc, C_HEADS * HEAD_DIM, D_MODEL), C_HEADS * HEAD_DIM),
        'd_w_in': w((nd, D_MODEL, D_IN), D_MODEL),
        'd_idx_knorm': gain((nd, IDX_DIM)),
        'd_w_out': w((nd, D_HEADS * HEAD_DIM, D_MODEL), D_HEADS * HEAD_DIM),
        'final_norm': gain((D_MODEL,)),
    }

def reference(x, positions, attn_norm, ffn_norm, ffn_w_up, ffn_conv_w, ffn_conv_b, ffn_w_down,
              a_w_in, a_sinks, a_w_out, b_w_in, b_lam_q1, b_lam_k1, b_lam_q2, b_lam_k2, b_subln, b_w_out,
              c_w_in, c_rel_bias, c_w_out, d_w_in, d_idx_knorm, d_w_out, final_norm):
    cos, sin = rope_tables(positions)
    for i in range(DEPTH):
        j, kind = divmod(i, N_MIXERS)
        h = rms_norm(x, attn_norm[i])
        if kind == 0:
            y = sliding_sink_attention(h, a_w_in[j], a_sinks[j], a_w_out[j], cos, sin)
        elif kind == 1:
            lambda_init = 0.8 - 0.6 * math.exp(-0.3 * i)
            y = differential_attention(h, b_w_in[j], b_lam_q1[j], b_lam_k1[j], b_lam_q2[j], b_lam_k2[j],
                                       b_subln[j], b_w_out[j], cos, sin, lambda_init)
        elif kind == 2:
            y = chunked_relpos_attention(h, c_w_in[j], c_rel_bias[j], c_w_out[j])
        else:
            y = dsa_attention(h, d_w_in[j], d_idx_knorm[j], d_w_out[j], cos, sin)
        x = x + y
        x = x + conv_ffn(rms_norm(x, ffn_norm[i]), ffn_w_up[i], ffn_conv_w[i], ffn_conv_b[i], ffn_w_down[i])
    return rms_norm(x, final_norm)


_drawn_inputs = setup_inputs


def setup_inputs(seed=0):
    import zlib

    import numpy as np

    out = dict(_drawn_inputs(seed))
    spreads = {}
    factors = {'attn_norm': 2.726,
     'ffn_conv_b': 3.625,
     'a_sinks': 64.0,
     'b_lam_q2': 190.151,
     'b_subln': 49.122,
     'final_norm': 23.215}
    for name, (base, spread) in spreads.items():
        noise = np.random.default_rng([zlib.crc32(name.encode()), seed]).standard_normal(out[name].shape)
        drawn = base * np.exp(spread * noise) if base else spread * noise
        out[name] = __import__('jax').numpy.asarray(drawn.astype(out[name].dtype))
    for name, factor in factors.items():
        out[name] = (out[name] * factor).astype(out[name].dtype)
    return out
```

```python
from contextlib import ExitStack
from itertools import chain
import math

import concourse.bass as bass
from concourse import mybir

P = 128
T = 512
NT = T // P
D = 1024
KC = D // P
HD = 64
UW = 384
F = 2816
FB = F // P
CONVW = 3
EPS = 1e-6
NEG = -1e30
SCALE = HD ** -0.5
THETA, ROT = 500000.0, HD // 4
HALF = ROT // 2
LAMBDA_INIT = 0.8 - 0.6 * math.exp(-0.3 * 1)
TWO_PI_PARTS = (6.28125, 0.0019350051879882812, 3.019916050561733e-07)
ROUND = 12582912.0
PI_BELOW = 3.1415925

UA, UB = 4, 8
OB, ODC = 4, 2

PHASES = {}
_first = _landed = _parts = 0
for _name, _n, _cols, _dmas, _cut in (
        ("attnA", UA, KC * UW, 3, 4), ("outA", OB, KC * ODC * P, 1, 1),
        ("up0", FB, KC * 2 * P, 2, 1), ("down0", FB, D, 1, 1),
        ("attnB", UB, KC * UW, 3, 4), ("outB", OB, KC * ODC * P, 1, 1),
        ("up1", FB, KC * 2 * P, 2, 1), ("down1", FB, D, 1, 1)):
    PHASES[_name] = (_first, _n, _cols, _dmas, _landed, _cut, _parts)
    _first += _n
    _landed += 16 * _dmas * (_n // 2)
    _parts += _cut * _n
ORDER = list(PHASES)
PER_UNIT_B = 3 + 4 * 4

R_CONVW, R_CONVB, R_ATTN, R_FFN, R_FINAL, R_SUBLN, R_ALL = 0, 66, 88, 96, 104, 112, 113

CONSTS = 1 + HALF + 4 + 10

ALU = mybir.AluOpType
ACT = mybir.ActivationFunctionType
AX = mybir.AxisListType
F32 = mybir.dt.float32
F32R = mybir.dt.float32r
BF16 = mybir.dt.bfloat16
I32 = mybir.dt.int32


class Chain:

    def __init__(self, eng, sem):
        self.eng, self.sem, self.base, self.k = eng, sem, 0, 0

    def link(self, ins):
        ins.then_inc(self.sem, 1)
        self.k += 1
        self.eng.wait_ge(self.sem, self.base + self.k)

    def mark(self, ins):
        ins.then_inc(self.sem, 1)
        self.k += 1

    def enter(self, r, per):
        self.start, self.per = self.base + self.k, per
        self.base, self.k = r * per + self.start, 0

    def leave(self, turns):
        assert self.k == self.per, (self.k, self.per)
        self.base, self.k = self.start + self.per * turns, 0


def trunk(nc, x, positions, attn_norm, ffn_norm, ffn_w_up, ffn_conv_w, ffn_conv_b, ffn_w_down,
          a_w_in, a_sinks, a_w_out, b_w_in, b_lam_q1, b_lam_k1, b_lam_q2, b_lam_k2, b_subln,
          b_w_out, final_norm, out):
    ctx = ExitStack()
    with ctx:
        def sb(name, shape, dt=F32, stack=ctx):
            return stack.enter_context(nc.sbuf_tensor(name, shape, dt))

        def sem(name):
            return ctx.enter_context(nc.semaphore(name))

        xT = sb("xT", [P, KC, T])
        h_hi = sb("h_hi", [P, KC, T], F32R)
        h_lo = sb("h_lo", [P, KC, T], F32R)
        raw = sb("raw", [P, 2, KC * UW])
        w_hi = sb("w_hi", [P, 2, KC * UW], F32R)
        w_lo = sb("w_lo", [P, 2, KC * UW], F32R)
        htmp = sb("htmp", [P, 2, T])
        sq = sb("sq", [P, 2, T])
        rstd = sb("rstd", [P, T])
        ident = sb("ident", [P, P])
        ones_d = sb("ones_d", [P, P])
        eps = sb("eps", [P, 1])
        mask_q = sb("mask_q", [P, P], BF16)
        mask_k = sb("mask_k", [P, 2 * P], BF16)
        vecT = sb("vecT", [P, 2, R_ALL])
        nsink = sb("nsink", [P, UA * 4])
        lam_s = sb("lam_s", [P, 4])
        neglam = sb("neglam", [P, 1])
        gainB = sb("gainB", [P, 1])
        cos16 = sb("cos16", [P, NT, ROT])
        sin16 = sb("sin16", [P, NT, ROT])
        ropeA = htmp[:, 1, 0:NT * 6 * ROT].rearrange("p (t h d) -> p t h d", t=NT, h=6)
        ropeB = sq[:, 1, 0:NT * 6 * ROT].rearrange("p (t h d) -> p t h d", t=NT, h=6)
        nb = sb("nb", [P, NT, 4])
        sd = sb("sd", [P, NT, 4])
        es = sb("es", [P, NT, 4])
        rowsum = sb("rowsum", [P, NT, 4])
        den = sb("den", [P, NT, 4])
        rden = sb("rden", [P, NT, 4])

        with ExitStack() as st:
            ot_hi = sb("ot_hi", [P, KC, T], F32R, st)
            ot_lo = sb("ot_lo", [P, KC, T], F32R, st)
            qk = sb("qk", [P, NT, UW], F32, st)
            qt_hi = sb("qt_hi", [P, 3, T], F32R, st)
            qt_lo = sb("qt_lo", [P, 3, T], F32R, st)
            v_hi = sb("v_hi", [P, 2, NT, P], F32R, st)
            v_lo = sb("v_lo", [P, 2, NT, P], F32R, st)
            prob = sb("prob", [P, 2, 1024], F32, st)
            pt_hi = sb("pt_hi", [P, 2, T], F32R, st)
            pt_lo = sb("pt_lo", [P, 2, T], F32R, st)
        with ExitStack() as st:
            u_all = sb("u_all", [P, FB, T], F32, st)
            u_hi = sb("u_hi", [P, 2, T], F32R, st)
            u_lo = sb("u_lo", [P, 2, T], F32R, st)
            conv = sb("conv", [P, 2, T], F32, st)
            gated = sb("gated", [P, 2, T], F32, st)
            ssacc = sb("ssacc", [P, T], F32, st)
        with ExitStack() as st:
            x_tok = sb("x_tok", [P, NT, D], F32, st)
            vrow = sb("vrow", [P, 2, P], F32, st)
            pos_i = sb("pos_i", [NT, P], I32, st)
            pos_f = sb("pos_f", [NT, P], F32, st)
            posT = sb("posT", [P, NT], F32, st)
            x_ss = sb("x_ss", [P, NT], F32, st)
            invf = sb("invf", [P, HALF], F32, st)
            ang = sb("ang", [P, NT, HALF], F32, st)
            turns = sb("turns", [P, NT, HALF], F32, st)
            angneg = sb("angneg", [P, NT, HALF], F32, st)
            lam = sb("lam", [P, 4, HD], F32, st)
            sink_in = sb("sink_in", [P, UA * 4], F32, st)
            angcos = sb("angcos", [P, NT, HALF], F32, st)

        ps = ctx.enter_context(nc.psum_tensor("ps", [P, 8, T], F32))
        PJ, TB, OBK = (0, 1), 6, 7

        def s_bank(t):
            return 2 + 2 * (t % 2)

        x_landed = [sem(f"x_landed{t}") for t in range(NT)]
        vec_landed = sem("vec_landed")
        sink_landed = sem("sink_landed")
        lam_landed = sem("lam_landed")
        pos_landed = sem("pos_landed")
        raw_landed = [sem("raw_landed0"), sem("raw_landed1")]
        hi_done = sem("hi_done")
        lo_done = sem("lo_done")
        const_done = sem("const_done")
        ident_done = sem("ident_done")
        pos_done = sem("pos_done")
        posT_tr = sem("posT_tr")
        posT_done = sem("posT_done")
        ang_done = sem("ang_done")
        trig_done = sem("trig_done")
        vecT_tr = sem("vecT_tr")
        vecT_done = sem("vecT_done")
        nsink_done = sem("nsink_done")
        lam_sum = sem("lam_sum")
        lam_exp = sem("lam_exp")
        x_tr = sem("x_tr")
        x_sq = sem("x_sq")
        x_diag = sem("x_diag")
        x_ready = sem("x_ready")
        sq_done = sem("sq_done")
        ss_done = sem("ss_done")
        ms_done = sem("ms_done")
        ln_done = sem("ln_done")
        rstd_done = sem("rstd_done")
        htmp_done = sem("htmp_done")
        hhi_done = sem("hhi_done")
        hlo_done = sem("hlo_done")
        proj_done = sem("proj_done")
        proj_out = sem("proj_out")
        rope_done = sem("rope_done")
        vlo_done = sem("vlo_done")
        tr_done = sem("tr_done")
        thi_done = sem("thi_done")
        tlo_done = sem("tlo_done")
        s_done = sem("s_done")
        nb_done = sem("nb_done")
        exp_done = sem("exp_done")
        rden_done = sem("rden_done")
        p_done = sem("p_done")
        pv_done = sem("pv_done")
        ohi_done = sem("ohi_done")
        olo_done = sem("olo_done")
        osq_done = sem("osq_done")
        oms_done = sem("oms_done")
        oln_done = sem("oln_done")
        orstd_done = sem("orstd_done")
        otmp_done = sem("otmp_done")
        oproj_done = sem("oproj_done")
        up_done = sem("up_done")
        conv_done = sem("conv_done")
        silu_done = sem("silu_done")
        u_done = sem("u_done")
        uhi_done = sem("uhi_done")
        ulo_done = sem("ulo_done")
        down_used = sem("down_used")
        down_done = sem("down_done")
        y_done = sem("y_done")
        y_tr = sem("y_tr")
        y_out = sem("y_out")
        stored = sem("stored")
        dve_self = sem("dve_self")

        def values(kind, dst, s, t):
            src = ps[:, PJ[t % 2], 2 * P:UW]
            if kind == "B":
                return dst[:, s, t, :], src
            return (dst[:, s, t, :].rearrange("p (c d) -> p c d", c=2),
                    src[:, HD:].unsqueeze(1).broadcast_to((P, 2, HD)))

        def split_of(kind, name, qt, pt):
            if name[0] == "q":
                return qt[:, int(name[1]), :]
            if kind == "A":
                return pt[:, "ab".index(name[2]), :]
            t = int(name[1])
            return pt[:, t % 2, 0:(t + 1) * P]

        def outputs_a(dst, u, t, e):
            rows = slice(e * HD, (e + 1) * HD)
            src = ps[:, OBK, :].rearrange("p (c e q) -> p c e q", c=2, e=2)
            return dst[rows, 2 * u:2 * u + 2, t * P:(t + 1) * P], src[rows, :, e, :]

        block = ctx.enter_context(nc.Block())

        def first(ph):
            return PHASES[ph][0]

        def n_blocks(ph):
            return PHASES[ph][1]

        def landed(ph, s, turn):
            return PHASES[ph][4] + 16 * PHASES[ph][3] * (turn + 1)

        def cols(ph):
            return PHASES[ph][2]

        def parts(ph):
            return PHASES[ph][5]

        def part_done(ph, i, c=None):
            n = parts(ph)
            return i * n + (PHASES[ph][6] + (n if c is None else c + 1))

        UNIT0 = {"A": 0, "B": UA}
        FILLS = {"A": ("p0b", "p1a", "p1b", "q0", "p2a", "p2b", "q1", "q2", "p3a", "p3b"),
                 "B": ("p0", "p1", "q0", "p2", "q1", "p3")}
        QFILLS = {"A": 3, "B": 2}
        FILL0 = {"A": 0, "B": UA * len(FILLS["A"])}
        UNITS = {"A": UA, "B": UB}
        NORM = {"A": 0, "F0": 1, "B": 2, "F1": 3, "end": 4}
        PHASE = {"A": "attnA", "B": "attnB"}

        def fill_no(kind, u, name):
            if isinstance(u, int) and u < 0:
                return FILL0[kind] + int(name[1]) + 1
            names = FILLS[kind]
            if isinstance(u, int) and u == UNITS[kind] - 1:
                names = [n for n in names if n[0] == "p"]
            return u * len(FILLS[kind]) + (FILL0[kind] + QFILLS[kind] + names.index(name) + 1)

        def layer(ph):
            return 0 if first(ph) < first("attnB") else 1

        def wait_used(eng, ph, i):
            l = layer(ph)
            if ph[:4] == "attn":
                eng.wait_ge(proj_done, i * NT + (NT * (UNIT0[ph[4]] + 1)))
            elif ph[:3] == "out":
                eng.wait_ge(oproj_done, i * ODC + (KC * l + ODC))
            elif ph[:2] == "up":
                eng.wait_ge(up_done, i + (FB * l + 1))
            elif isinstance(i, int) and i == FB - 1:
                eng.wait_ge(down_done, KC * (l + 1))
            else:
                eng.wait_ge(down_used, i + ((FB - 1) * l + 1))

        @block.sync
        def _(sp):
            xv = x.rearrange("b (t p) d -> p (b t) d", p=P)
            sp.dma_start(pos_i[:, :], positions.rearrange("b (t p) -> (b t) p", p=P))\
              .then_inc(pos_landed, 16)
            for t in range(NT):
                sp.dma_start(x_tok[:, t, :], xv[:, t, :]).then_inc(x_landed[t], 16)

            def load(ph, s, turn, wait):
                i = 2 * turn + s
                if wait == "own":
                    sp.wait_ge(lo_done, part_done(ph, i - 2))
                elif wait == "before":
                    q = ORDER[ORDER.index(ph) - 1]
                    sp.wait_ge(lo_done, part_done(q, n_blocks(q) - 2 + s))
                if ph[:4] == "attn":
                    w, qw, kvw = (a_w_in, 256, 64) if ph == "attnA" else (b_w_in, P, P)
                    wv = w[0].rearrange("(k p) n -> p k n", p=P)
                    rv = raw[:, s, :].rearrange("p (k n) -> p k n", k=KC)
                    at = qw
                    sp.dma_start(rv[:, :, 0:qw], wv[:, :, bass.ds(i * qw, qw)])\
                      .then_inc(raw_landed[s], 16)
                    for side in range(2):
                        sp.dma_start(rv[:, :, at:at + kvw],
                                     wv[:, :, bass.ds(i * kvw + (D if side == 0 else v_at(ph)), kvw)])\
                          .then_inc(raw_landed[s], 16)
                        at += kvw
                elif ph[:3] == "out":
                    w = a_w_out if ph == "outA" else b_w_out
                    wv = w[0].rearrange("(k p) n -> p k n", p=P)
                    rv = raw[:, s, 0:cols(ph)].rearrange("p (k n) -> p k n", k=KC)
                    sp.dma_start(rv, wv[:, :, bass.ds(i * ODC * P, ODC * P)])\
                      .then_inc(raw_landed[s], 16)
                elif ph[:2] == "up":
                    wv = ffn_w_up[int(ph[2])].rearrange("(k p) n -> p k n", p=P)
                    rv = raw[:, s, 0:cols(ph)].rearrange("p (k g n) -> p k g n", k=KC, g=2)
                    for g in range(2):
                        sp.dma_start(rv[:, :, g, :], wv[:, :, bass.ds(i * P + g * F, P)])\
                          .then_inc(raw_landed[s], 16)
                else:
                    wv = ffn_w_down[int(ph[4])].rearrange("(f p) n -> p f n", p=P)
                    sp.dma_start(raw[:, s, 0:D], wv[:, bass.ds(i, 1), :])\
                      .then_inc(raw_landed[s], 16)

            def v_at(ph):
                return D + 256 if ph == "attnA" else 2 * D

            def vectors(l):
                n = CONVW * FB
                sp.dma_start(vrow[R_CONVW:R_CONVW + n, l, :],
                             ffn_conv_w[l].rearrange("c (f p) -> (c f) p", p=P)).then_inc(vec_landed, 16)
                sp.dma_start(vrow[R_CONVB:R_CONVB + FB, l, :],
                             ffn_conv_b[l].rearrange("(f p) -> f p", p=P)).then_inc(vec_landed, 16)
                sp.dma_start(vrow[R_ATTN:R_ATTN + KC, l, :],
                             attn_norm[l].rearrange("(f p) -> f p", p=P)).then_inc(vec_landed, 16)
                sp.dma_start(vrow[R_FFN:R_FFN + KC, l, :],
                             ffn_norm[l].rearrange("(f p) -> f p", p=P)).then_inc(vec_landed, 16)

            vectors(0)
            vectors(1)
            sp.dma_start(vrow[R_FINAL:R_FINAL + KC, 1, :],
                         final_norm.rearrange("(f p) -> f p", p=P)).then_inc(vec_landed, 16)
            sp.dma_start(vrow[R_SUBLN:R_SUBLN + 1, 1, :], b_subln).then_inc(vec_landed, 16)
            load("attnA", 0, 0, None)
            load("attnA", 1, 0, None)
            sp.dma_start(sink_in[:, :], a_sinks.partition_broadcast(P)).then_inc(sink_landed, 16)
            for i, v in enumerate((b_lam_q1, b_lam_k1, b_lam_q2, b_lam_k2)):
                sp.dma_start(lam[:, i, :], v.partition_broadcast(P)).then_inc(lam_landed, 16)

            for ph in ORDER:
                for s in range(2):
                    if ph != ORDER[0]:
                        load(ph, s, 0, "before")
                if n_blocks(ph) == 4:
                    for s in range(2):
                        load(ph, s, 1, "own")
                else:
                    with sp.Fori(1, n_blocks(ph) // 2) as r:
                        for s in range(2):
                            load(ph, s, r, "own")

            ov = out.rearrange("b (t p) d -> p (b t) d", p=P)
            piece = 2 * P
            for c in range(D // piece):
                sp.wait_ge(y_out, 2 * (c + 1))
                sp.dma_start(ov[:, :, c * piece:(c + 1) * piece],
                             x_tok[:, :, c * piece:(c + 1) * piece]).then_inc(stored, 16)
            sp.wait_ge(stored, 16 * (D // piece))

        @block.gpsimd
        def _(pool):
            pool.memset(ident[:, :], 0.0).then_inc(const_done, 1)
            pool.wait_ge(const_done, 1)
            pool.affine_select(out=ident[:, :], in_=ident[:, :], compare_op=ALU.not_equal, fill=1.0,
                               base=0, pattern=[[-1, P]], channel_multiplier=1).then_inc(ident_done, 1)
            for i in range(HALF):
                pool.memset(invf[:, i:i + 1], inv_freq(i)).then_inc(const_done, 1)
            pool.memset(ones_d[:, :], 1.0 / D).then_inc(const_done, 1)
            pool.memset(eps[:, :], EPS).then_inc(const_done, 1)
            pool.memset(mask_q[:, :], 0.0).then_inc(const_done, 1)
            pool.memset(mask_k[:, :], 0.0).then_inc(const_done, 1)
            pool.wait_ge(const_done, 1 + HALF + 4)
            for row in (0, HD):
                pool.memset(mask_q[row:row + 1, 0:HD], 1.0).then_inc(const_done, 1)
                pool.memset(mask_q[row + 32:row + 33, HD:P], 1.0).then_inc(const_done, 1)
                pool.memset(mask_k[row:row + 1, 0:HD], NEG).then_inc(const_done, 1)
                pool.memset(mask_k[row:row + 1, 3 * HD:4 * HD], NEG).then_inc(const_done, 1)
                pool.memset(mask_k[row + 32:row + 33, 0:2 * HD], NEG).then_inc(const_done, 1)
            pool.wait_ge(const_done, CONSTS)

            def low(ph, s, i):
                n = cols(ph) // parts(ph)
                for c in range(parts(ph)):
                    at = slice(c * n, (c + 1) * n)
                    pool.wait_ge(hi_done, part_done(ph, i, c))
                    pool.tensor_tensor(w_lo[:, s, at], raw[:, s, at], w_hi[:, s, at].bitcast(F32),
                                       ALU.subtract).then_inc(lo_done, 1)

            for ph in ORDER:
                with pool.Fori(0, n_blocks(ph) // 2) as r:
                    for s in range(2):
                        low(ph, s, r * 2 + s)

        @block.tensor
        def _(pe):
            def hi_lo(out_, a_hi, a_lo, b_hi, b_lo, start, stop):
                pe.matmul(out_, a_lo, b_hi, start=start, stop=False)
                pe.matmul(out_, a_hi, b_lo, start=False, stop=False)
                return pe.matmul(out_, a_hi, b_hi, start=False, stop=stop)

            pe.wait_ge(ident_done, 1)
            pe.wait_ge(pos_done, 1)
            pe.transpose(ps[:, 7, 0:NT], pos_f[:, :], ident[0:NT, 0:NT]).then_inc(posT_tr, 1)
            for t in range(NT):
                pe.wait_ge(x_landed[t], 16)
                for kc in range(KC):
                    if t == 0 and kc == KC - 1:
                        pe.wait_ge(posT_done, 1)
                    ins = pe.transpose(ps[:, kc, t * P:(t + 1) * P], x_tok[:, t, kc * P:(kc + 1) * P],
                                       ident[:, :])
                    if t == NT - 1:
                        ins.then_inc(x_tr, 1)
            pe.wait_ge(const_done, CONSTS)
            pe.wait_ge(x_diag, NT)
            pe.wait_ge(x_ready, TB + 1)
            pe.matmul(ps[:, TB, :], ones_d[:, :], ssacc[:, :], start=True, stop=True)\
              .then_inc(ms_done, 1)
            pe.wait_ge(vec_landed, 16 * 10)
            pe.transpose(ps[:, 0, 0:R_FINAL], vrow[0:R_FINAL, 0, :], ident[0:R_FINAL, 0:R_FINAL])
            pe.transpose(ps[:, 0, P:P + R_ALL], vrow[0:R_ALL, 1, :],
                         ident[0:R_ALL, 0:R_ALL]).then_inc(vecT_tr, 1)

            def mean_square(norm):
                pe.wait_ge(ss_done, KC * norm)
                pe.matmul(ps[:, TB, :], ones_d[:, :], ssacc[:, :], start=True, stop=True)\
                  .then_inc(ms_done, 1)

            def projection(kind, u, s, tiles):
                ph = PHASE[kind]
                wh = w_hi[:, s, :].rearrange("p (k n) -> p k n", k=KC)
                wl = w_lo[:, s, :].rearrange("p (k n) -> p k n", k=KC)
                tile0 = NT * (u + UNIT0[kind])
                coming = tiles[0] == 0
                first_unit = isinstance(u, int) and u == 0
                order = [(t, kc) for t in tiles for kc in range(KC)]
                if coming and first_unit:
                    order.sort(key=lambda x: x[1])
                n = 0
                for t, kc in order:
                    tok = slice(t * P, (t + 1) * P)
                    if kc == 0 and not (isinstance(tile0, int) and tile0 + t < 2):
                        pe.wait_ge(vlo_done, tile0 + (t - 1))
                    if t == 0 and kc % 2 == 0:
                        pe.wait_ge(lo_done, part_done(ph, u, kc // 2))
                    if first_unit and t == 0:
                        pe.wait_ge(hlo_done, KC * NORM[kind] + kc + 1)
                    for m, (a, b) in enumerate(((h_lo, wh), (h_hi, wl), (h_hi, wh))):
                        ins = pe.matmul(ps[:, PJ[t % 2], 0:UW], a[:, kc, tok], b[:, kc, :],
                                        start=(kc == 0 and m == 0), stop=(kc == KC - 1 and m == 2))
                        n += 1
                        if kc == KC - 1 and m == 2:
                            ins.then_inc(proj_done, 1)
                        if n % 4 == 0:
                            yield

            def run(slabs, k):
                for _ in range(k):
                    next(slabs, None)

            def fill(kind, u, name, blocks, inputs):
                pe.wait_ge(tlo_done, fill_no(kind, u, name) - 1)
                for (c, i) in zip(blocks, inputs):
                    ins = pe.transpose(ps[:, TB, c * P:(c + 1) * P], i, ident[:, :])
                ins.then_inc(tr_done, 1)

            def fill_qk(kind, u, c):
                if c == 0:
                    pe.wait_ge(rope_done, u + (UNIT0[kind] + 2))
                fill(kind, u, f"q{c}", range(NT), [qk[:, t, c * P:(c + 1) * P] for t in range(NT)])

            def start_unit0(kind):
                for tiles in ((0, 1), (2, 3)):
                    for _ in projection(kind, 0, 0, tiles):
                        pass
                slabs = projection(kind, 1, 1, (0, 1))
                run(slabs, 6)
                for c in range(QFILLS[kind]):
                    fill_qk(kind, -1, c)
                    run(slabs, 2)
                scores = scores_a if kind == "A" else scores_b
                scores(0, 0)
                scores(0, 1)
                run(slabs, 24)

            def scores_a(u, t):
                if t == 0:
                    pe.wait_ge(tlo_done, fill_no("A", u - 1, "q2"))
                if NT * u + t >= 2:
                    pe.wait_ge(exp_done, NT * u + t - 1)
                q = slice(t * P, (t + 1) * P)
                lo = 0 if t else P
                keys = slice((t - 1) * P if t else 0, (t + 1) * P)
                for e in range(2):
                    rows = slice(e * HD, (e + 1) * HD)
                    bank = ps[:, s_bank(t) + e, :].rearrange("p (h k) -> p h k", h=2)
                    pe.matmul(bank[:, :, lo:], mask_q[rows, :],
                              mask_k[rows, lo:].unsqueeze(1).broadcast_to((HD, 2, 2 * P - lo)),
                              start=True, stop=False)
                    for c in range(2):
                        for m, (a, b) in enumerate(((qt_lo, qt_hi), (qt_hi, qt_lo), (qt_hi, qt_hi))):
                            ins = pe.matmul(bank[:, c, lo:], a[rows, c, q], b[rows, 2, keys],
                                            start=False, stop=(c == 1 and m == 2))
                ins.then_inc(s_done, 1)

            def fill_p_a(u, t, kt):
                pe.wait_ge(p_done, u * NT + t + 1)
                fill("A", u, f"p{t}{'ab'[kt]}", (0, 2, 1, 3),
                     [prob[:, t % 2, h * 256 + kt * P:h * 256 + (kt + 1) * P] for h in range(4)])

            def outputs(u, t):
                pe.wait_ge(tlo_done, fill_no("A", u, f"p{t}b"))
                if NT * u + t:
                    pe.wait_ge(olo_done, NT * u + t)
                if t == 0:
                    pe.wait_ge(vlo_done, NT * (u + 1))
                for kt in (0, 1) if t else (1,):
                    v = t - 1 + kt
                    ins = hi_lo(ps[:, OBK, :], v_hi[:, u % 2, v, :], v_lo[:, u % 2, v, :],
                                pt_hi[:, kt, :], pt_lo[:, kt, :], start=(kt == 0 or t == 0),
                                stop=(kt == 1))
                ins.then_inc(pv_done, 1)

            def unit_a(u):
                more = u + 1 < UA
                slabs = chain(projection("A", u + 1, (u + 1) % 2, (2, 3)) if more else (),
                              projection("A", u + 2, u % 2, (0, 1)) if u + 2 < UA else ())
                fill_p_a(u, 0, 1)
                run(slabs, 3)
                outputs(u, 0)
                scores_a(u, 2)
                run(slabs, 3)
                fill_p_a(u, 1, 0)
                run(slabs, 3)
                fill_p_a(u, 1, 1)
                run(slabs, 3)
                outputs(u, 1)
                scores_a(u, 3)
                if more:
                    run(slabs, 3)
                    fill_qk("A", u, 0)
                    run(slabs, 2)
                fill_p_a(u, 2, 0)
                run(slabs, 2)
                fill_p_a(u, 2, 1)
                run(slabs, 1)
                if more:
                    fill_qk("A", u, 1)
                outputs(u, 2)
                run(slabs, 1)
                if more:
                    fill_qk("A", u, 2)
                    run(slabs, 1)
                fill_p_a(u, 3, 0)
                if more:
                    scores_a(u + 1, 0)
                fill_p_a(u, 3, 1)
                run(slabs, 1)
                outputs(u, 3)
                if more:
                    scores_a(u + 1, 1)
                run(slabs, 24)

            def scores_b(u, t):
                if t == 0:
                    pe.wait_ge(tlo_done, fill_no("B", u - 1, "q1"))
                pe.wait_ge(exp_done, u * NT + (NT * UNIT0["B"] + t - 1))
                q = slice(t * P, (t + 1) * P)
                n = (t + 1) * P
                for e in range(2):
                    rows = slice(e * HD, (e + 1) * HD)
                    bank = ps[:, s_bank(t) + e, :]
                    for m, (a, b) in enumerate(((qt_lo, qt_hi), (qt_hi, qt_lo), (qt_hi, qt_hi))):
                        pe.matmul(bank[:, 0:n], a[rows, 0, q], b[rows, 1, 0:n], start=(m == 0),
                                  stop=False)
                    ins = pe.matmul(bank[:, n - P:n], mask_q[rows, :], mask_k[rows, P:2 * P],
                                    start=False, stop=True)
                ins.then_inc(s_done, 1)

            def fill_p_b(u, t):
                pe.wait_ge(p_done, u * NT + (NT * UNIT0["B"] + t + 1))
                if t == 0 and not (isinstance(u, int) and u == 0):
                    pe.wait_ge(oln_done, u)
                fill("B", u, f"p{t}", range(t + 1),
                     [prob[:, t % 2, k * P:(k + 1) * P] for k in range(t + 1)])

            def outputs_b(u, s, t):
                pe.wait_ge(tlo_done, fill_no("B", u, f"p{t}"))
                if t == 0:
                    pe.wait_ge(vlo_done, u * NT + (NT * (UNIT0["B"] + 1)))
                    if not (isinstance(u, int) and u == 0):
                        pe.wait_ge(otmp_done, u)
                o = ps[:, OBK, t * P:(t + 1) * P]
                for k in range(t + 1):
                    ins = hi_lo(o, v_hi[:, s, k, :], v_lo[:, s, k, :], pt_hi[:, t % 2, k * P:(k + 1) * P],
                                pt_lo[:, t % 2, k * P:(k + 1) * P], start=(k == 0), stop=(k == t))
                ins.then_inc(pv_done, 1)

            def unit_b(u, s, more=True, more2=True):
                slabs = chain(projection("B", u + 1, 1 - s, (2, 3)) if more else (),
                              projection("B", u + 2, s, (0, 1)) if more2 else ())
                fill_p_b(u, 0)
                run(slabs, 3)
                outputs_b(u, s, 0)
                scores_b(u, 2)
                run(slabs, 3)
                fill_p_b(u, 1)
                run(slabs, 6)
                outputs_b(u, s, 1)
                scores_b(u, 3)
                if more:
                    run(slabs, 3)
                    fill_qk("B", u, 0)
                    run(slabs, 2)
                fill_p_b(u, 2)
                run(slabs, 2)
                if more:
                    fill_qk("B", u, 1)
                    run(slabs, 1)
                outputs_b(u, s, 2)
                if more:
                    scores_b(u + 1, 0)
                    run(slabs, 1)
                fill_p_b(u, 3)
                run(slabs, 1)
                outputs_b(u, s, 3)
                if more:
                    scores_b(u + 1, 1)
                run(slabs, 24)
                pe.wait_ge(osq_done, u + 1)
                pe.matmul(ps[:, TB, :], ones_d[:, :], osq[:, :], start=True, stop=True)\
                  .then_inc(oms_done, 1)

            osq = sq[:, 0, :]

            start_unit0("A")
            for u in range(UA):
                unit_a(u)

            def out_projection(l):
                ph, norm = ("outA", "outB")[l], NORM["F0"] if l == 0 else NORM["F1"]
                pe.wait_ge(olo_done, NT * UA + UB * l)
                with pe.Fori(0, OB // 2) as r:
                    for s in range(2):
                        pe.wait_ge(lo_done, part_done(ph, r * 2 + s))
                        wh = w_hi[:, s, 0:cols(ph)].rearrange("p (k n) -> p k n", k=KC)
                        wl = w_lo[:, s, 0:cols(ph)].rearrange("p (k n) -> p k n", k=KC)
                        for e in range(ODC):
                            j = ODC * s + e
                            pe.wait_ge(x_ready, r * 4 + (KC * norm + j - 3))
                            for kc in range(KC):
                                c = slice(e * P, (e + 1) * P)
                                ins = hi_lo(ps[:, j, :], wh[:, kc, c], wl[:, kc, c], ot_hi[:, kc, :],
                                            ot_lo[:, kc, :], start=(kc == 0), stop=(kc == KC - 1))
                            ins.then_inc(oproj_done, 1)

            def up_pair(l, r, is_first):
                ph, norm = f"up{l}", NORM["F0"] if l == 0 else NORM["F1"]
                for s in range(2):
                    pe.wait_ge(lo_done, part_done(ph, r * 2 + s))
                    if not is_first:
                        pe.wait_ge(u_done, r * 2 + (FB * l + s - 1))
                    wh = w_hi[:, s, 0:cols(ph)].rearrange("p (k g n) -> p k g n", k=KC, g=2)
                    wl = w_lo[:, s, 0:cols(ph)].rearrange("p (k g n) -> p k g n", k=KC, g=2)
                    order = [(g, kc) for g in range(2) for kc in range(KC)]
                    if is_first and s == 0:
                        order.sort(key=lambda x: x[1])
                    for g, kc in order:
                        if is_first and s == 0 and g == 0:
                            pe.wait_ge(hlo_done, KC * norm + kc + 1)
                        ins = hi_lo(ps[:, 2 * s + g, :], wh[:, kc, g, :], wl[:, kc, g, :],
                                    h_hi[:, kc, :], h_lo[:, kc, :], start=(kc == 0),
                                    stop=(kc == KC - 1))
                    ins.then_inc(up_done, 1)

            def down_pair(l, r, is_first, is_last):
                ph = f"down{l}"
                for s in range(2):
                    pe.wait_ge(lo_done, part_done(ph, r * 2 + s))
                    pe.wait_ge(ulo_done, r * 2 + (FB * l + s + 1))
                    for dc in range(KC):
                        if is_first and s == 0 and dc == 4:
                            pe.wait_ge(u_done, FB * (l + 1))
                        c = slice(dc * P, (dc + 1) * P)
                        ins = hi_lo(ps[:, (4 + dc) % 8, :], w_hi[:, s, c], w_lo[:, s, c],
                                    u_hi[:, s, :], u_lo[:, s, :], start=(is_first and s == 0),
                                    stop=(is_last and s == 1))
                        if is_last and s == 1:
                            ins.then_inc(down_done, 1)
                    if not (is_last and s == 1):
                        ins.then_inc(down_used, 1)

            def feed_forward(l):
                mean_square(NORM["F0"] if l == 0 else NORM["F1"])
                up_pair(l, 0, True)
                with pe.Fori(1, FB // 2) as r:
                    up_pair(l, r, False)
                down_pair(l, 0, True, False)
                with pe.Fori(1, FB // 2 - 1) as r:
                    down_pair(l, r, False, False)
                down_pair(l, FB // 2 - 1, False, True)

            out_projection(0)
            feed_forward(0)

            mean_square(NORM["B"])
            start_unit0("B")
            unit_b(0, 0)
            unit_b(1, 1)
            with pe.Fori(1, UB // 2 - 1) as r:
                for s in range(2):
                    unit_b(r * 2 + s, s)
            unit_b(UB - 2, 0, more2=False)
            unit_b(UB - 1, 1, more=False, more2=False)
            out_projection(1)
            feed_forward(1)

            mean_square(NORM["end"])
            for kc in range(KC):
                pe.wait_ge(y_done, kc + 1)
                if kc == TB:
                    pe.wait_ge(rstd_done, 5)
                for t in range(NT):
                    ins = pe.transpose(ps[:, kc, t * P:(t + 1) * P], htmp[:, kc % 2, t * P:(t + 1) * P],
                                       ident[:, :])
                ins.then_inc(y_tr, 1)

        @block.scalar
        def _(act):
            def high(ph, s, turn, used=None, c=0):
                if c >= parts(ph):
                    return
                n = cols(ph) // parts(ph)
                at = slice(c * n, (c + 1) * n)
                if used is not None and c == 0:
                    wait_used(act, *used)
                if c == 0:
                    act.wait_ge(raw_landed[s], landed(ph, s, turn) if isinstance(turn, int)
                                else turn * (16 * PHASES[ph][3]) + landed(ph, s, 0))
                act.activation(w_hi[:, s, at], raw[:, s, at], ACT.Copy).then_inc(hi_done, 1)

            def high_after(ph, b, c=0):
                if b + 2 < n_blocks(ph):
                    high(ph, b % 2, b // 2 + 1, (ph, b), c)
                elif ph != ORDER[-1]:
                    high(ORDER[ORDER.index(ph) + 1], b % 2, 0, (ph, b), c)

            def square(norm, dc):
                act.wait_ge(x_ready, KC * norm + dc + 1)
                if KC * (norm - 1) + dc >= 2:
                    act.wait_ge(ss_done, KC * (norm - 1) + dc - 1)
                act.activation(sq[:, dc % 2, :], xT[:, dc, :], ACT.Square).then_inc(sq_done, 1)

            def rsqrt(norm):
                act.wait_ge(ms_done, norm + 1)
                act.activation(rstd[:, :], ps[:, TB, :], ACT.Ln, bias=eps[:, :]).then_inc(ln_done, 1)
                act.wait_ge(ln_done, norm + 1)
                act.activation(rstd[:, :], rstd[:, :], ACT.Exp, scale=-0.5).then_inc(rstd_done, 1)

            def high_h(norm, between):
                for kc in range(KC):
                    act.wait_ge(htmp_done, KC * norm + kc + 1)
                    act.activation(h_hi[:, kc, :], htmp[:, kc % 2, :], ACT.Copy).then_inc(hhi_done, 1)
                    between(kc)

            def take(kind, u, s, t):
                n = u * NT + (NT * UNIT0[kind] + t)
                act.wait_ge(proj_done, n + 1)
                bank = ps[:, PJ[t % 2], :]
                if kind == "A":
                    act.activation(qk[:, t, 5 * HD:6 * HD], bank[:, 4 * HD:5 * HD], ACT.Copy)
                    act.activation(qk[:, t, 0:5 * HD], bank[:, 0:5 * HD], ACT.Copy)
                else:
                    act.activation(qk[:, t, 0:2 * P], bank[:, 0:2 * P], ACT.Copy)
                dst, src = values(kind, v_hi, s, t)
                act.activation(dst, src, ACT.Copy).then_inc(proj_out, 1)

            def high_t(kind, u, name):
                n = int(name[1]) * P + P if kind == "B" and name[0] == "p" else T
                act.wait_ge(tr_done, fill_no(kind, u, name))
                act.activation(split_of(kind, name, qt_hi, pt_hi), ps[:, TB, 0:n], ACT.Copy)\
                   .then_inc(thi_done, 1)

            def exps_a(u, t):
                lo = 0 if t else P
                act.wait_ge(nb_done, NT * u + t + 1)
                act.activation(es[:, t, :], sd[:, t, :], ACT.Exp)
                for h in range(4):
                    s = ps[:, s_bank(t) + h // 2, (h % 2) * 256 + lo:(h % 2 + 1) * 256]
                    ins = act.activation(prob[:, t % 2, h * 256 + lo:(h + 1) * 256], s, ACT.Exp,
                                         bias=nb[:, t, h:h + 1], scale=SCALE,
                                         accum_out=rowsum[:, t, h:h + 1])
                ins.then_inc(exp_done, 1)

            def exps_b(u, t):
                n = (t + 1) * P
                act.wait_ge(nb_done, u * NT + (NT * UNIT0["B"] + t + 1))
                for e in range(2):
                    ins = act.activation(prob[:, t % 2, e * T:e * T + n], ps[:, s_bank(t) + e, 0:n],
                                         ACT.Exp, bias=nb[:, t, e:e + 1], scale=SCALE,
                                         accum_out=rowsum[:, t, e:e + 1])
                ins.then_inc(exp_done, 1)

            act.wait_ge(ang_done, 1)
            act.activation(cos16[:, :, 0:HALF], angcos[:, :, :], ACT.Sin)
            act.activation(cos16[:, :, HALF:ROT], angcos[:, :, :], ACT.Sin)
            act.activation(sin16[:, :, 0:HALF], ang[:, :, :], ACT.Sin, scale=-1.0)
            act.activation(sin16[:, :, HALF:ROT], ang[:, :, :], ACT.Sin).then_inc(trig_done, 1)
            act.preload_act_table_set("natural_log_exp_and_others")
            for t in range(NT):
                act.wait_ge(x_landed[t], 16)
                if t:
                    act.wait_ge(x_sq, t)
                act.activation(sq[:, :, :].rearrange("p a b -> p (a b)"), x_tok[:, t, :], ACT.Square,
                               accum_out=x_ss[:, t:t + 1]).then_inc(x_sq, 1)
            act.wait_ge(const_done, CONSTS)
            rsqrt(NORM["A"])
            high("attnA", 0, 0)

            def weights0(kc):
                if kc % 2 and kc < KC - 1:
                    high("attnA", 0, 0, None, kc // 2 + 1)

            high_h(NORM["A"], weights0)
            act.wait_ge(lam_sum, 1)
            act.activation(lam_s[:, 2:4], lam_s[:, 0:2], ACT.Exp).then_inc(lam_exp, 1)

            for t in range(NT):
                take("A", 0, 0, t)
                high("attnA", 1, 0, None, t)

            def first_scores(kind, exps):
                for c in range(QFILLS[kind]):
                    high_t(kind, -1, f"q{c}")
                exps(0, 0)
                take(kind, 1, 1, 0)
                exps(0, 1)
                take(kind, 1, 1, 1)

            def high_out_a(u, t):
                act.wait_ge(pv_done, NT * u + t + 1)
                for e in range(2):
                    dst, src = outputs_a(ot_hi, u, t, e)
                    ins = act.activation(dst, src, ACT.Copy)
                ins.then_inc(ohi_done, 1)

            first_scores("A", exps_a)
            for u in range(UA):
                more, more2 = u + 1 < UA, u + 2 < UA
                high_t("A", u, "p0b")
                high_after("attnA", u, 0)
                high_out_a(u, 0)
                high_after("attnA", u, 1)
                exps_a(u, 2)
                if more:
                    take("A", u + 1, (u + 1) % 2, 2)
                high_after("attnA", u, 2)
                high_t("A", u, "p1a")
                high_after("attnA", u, 3)
                high_t("A", u, "p1b")
                if more:
                    take("A", u + 1, (u + 1) % 2, 3)
                high_out_a(u, 1)
                exps_a(u, 3)
                if more:
                    high_t("A", u, "q0")
                high_t("A", u, "p2a")
                high_t("A", u, "p2b")
                if more:
                    high_t("A", u, "q1")
                high_out_a(u, 2)
                if more:
                    high_t("A", u, "q2")
                if more2:
                    take("A", u + 2, u % 2, 0)
                high_t("A", u, "p3a")
                if more:
                    exps_a(u + 1, 0)
                high_t("A", u, "p3b")
                if more2:
                    take("A", u + 2, u % 2, 1)
                high_out_a(u, 3)
                if more:
                    exps_a(u + 1, 1)

            def after_out(l):
                ph, norm = ("outA", "outB")[l], NORM["F0"] if l == 0 else NORM["F1"]
                for b in range(OB):
                    for e in range(ODC):
                        square(norm, ODC * b + e)
                    if b < OB - 1:
                        high_after(ph, b)
                rsqrt(norm)
                high_h(norm, lambda kc: high_after(ph, OB - 1) if kc == 1 else None)

            def high_u(l, s, f):
                act.wait_ge(u_done, f + (FB * l + 1))
                act.activation(u_hi[:, s, :], u_all[:, bass.ds(f, 1), :], ACT.Copy).then_inc(uhi_done, 1)

            def silu(l, s, f):
                act.wait_ge(conv_done, f + (FB * l + 1))
                act.activation(gated[:, s, :], conv[:, s, :], ACT.Silu).then_inc(silu_done, 1)

            def feed_forward(l):
                up, down = f"up{l}", f"down{l}"
                act.preload_act_table_set("silu_and_others")
                with act.Fori(0, FB // 2 - 1) as r:
                    for s in range(2):
                        high(up, s, r + 1, (up, r * 2 + s))
                        silu(l, s, r * 2 + s)
                for s in range(2):
                    high_after(up, FB - 2 + s)
                    silu(l, s, FB - 2 + s)
                    high_u(l, s, s)
                with act.Fori(0, FB // 2 - 1) as r:
                    for s in range(2):
                        wait_used(act, down, r * 2 + s)
                        high_u(l, s, r * 2 + (s + 2))
                        high(down, s, r + 1)
                act.preload_act_table_set("natural_log_exp_and_others")
                norm = NORM["B"] if l == 0 else NORM["end"]
                for dc in range(KC):
                    square(norm, dc)
                    if dc % 2 and dc > 1:
                        high_after(down, FB - 2, dc // 2 - 1)
                rsqrt(norm)
                high_after(down, FB - 2, 3)

            after_out(0)
            feed_forward(0)

            def weights1(kc):
                if kc % 2:
                    high_after("down0", FB - 1, kc // 2)

            high_h(NORM["B"], weights1)

            def unit_b(u, s, more=True, more2=True):
                def weights(c):
                    if isinstance(u, int):
                        high_after("attnB", u, c)
                    else:
                        high("attnB", s, r + 1, ("attnB", u), c)

                weights(0)
                high_t("B", u, "p0")
                weights(1)
                exps_b(u, 2)
                weights(2)
                if more:
                    take("B", u + 1, 1 - s, 2)
                high_t("B", u, "p1")
                weights(3)
                if more:
                    take("B", u + 1, 1 - s, 3)
                exps_b(u, 3)
                if more:
                    high_t("B", u, "q0")
                high_t("B", u, "p2")
                if more:
                    high_t("B", u, "q1")
                    exps_b(u + 1, 0)
                high_t("B", u, "p3")
                act.wait_ge(pv_done, u * NT + (NT * (UNIT0["B"] + 1)))
                act.activation(sq[:, 0, :], ps[:, OBK, :], ACT.Square).then_inc(osq_done, 1)
                if more:
                    exps_b(u + 1, 1)
                if more2:
                    take("B", u + 2, s, 0)
                act.wait_ge(oms_done, u + 1)
                act.activation(rstd[:, :], ps[:, TB, :], ACT.Ln, bias=eps[:, :], scale=float(D // P))\
                   .then_inc(oln_done, 1)
                act.wait_ge(oln_done, u + 1)
                act.activation(rstd[:, :], rstd[:, :], ACT.Exp, scale=-0.5).then_inc(orstd_done, 1)
                if more2:
                    take("B", u + 2, s, 1)
                act.wait_ge(otmp_done, u + 1)
                act.activation(ot_hi[:, bass.ds(u, 1), :], htmp[:, 0, :], ACT.Copy).then_inc(ohi_done, 1)

            for t in range(NT):
                take("B", 0, 0, t)
            first_scores("B", exps_b)
            with act.Fori(0, UB // 2 - 1) as r:
                for s in range(2):
                    unit_b(r * 2 + s, s)
            unit_b(UB - 2, 0, more2=False)
            unit_b(UB - 1, 1, more=False, more2=False)
            after_out(1)
            feed_forward(1)
            for kc in range(KC):
                act.wait_ge(y_tr, kc + 1)
                act.activation(x_tok[:, :, kc * P:(kc + 1) * P],
                               ps[:, kc, :].rearrange("p (t d) -> p t d", t=NT), ACT.Copy)\
                   .then_inc(y_out, 1)

        @block.vector
        def _(dve):
            own = Chain(dve, dve_self)

            def add_squares(norm, dc):
                n = KC * (norm - 1) + dc
                dve.wait_ge(sq_done, n + 1)
                if dc == 0:
                    dve.tensor_copy(ssacc[:, :], sq[:, 0, :]).then_inc(ss_done, 1)
                    return
                if n:
                    dve.wait_ge(ss_done, n)
                dve.tensor_tensor(ssacc[:, :], ssacc[:, :], sq[:, dc % 2, :], ALU.add)\
                   .then_inc(ss_done, 1)

            def normed(norm, kc, gain, done):
                dve.scalar_tensor_tensor(out=htmp[:, kc % 2, :], in0=xT[:, kc, :], scalar=gain,
                                         in1=rstd[:, :], op0=ALU.mult, op1=ALU.mult).then_inc(done, 1)

            def low_h(norm, l, row):
                dve.wait_ge(rstd_done, norm + 1)
                for kc in range(KC + 1):
                    if kc >= 2 and kc < KC:
                        dve.wait_ge(hlo_done, KC * norm + kc - 1)
                    if kc < KC:
                        normed(norm, kc, vecT[:, l, row + kc:row + kc + 1], htmp_done)
                    if kc >= 1:
                        dve.wait_ge(hhi_done, KC * norm + kc)
                        dve.tensor_tensor(h_lo[:, kc - 1, :], htmp[:, (kc - 1) % 2, :],
                                          h_hi[:, kc - 1, :].bitcast(F32), ALU.subtract)\
                           .then_inc(hlo_done, 1)

            def rope(kind, u):
                nh = 6 if kind == "A" else 4
                x_ = qk[:, :, 0:nh * HD].rearrange("p t (h d) -> p t h d", h=nh)
                c = cos16[:, :, :].unsqueeze(2)
                s = sin16[:, :, :].unsqueeze(2)
                a, b = ropeA[:, :, 0:nh, :], ropeB[:, :, 0:nh, :]
                lo, hi = slice(0, HALF), slice(HALF, ROT)
                dve.wait_ge(proj_out, u * NT + (NT * (UNIT0[kind] + 1)))
                own.mark(dve.tensor_tensor(a, x_[:, :, :, 0:ROT], c.broadcast_to((P, NT, nh, ROT)), ALU.mult))
                own.mark(dve.tensor_tensor(b[:, :, :, lo], x_[:, :, :, hi],
                                           s[:, :, :, lo].broadcast_to((P, NT, nh, HALF)), ALU.mult))
                own.link(dve.tensor_tensor(b[:, :, :, hi], x_[:, :, :, lo],
                                           s[:, :, :, hi].broadcast_to((P, NT, nh, HALF)), ALU.mult))
                dve.tensor_tensor(x_[:, :, :, 0:ROT], a, b, ALU.add).then_inc(rope_done, 1)

            def low_v(kind, u, s, t):
                dve.wait_ge(proj_out, u * NT + (NT * UNIT0[kind] + t + 1))
                dst, src = values(kind, v_lo, s, t)
                dve.tensor_tensor(dst, src, values(kind, v_hi, s, t)[0].bitcast(F32), ALU.subtract)\
                   .then_inc(vlo_done, 1)

            def low_t(kind, u, name):
                n = int(name[1]) * P + P if kind == "B" and name[0] == "p" else T
                dve.wait_ge(thi_done, fill_no(kind, u, name))
                dve.tensor_tensor(split_of(kind, name, qt_lo, pt_lo), ps[:, TB, 0:n],
                                  split_of(kind, name, qt_hi, pt_hi).bitcast(F32), ALU.subtract)\
                   .then_inc(tlo_done, 1)

            def maxima_a(u, t):
                lo = 0 if t else P
                s = ps[:, s_bank(t):s_bank(t) + 2, :].rearrange("p b (h k) -> p (b h) k", h=2)
                sink = nsink[:, 4 * u:4 * u + 4]
                dve.wait_ge(s_done, NT * u + t + 1)
                own.link(dve.tensor_reduce(den[:, t, :], s[:, :, lo:], AX.X, ALU.max, negate=True))
                own.link(dve.scalar_tensor_tensor(out=nb[:, t, :], in0=den[:, t, :], scalar=SCALE,
                                                  in1=sink, op0=ALU.mult, op1=ALU.min))
                dve.tensor_tensor(sd[:, t, :], nb[:, t, :], sink, ALU.subtract).then_inc(nb_done, 1)

            def divide_a(u, t):
                lo = 0 if t else P
                dve.wait_ge(exp_done, NT * u + t + 1)
                own.link(dve.tensor_tensor(den[:, t, :], rowsum[:, t, :], es[:, t, :], ALU.add))
                own.link(dve.reciprocal(rden[:, t, :], den[:, t, :]))
                p = prob[:, t % 2, :].rearrange("p (h k) -> p h k", h=4)[:, :, lo:]
                r = rden[:, t, :].unsqueeze(2).broadcast_to((P, 4, 256 - lo))
                dve.tensor_tensor(p, p, r, ALU.mult).then_inc(p_done, 1)

            def maxima_b(u, t):
                n = (t + 1) * P
                dve.wait_ge(s_done, u * NT + (NT * UNIT0["B"] + t + 1))
                own.link(dve.tensor_reduce(den[:, t, 0:2], ps[:, s_bank(t):s_bank(t) + 2, 0:n], AX.X,
                                           ALU.max, negate=True))
                dve.tensor_scalar(nb[:, t, 0:2], den[:, t, 0:2], SCALE, None, ALU.mult)\
                   .then_inc(nb_done, 1)

            def combine_b(u, t):
                n = (t + 1) * P
                dve.wait_ge(exp_done, u * NT + (NT * UNIT0["B"] + t + 1))
                own.link(dve.reciprocal(rden[:, t, 0:2], rowsum[:, t, 0:2]))
                own.link(dve.tensor_scalar(rden[:, t, 2:3], rden[:, t, 1:2], neglam[:, :], None, ALU.mult))
                p0, p1 = prob[:, t % 2, 0:n], prob[:, t % 2, T:T + n]
                own.link(dve.tensor_scalar(p1, p1, rden[:, t, 2:3], None, ALU.mult))
                dve.scalar_tensor_tensor(out=p0, in0=p0, scalar=rden[:, t, 0:1], in1=p1, op0=ALU.mult,
                                         op1=ALU.add).then_inc(p_done, 1)

            dve.wait_ge(pos_landed, 16)
            dve.tensor_copy(pos_f[:, :], pos_i[:, :]).then_inc(pos_done, 1)
            dve.wait_ge(posT_tr, 1)
            dve.tensor_copy(posT[:, :], ps[:, 7, 0:NT]).then_inc(posT_done, 1)

            dve.wait_ge(posT_done, 1)
            dve.wait_ge(const_done, 1 + HALF)
            own.link(dve.tensor_tensor(ang[:, :, :], posT[:, :].unsqueeze(2).broadcast_to((P, NT, HALF)),
                                       invf[:, :].unsqueeze(1).broadcast_to((P, NT, HALF)), ALU.mult))
            own.link(dve.tensor_scalar(turns[:, :, :], ang[:, :, :], 1.0 / (2 * math.pi), ROUND,
                                       ALU.mult, ALU.add))
            own.link(dve.tensor_scalar(turns[:, :, :], turns[:, :, :], ROUND, None, ALU.subtract))
            for part in TWO_PI_PARTS:
                own.link(dve.scalar_tensor_tensor(out=ang[:, :, :], in0=turns[:, :, :], scalar=-part,
                                                  in1=ang[:, :, :], op0=ALU.mult, op1=ALU.add))
            own.link(dve.tensor_scalar(ang[:, :, :], ang[:, :, :], PI_BELOW, -PI_BELOW, ALU.min, ALU.max))
            own.link(dve.tensor_scalar(angneg[:, :, :], ang[:, :, :], -1.0, None, ALU.mult))
            own.link(dve.tensor_tensor(angneg[:, :, :], ang[:, :, :], angneg[:, :, :], ALU.max))
            dve.tensor_scalar(angcos[:, :, :], angneg[:, :, :], -1.0, math.pi / 2, ALU.mult, ALU.add)\
               .then_inc(ang_done, 1)
            dve.wait_ge(ident_done, 1)
            for t in range(NT):
                dve.wait_ge(x_sq, t + 1)
                dve.tensor_scalar(ssacc[:, t * P:(t + 1) * P], ident[:, :], x_ss[:, t:t + 1], None, ALU.mult)\
                   .then_inc(x_diag, 1)
            for kc in range(KC):
                dve.wait_ge(x_tr, kc + 1)
                dve.tensor_copy(xT[:, kc, :], ps[:, kc, :]).then_inc(x_ready, 1)
            dve.wait_ge(vecT_tr, 1)
            own.mark(dve.tensor_copy(vecT[:, 0, 0:R_FINAL], ps[:, 0, 0:R_FINAL]))
            own.link(dve.tensor_copy(vecT[:, 1, :], ps[:, 0, P:P + R_ALL]))
            low_h(NORM["A"], 0, R_ATTN)

            dve.wait_ge(lam_landed, 64)
            for i in range(2):
                ins = dve.tensor_tensor_reduce(lam[:, 2 * i, :], lam[:, 2 * i, :], lam[:, 2 * i + 1, :], 1.0,
                                               0.0, ALU.mult, ALU.add, lam_s[:, i:i + 1])
                if i == 0:
                    own.mark(ins)
            ins.then_inc(lam_sum, 1)
            dve.wait_ge(lam_exp, 1)
            own.link(dve.tensor_tensor(neglam[:, :], lam_s[:, 3:4], lam_s[:, 2:3], ALU.subtract))
            own.link(dve.tensor_scalar(neglam[:, :], neglam[:, :], LAMBDA_INIT, None, ALU.subtract))
            own.link(dve.tensor_scalar(gainB[:, :], vecT[:, 1, R_SUBLN:R_SUBLN + 1], 1.0 - LAMBDA_INIT,
                                       None, ALU.mult))
            dve.wait_ge(sink_landed, 16)
            own.link(dve.tensor_scalar(nsink[:, :].rearrange("p (u e c) -> p u e c", u=UA, e=2),
                                       sink_in[:, :].rearrange("p (u c e) -> p u e c", u=UA, e=2),
                                       -1.0, None, ALU.mult))
            dve.wait_ge(trig_done, 1)

            def first_scores(kind, maxima, divide):
                for t in range(NT):
                    low_v(kind, 0, 0, t)
                rope(kind, 0)
                for c in range(QFILLS[kind]):
                    low_t(kind, -1, f"q{c}")
                maxima(0, 0)
                maxima(0, 1)
                low_v(kind, 1, 1, 0)
                divide(0, 0)
                low_v(kind, 1, 1, 1)

            def low_out_a(u, t):
                dve.wait_ge(ohi_done, NT * u + t + 1)
                for e in range(2):
                    dst, src = outputs_a(ot_lo, u, t, e)
                    ins = dve.tensor_tensor(dst, src, outputs_a(ot_hi, u, t, e)[0].bitcast(F32),
                                            ALU.subtract)
                    if e == 0:
                        own.mark(ins)
                ins.then_inc(olo_done, 1)

            first_scores("A", maxima_a, divide_a)
            for u in range(UA):
                more, more2 = u + 1 < UA, u + 2 < UA
                low_t("A", u, "p0b")
                divide_a(u, 1)
                low_out_a(u, 0)
                maxima_a(u, 2)
                if more:
                    low_v("A", u + 1, (u + 1) % 2, 2)
                low_t("A", u, "p1a")
                low_t("A", u, "p1b")
                if more:
                    low_v("A", u + 1, (u + 1) % 2, 3)
                    rope("A", u + 1)
                divide_a(u, 2)
                low_out_a(u, 1)
                maxima_a(u, 3)
                if more:
                    low_t("A", u, "q0")
                low_t("A", u, "p2a")
                low_t("A", u, "p2b")
                divide_a(u, 3)
                if more:
                    low_t("A", u, "q1")
                low_out_a(u, 2)
                if more:
                    low_t("A", u, "q2")
                if more2:
                    low_v("A", u + 2, u % 2, 0)
                low_t("A", u, "p3a")
                if more:
                    maxima_a(u + 1, 0)
                low_t("A", u, "p3b")
                if more2:
                    low_v("A", u + 2, u % 2, 1)
                low_out_a(u, 3)
                if more:
                    divide_a(u + 1, 0)
                    maxima_a(u + 1, 1)

            def add_to_stream(norm, dc, done, n, bank):
                if dc < KC:
                    dve.wait_ge(done, n + dc + 1)
                    dve.tensor_tensor(xT[:, dc, :], xT[:, dc, :], ps[:, bank, :], ALU.add)\
                       .then_inc(x_ready, 1)
                if dc >= 1:
                    add_squares(norm, dc - 1)

            def after_out(l):
                norm = NORM["F0"] if l == 0 else NORM["F1"]
                for dc in range(KC + 1):
                    add_to_stream(norm, dc, oproj_done, KC * l, dc % 4)
                low_h(norm, l, R_FFN)

            def low_u(l, s, f):
                dve.wait_ge(uhi_done, f + (FB * l + 1))
                dve.tensor_tensor(u_lo[:, s, :], u_all[:, bass.ds(f, 1), :].rearrange("p a b -> p (a b)"),
                                  u_hi[:, s, :].bitcast(F32), ALU.subtract).then_inc(ulo_done, 1)

            def gate(l, s, f):
                def w(row):
                    return vecT[:, l, bass.ds(f + row, 1)]
                a, g, c = ps[:, 2 * s, :], ps[:, 2 * s + 1, :], conv[:, s, :]
                dve.wait_ge(up_done, f + (FB * l + 1))
                own.link(dve.tensor_scalar(c, a, w(R_CONVW + 2 * FB), w(R_CONVB), ALU.mult, ALU.add))
                own.link(dve.scalar_tensor_tensor(out=c[:, 1:], in0=a[:, 0:T - 1], scalar=w(R_CONVW + FB),
                                                  in1=c[:, 1:], op0=ALU.mult, op1=ALU.add))
                dve.scalar_tensor_tensor(out=c[:, 2:], in0=a[:, 0:T - 2], scalar=w(R_CONVW),
                                         in1=c[:, 2:], op0=ALU.mult, op1=ALU.add).then_inc(conv_done, 1)
                dve.wait_ge(silu_done, f + (FB * l + 1))
                dve.tensor_tensor(u_all[:, bass.ds(f, 1), :].rearrange("p a b -> p (a b)"), gated[:, s, :],
                                  g, ALU.mult).then_inc(u_done, 1)

            def feed_forward(l):
                with dve.Fori(0, FB // 2 - 1) as r:
                    own.enter(r, 4)
                    for s in range(2):
                        gate(l, s, r * 2 + s)
                own.leave(FB // 2 - 1)
                for s in range(2):
                    gate(l, s, FB - 2 + s)
                    low_u(l, s, s)
                with dve.Fori(0, FB // 2 - 1) as r:
                    for s in range(2):
                        low_u(l, s, r * 2 + (s + 2))
                norm = NORM["B"] if l == 0 else NORM["end"]
                for dc in range(KC + 1):
                    add_to_stream(norm, dc, down_done, KC * l, (4 + dc) % 8)

            after_out(0)
            feed_forward(0)
            low_h(NORM["B"], 1, R_ATTN)

            def unit_b(u, s, more=True, more2=True):
                low_t("B", u, "p0")
                combine_b(u, 1)
                maxima_b(u, 2)
                if more:
                    low_v("B", u + 1, 1 - s, 2)
                low_t("B", u, "p1")
                if more:
                    low_v("B", u + 1, 1 - s, 3)
                    rope("B", u + 1)
                combine_b(u, 2)
                maxima_b(u, 3)
                if more:
                    low_t("B", u, "q0")
                low_t("B", u, "p2")
                combine_b(u, 3)
                if more:
                    low_t("B", u, "q1")
                    maxima_b(u + 1, 0)
                low_t("B", u, "p3")
                if more:
                    combine_b(u + 1, 0)
                    maxima_b(u + 1, 1)
                if more2:
                    low_v("B", u + 2, s, 0)
                    low_v("B", u + 2, s, 1)
                dve.wait_ge(orstd_done, u + 1)
                dve.scalar_tensor_tensor(out=htmp[:, 0, :], in0=ps[:, OBK, :], scalar=gainB[:, :],
                                         in1=rstd[:, :], op0=ALU.mult, op1=ALU.mult).then_inc(otmp_done, 1)
                dve.wait_ge(ohi_done, u + (NT * UA + 1))
                dve.tensor_tensor(ot_lo[:, bass.ds(u, 1), :].rearrange("p a b -> p (a b)"), htmp[:, 0, :],
                                  ot_hi[:, bass.ds(u, 1), :].rearrange("p a b -> p (a b)").bitcast(F32),
                                  ALU.subtract).then_inc(olo_done, 1)

            first_scores("B", maxima_b, combine_b)
            with dve.Fori(0, UB // 2 - 1) as r:
                own.enter(r, PER_UNIT_B * 2)
                for s in range(2):
                    unit_b(r * 2 + s, s)
            own.leave(UB // 2 - 1)
            unit_b(UB - 2, 0, more2=False)
            unit_b(UB - 1, 1, more=False, more2=False)
            after_out(1)
            feed_forward(1)
            dve.wait_ge(rstd_done, NORM["end"] + 1)
            for kc in range(KC):
                if kc >= 2:
                    dve.wait_ge(y_tr, kc - 1)
                normed(NORM["end"], kc, vecT[:, 1, R_FINAL + kc:R_FINAL + kc + 1], y_done)


def inv_freq(i):
    import numpy as np
    return float(np.power(np.float32(THETA), np.float32(-2.0 * i / ROT), dtype=np.float32))


_INS = ["x", "positions", "attn_norm", "ffn_norm", "ffn_w_up", "ffn_conv_w", "ffn_conv_b", "ffn_w_down",
        "a_w_in", "a_sinks", "a_w_out", "b_w_in", "b_lam_q1", "b_lam_k1", "b_lam_q2", "b_lam_k2",
        "b_subln", "b_w_out", "final_norm"]


def kernel(**inputs):
    import numpy as _np
    import concourse.bacc as _bacc
    from concourse import mybir as _mybir
    from concourse.bass_utils import run_bass_kernel_spmd as _run

    nc = _bacc.Bacc("TRN2", target_bir_lowering=False, num_devices=1)
    arrays, args = {}, []
    for name in _INS:
        a = _np.ascontiguousarray(inputs[name])
        arrays[f"in_{name}"] = a
        args.append(nc.dram_tensor(f"in_{name}", a.shape, _mybir.dt.from_np(a.dtype),
                                   kind="ExternalInput").ap())
    args.append(nc.dram_tensor("out_0", (1, T, D), _mybir.dt.float32, kind="ExternalOutput").ap())
    trunk(nc, *args)
    r = _run(nc, [arrays], core_ids=[0])
    return r.results[0]["out_0"]
```

```python
from contextlib import ExitStack
from itertools import chain
import math

import concourse.bass as bass
from concourse import mybir

P = 128
T = 512
NT = T // P
D = 1024
KC = D // P
HD = 64
UW = 384
F = 2816
FB = F // P
CONVW = 3
EPS = 1e-6
NEG = -1e30
SCALE = HD ** -0.5
THETA, ROT = 500000.0, HD // 4
HALF = ROT // 2
LAMBDA_INIT = 0.8 - 0.6 * math.exp(-0.3 * 1)
TWO_PI_PARTS = (6.28125, 0.0019350051879882812, 3.019916050561733e-07)
ROUND = 12582912.0
PI_BELOW = 3.1415925

UA, UB = 4, 8
OB, ODC = 4, 2

PHASES = {}
_first = _landed = _parts = 0
for _name, _n, _cols, _dmas, _cut in (
        ("attnA", UA, KC * UW, 3, 4), ("outA", OB, KC * ODC * P, 1, 1),
        ("up0", FB, KC * 2 * P, 2, 1), ("down0", FB, D, 1, 1),
        ("attnB", UB, KC * UW, 3, 4), ("outB", OB, KC * ODC * P, 1, 1),
        ("up1", FB, KC * 2 * P, 2, 1), ("down1", FB, D, 1, 1)):
    PHASES[_name] = (_first, _n, _cols, _dmas, _landed, _cut, _parts)
    _first += _n
    _landed += 16 * _dmas * (_n // 2)
    _parts += _cut * _n
ORDER = list(PHASES)
PER_UNIT_B = 3 + 4 * 4

R_CONVW, R_CONVB, R_ATTN, R_FFN, R_FINAL, R_SUBLN, R_ALL = 0, 66, 88, 96, 104, 112, 113

CONSTS = 1 + HALF + 4 + 10

ALU = mybir.AluOpType
ACT = mybir.ActivationFunctionType
AX = mybir.AxisListType
F32 = mybir.dt.float32
F32R = mybir.dt.float32r
BF16 = mybir.dt.bfloat16
I32 = mybir.dt.int32


class Chain:

    def __init__(self, eng, sem):
        self.eng, self.sem, self.base, self.k = eng, sem, 0, 0

    def link(self, ins):
        ins.then_inc(self.sem, 1)
        self.k += 1
        self.eng.wait_ge(self.sem, self.base + self.k)

    def mark(self, ins):
        ins.then_inc(self.sem, 1)
        self.k += 1

    def enter(self, r, per):
        self.start, self.per = self.base + self.k, per
        self.base, self.k = r * per + self.start, 0

    def leave(self, turns):
        assert self.k == self.per, (self.k, self.per)
        self.base, self.k = self.start + self.per * turns, 0


def trunk(nc, x, positions, attn_norm, ffn_norm, ffn_w_up, ffn_conv_w, ffn_conv_b, ffn_w_down,
          a_w_in, a_sinks, a_w_out, b_w_in, b_lam_q1, b_lam_k1, b_lam_q2, b_lam_k2, b_subln,
          b_w_out, final_norm, out):
    ctx = ExitStack()
    with ctx:
        def sb(name, shape, dt=F32, stack=ctx):
            return stack.enter_context(nc.sbuf_tensor(name, shape, dt))

        def sem(name):
            return ctx.enter_context(nc.semaphore(name))

        xT = sb("xT", [P, KC, T])
        h_hi = sb("h_hi", [P, KC, T], F32R)
        h_lo = sb("h_lo", [P, KC, T], F32R)
        raw = sb("raw", [P, 2, KC * UW])
        w_hi = sb("w_hi", [P, 2, KC * UW], F32R)
        w_lo = sb("w_lo", [P, 2, KC * UW], F32R)
        htmp = sb("htmp", [P, 2, T])
        sq = sb("sq", [P, 2, T])
        rstd = sb("rstd", [P, T])
        ident = sb("ident", [P, P])
        ones_d = sb("ones_d", [P, P])
        eps = sb("eps", [P, 1])
        mask_q = sb("mask_q", [P, P], BF16)
        mask_k = sb("mask_k", [P, 2 * P], BF16)
        vecT = sb("vecT", [P, 2, R_ALL])
        nsink = sb("nsink", [P, UA * 4])
        lam_s = sb("lam_s", [P, 4])
        neglam = sb("neglam", [P, 1])
        gainB = sb("gainB", [P, 1])
        cos16 = sb("cos16", [P, NT, ROT])
        sin16 = sb("sin16", [P, NT, ROT])
        ropeA = htmp[:, 1, 0:NT * 6 * ROT].rearrange("p (t h d) -> p t h d", t=NT, h=6)
        ropeB = sq[:, 1, 0:NT * 6 * ROT].rearrange("p (t h d) -> p t h d", t=NT, h=6)
        nb = sb("nb", [P, NT, 4])
        sd = sb("sd", [P, NT, 4])
        es = sb("es", [P, NT, 4])
        rowsum = sb("rowsum", [P, NT, 4])
        den = sb("den", [P, NT, 4])
        rden = sb("rden", [P, NT, 4])

        with ExitStack() as st:
            ot_hi = sb("ot_hi", [P, KC, T], F32R, st)
            ot_lo = sb("ot_lo", [P, KC, T], F32R, st)
            qk = sb("qk", [P, NT, UW], F32, st)
            qt_hi = sb("qt_hi", [P, 3, T], F32R, st)
            qt_lo = sb("qt_lo", [P, 3, T], F32R, st)
            v_hi = sb("v_hi", [P, 2, NT, P], F32R, st)
            v_lo = sb("v_lo", [P, 2, NT, P], F32R, st)
            prob = sb("prob", [P, 2, 1024], F32, st)
            pt_hi = sb("pt_hi", [P, 2, T], F32R, st)
            pt_lo = sb("pt_lo", [P, 2, T], F32R, st)
        with ExitStack() as st:
            u_all = sb("u_all", [P, FB, T], F32, st)
            u_hi = sb("u_hi", [P, 2, T], F32R, st)
            u_lo = sb("u_lo", [P, 2, T], F32R, st)
            conv = sb("conv", [P, 2, T], F32, st)
            gated = sb("gated", [P, 2, T], F32, st)
            ssacc = sb("ssacc", [P, T], F32, st)
        with ExitStack() as st:
            x_tok = sb("x_tok", [P, NT, D], F32, st)
            vrow = sb("vrow", [P, 2, P], F32, st)
            pos_i = sb("pos_i", [NT, P], I32, st)
            pos_f = sb("pos_f", [NT, P], F32, st)
            posT = sb("posT", [P, NT], F32, st)
            x_ss = sb("x_ss", [P, NT], F32, st)
            invf = sb("invf", [P, HALF], F32, st)
            ang = sb("ang", [P, NT, HALF], F32, st)
            turns = sb("turns", [P, NT, HALF], F32, st)
            angneg = sb("angneg", [P, NT, HALF], F32, st)
            lam = sb("lam", [P, 4, HD], F32, st)
            sink_in = sb("sink_in", [P, UA * 4], F32, st)
            angcos = sb("angcos", [P, NT, HALF], F32, st)

        ps = ctx.enter_context(nc.psum_tensor("ps", [P, 8, T], F32))
        PJ, TB, OBK = (0, 1), 6, 7

        def s_bank(t):
            return 2 + 2 * (t % 2)

        x_landed = [sem(f"x_landed{t}") for t in range(NT)]
        vec_landed = sem("vec_landed")
        sink_landed = sem("sink_landed")
        lam_landed = sem("lam_landed")
        pos_landed = sem("pos_landed")
        raw_landed = [sem("raw_landed0"), sem("raw_landed1")]
        hi_done = sem("hi_done")
        lo_done = sem("lo_done")
        const_done = sem("const_done")
        ident_done = sem("ident_done")
        pos_done = sem("pos_done")
        posT_tr = sem("posT_tr")
        posT_done = sem("posT_done")
        ang_done = sem("ang_done")
        trig_done = sem("trig_done")
        vecT_tr = sem("vecT_tr")
        vecT_done = sem("vecT_done")
        nsink_done = sem("nsink_done")
        lam_sum = sem("lam_sum")
        lam_exp = sem("lam_exp")
        x_tr = sem("x_tr")
        x_sq = sem("x_sq")
        x_diag = sem("x_diag")
        x_ready = sem("x_ready")
        sq_done = sem("sq_done")
        ss_done = sem("ss_done")
        ms_done = sem("ms_done")
        ln_done = sem("ln_done")
        rstd_done = sem("rstd_done")
        htmp_done = sem("htmp_done")
        hhi_done = sem("hhi_done")
        hlo_done = sem("hlo_done")
        proj_done = sem("proj_done")
        proj_out = sem("proj_out")
        rope_done = sem("rope_done")
        vlo_done = sem("vlo_done")
        tr_done = sem("tr_done")
        thi_done = sem("thi_done")
        tlo_done = sem("tlo_done")
        ptr_done = sem("ptr_done")
        phi_done = sem("phi_done")
        plo_done = sem("plo_done")
        s_done = sem("s_done")
        nb_done = sem("nb_done")
        exp_done = sem("exp_done")
        rden_done = sem("rden_done")
        p_done = sem("p_done")
        pv_done = sem("pv_done")
        ohi_done = sem("ohi_done")
        olo_done = sem("olo_done")
        osq_done = sem("osq_done")
        oms_done = sem("oms_done")
        oln_done = sem("oln_done")
        orstd_done = sem("orstd_done")
        otmp_done = sem("otmp_done")
        oproj_done = sem("oproj_done")
        up_done = sem("up_done")
        conv_done = sem("conv_done")
        silu_done = sem("silu_done")
        u_done = sem("u_done")
        uhi_done = sem("uhi_done")
        ulo_done = sem("ulo_done")
        down_used = sem("down_used")
        down_done = sem("down_done")
        y_done = sem("y_done")
        y_tr = sem("y_tr")
        y_out = sem("y_out")
        stored = sem("stored")
        dve_self = sem("dve_self")

        def values(kind, dst, s, t):
            src = ps[:, PJ[t % 2], 2 * P:UW]
            if kind == "B":
                return dst[:, s, t, :], src
            return (dst[:, s, t, :].rearrange("p (c d) -> p c d", c=2),
                    src[:, HD:].unsqueeze(1).broadcast_to((P, 2, HD)))

        def probs(kind, dst, t):
            if kind == "B":
                n = (t + 1) * P
                return dst[:, t % 2, 0:n], ps[:, s_bank(t), 0:n]
            if t == 0:
                return dst[:, 1, :], ps[:, s_bank(t) + 1, :]
            return dst[:, :, :], ps[:, s_bank(t):s_bank(t) + 2, :]

        def outputs_a(dst, u, t, e):
            rows = slice(e * HD, (e + 1) * HD)
            src = ps[:, OBK, :].rearrange("p (c e q) -> p c e q", c=2, e=2)
            return dst[rows, 2 * u:2 * u + 2, t * P:(t + 1) * P], src[rows, :, e, :]

        block = ctx.enter_context(nc.Block())

        def first(ph):
            return PHASES[ph][0]

        def n_blocks(ph):
            return PHASES[ph][1]

        def landed(ph, s, turn):
            return PHASES[ph][4] + 16 * PHASES[ph][3] * (turn + 1)

        def cols(ph):
            return PHASES[ph][2]

        def parts(ph):
            return PHASES[ph][5]

        def part_done(ph, i, c=None):
            n = parts(ph)
            return i * n + (PHASES[ph][6] + (n if c is None else c + 1))

        UNIT0 = {"A": 0, "B": UA}
        QFILLS = {"A": 3, "B": 2}
        FILL0 = {"A": 0, "B": UA * 3}
        NORM = {"A": 0, "F0": 1, "B": 2, "F1": 3, "end": 4}
        PHASE = {"A": "attnA", "B": "attnB"}

        def fill_no(kind, u, c):
            return u * QFILLS[kind] + (FILL0[kind] + c + 1)

        def tile_no(kind, u, t):
            return u * NT + (NT * UNIT0[kind] + t + 1)

        def layer(ph):
            return 0 if first(ph) < first("attnB") else 1

        def wait_used(eng, ph, i):
            l = layer(ph)
            if ph[:4] == "attn":
                eng.wait_ge(proj_done, i * NT + (NT * (UNIT0[ph[4]] + 1)))
            elif ph[:3] == "out":
                eng.wait_ge(oproj_done, i * ODC + (KC * l + ODC))
            elif ph[:2] == "up":
                eng.wait_ge(up_done, i + (FB * l + 1))
            elif isinstance(i, int) and i == FB - 1:
                eng.wait_ge(down_done, KC * (l + 1))
            else:
                eng.wait_ge(down_used, i + ((FB - 1) * l + 1))

        @block.sync
        def _(sp):
            xv = x.rearrange("b (t p) d -> p (b t) d", p=P)
            sp.dma_start(pos_i[:, :], positions.rearrange("b (t p) -> (b t) p", p=P))\
              .then_inc(pos_landed, 16)
            for t in range(NT):
                sp.dma_start(x_tok[:, t, :], xv[:, t, :]).then_inc(x_landed[t], 16)

            def load(ph, s, turn, wait):
                i = 2 * turn + s
                if wait == "own":
                    sp.wait_ge(lo_done, part_done(ph, i - 2))
                elif wait == "before":
                    q = ORDER[ORDER.index(ph) - 1]
                    sp.wait_ge(lo_done, part_done(q, n_blocks(q) - 2 + s))
                if ph[:4] == "attn":
                    w, qw, kvw = (a_w_in, 256, 64) if ph == "attnA" else (b_w_in, P, P)
                    wv = w[0].rearrange("(k p) n -> p k n", p=P)
                    rv = raw[:, s, :].rearrange("p (k n) -> p k n", k=KC)
                    at = qw
                    sp.dma_start(rv[:, :, 0:qw], wv[:, :, bass.ds(i * qw, qw)])\
                      .then_inc(raw_landed[s], 16)
                    for side in range(2):
                        sp.dma_start(rv[:, :, at:at + kvw],
                                     wv[:, :, bass.ds(i * kvw + (D if side == 0 else v_at(ph)), kvw)])\
                          .then_inc(raw_landed[s], 16)
                        at += kvw
                elif ph[:3] == "out":
                    w = a_w_out if ph == "outA" else b_w_out
                    wv = w[0].rearrange("(k p) n -> p k n", p=P)
                    rv = raw[:, s, 0:cols(ph)].rearrange("p (k n) -> p k n", k=KC)
                    sp.dma_start(rv, wv[:, :, bass.ds(i * ODC * P, ODC * P)])\
                      .then_inc(raw_landed[s], 16)
                elif ph[:2] == "up":
                    wv = ffn_w_up[int(ph[2])].rearrange("(k p) n -> p k n", p=P)
                    rv = raw[:, s, 0:cols(ph)].rearrange("p (k g n) -> p k g n", k=KC, g=2)
                    for g in range(2):
                        sp.dma_start(rv[:, :, g, :], wv[:, :, bass.ds(i * P + g * F, P)])\
                          .then_inc(raw_landed[s], 16)
                else:
                    wv = ffn_w_down[int(ph[4])].rearrange("(f p) n -> p f n", p=P)
                    sp.dma_start(raw[:, s, 0:D], wv[:, bass.ds(i, 1), :])\
                      .then_inc(raw_landed[s], 16)

            def v_at(ph):
                return D + 256 if ph == "attnA" else 2 * D

            def vectors(l):
                n = CONVW * FB
                sp.dma_start(vrow[R_CONVW:R_CONVW + n, l, :],
                             ffn_conv_w[l].rearrange("c (f p) -> (c f) p", p=P)).then_inc(vec_landed, 16)
                sp.dma_start(vrow[R_CONVB:R_CONVB + FB, l, :],
                             ffn_conv_b[l].rearrange("(f p) -> f p", p=P)).then_inc(vec_landed, 16)
                sp.dma_start(vrow[R_ATTN:R_ATTN + KC, l, :],
                             attn_norm[l].rearrange("(f p) -> f p", p=P)).then_inc(vec_landed, 16)
                sp.dma_start(vrow[R_FFN:R_FFN + KC, l, :],
                             ffn_norm[l].rearrange("(f p) -> f p", p=P)).then_inc(vec_landed, 16)

            vectors(0)
            vectors(1)
            sp.dma_start(vrow[R_FINAL:R_FINAL + KC, 1, :],
                         final_norm.rearrange("(f p) -> f p", p=P)).then_inc(vec_landed, 16)
            sp.dma_start(vrow[R_SUBLN:R_SUBLN + 1, 1, :], b_subln).then_inc(vec_landed, 16)
            load("attnA", 0, 0, None)
            load("attnA", 1, 0, None)
            sp.dma_start(sink_in[:, :], a_sinks.partition_broadcast(P)).then_inc(sink_landed, 16)
            for i, v in enumerate((b_lam_q1, b_lam_k1, b_lam_q2, b_lam_k2)):
                sp.dma_start(lam[:, i, :], v.partition_broadcast(P)).then_inc(lam_landed, 16)

            for ph in ORDER:
                for s in range(2):
                    if ph != ORDER[0]:
                        load(ph, s, 0, "before")
                if n_blocks(ph) == 4:
                    for s in range(2):
                        load(ph, s, 1, "own")
                else:
                    with sp.Fori(1, n_blocks(ph) // 2) as r:
                        for s in range(2):
                            load(ph, s, r, "own")

            ov = out.rearrange("b (t p) d -> p (b t) d", p=P)
            piece = 2 * P
            for c in range(D // piece):
                sp.wait_ge(y_out, 2 * (c + 1))
                sp.dma_start(ov[:, :, c * piece:(c + 1) * piece],
                             x_tok[:, :, c * piece:(c + 1) * piece]).then_inc(stored, 16)
            sp.wait_ge(stored, 16 * (D // piece))

        @block.gpsimd
        def _(pool):
            pool.memset(ident[:, :], 0.0).then_inc(const_done, 1)
            pool.wait_ge(const_done, 1)
            pool.affine_select(out=ident[:, :], in_=ident[:, :], compare_op=ALU.not_equal, fill=1.0,
                               base=0, pattern=[[-1, P]], channel_multiplier=1).then_inc(ident_done, 1)
            for i in range(HALF):
                pool.memset(invf[:, i:i + 1], inv_freq(i)).then_inc(const_done, 1)
            pool.memset(ones_d[:, :], 1.0 / D).then_inc(const_done, 1)
            pool.memset(eps[:, :], EPS).then_inc(const_done, 1)
            pool.memset(mask_q[:, :], 0.0).then_inc(const_done, 1)
            pool.memset(mask_k[:, :], 0.0).then_inc(const_done, 1)
            pool.wait_ge(const_done, 1 + HALF + 4)
            for row in (0, HD):
                pool.memset(mask_q[row:row + 1, 0:HD], 1.0).then_inc(const_done, 1)
                pool.memset(mask_q[row + 32:row + 33, HD:P], 1.0).then_inc(const_done, 1)
                pool.memset(mask_k[row:row + 1, 0:HD], NEG).then_inc(const_done, 1)
                pool.memset(mask_k[row:row + 1, 3 * HD:4 * HD], NEG).then_inc(const_done, 1)
                pool.memset(mask_k[row + 32:row + 33, 0:2 * HD], NEG).then_inc(const_done, 1)
            pool.wait_ge(const_done, CONSTS)

            def low(ph, s, i):
                n = cols(ph) // parts(ph)
                for c in range(parts(ph)):
                    at = slice(c * n, (c + 1) * n)
                    pool.wait_ge(hi_done, part_done(ph, i, c))
                    pool.tensor_tensor(w_lo[:, s, at], raw[:, s, at], w_hi[:, s, at].bitcast(F32),
                                       ALU.subtract).then_inc(lo_done, 1)

            for ph in ORDER:
                with pool.Fori(0, n_blocks(ph) // 2) as r:
                    for s in range(2):
                        low(ph, s, r * 2 + s)

        @block.tensor
        def _(pe):
            def hi_lo(out_, a_hi, a_lo, b_hi, b_lo, start, stop):
                pe.matmul(out_, a_lo, b_hi, start=start, stop=False)
                pe.matmul(out_, a_hi, b_lo, start=False, stop=False)
                return pe.matmul(out_, a_hi, b_hi, start=False, stop=stop)

            pe.wait_ge(ident_done, 1)
            pe.wait_ge(pos_done, 1)
            pe.transpose(ps[:, 7, 0:NT], pos_f[:, :], ident[0:NT, 0:NT]).then_inc(posT_tr, 1)
            for t in range(NT):
                pe.wait_ge(x_landed[t], 16)
                for kc in range(KC):
                    if t == 0 and kc == KC - 1:
                        pe.wait_ge(posT_done, 1)
                    ins = pe.transpose(ps[:, kc, t * P:(t + 1) * P], x_tok[:, t, kc * P:(kc + 1) * P],
                                       ident[:, :])
                    if t == NT - 1:
                        ins.then_inc(x_tr, 1)
            pe.wait_ge(const_done, CONSTS)
            pe.wait_ge(x_diag, NT)
            pe.wait_ge(x_ready, TB + 1)
            pe.matmul(ps[:, TB, :], ones_d[:, :], ssacc[:, :], start=True, stop=True)\
              .then_inc(ms_done, 1)
            pe.wait_ge(vec_landed, 16 * 10)
            pe.transpose(ps[:, 0, 0:R_FINAL], vrow[0:R_FINAL, 0, :], ident[0:R_FINAL, 0:R_FINAL])
            pe.transpose(ps[:, 0, P:P + R_ALL], vrow[0:R_ALL, 1, :],
                         ident[0:R_ALL, 0:R_ALL]).then_inc(vecT_tr, 1)

            def mean_square(norm):
                pe.wait_ge(ss_done, KC * norm)
                pe.matmul(ps[:, TB, :], ones_d[:, :], ssacc[:, :], start=True, stop=True)\
                  .then_inc(ms_done, 1)

            def projection(kind, u, s, tiles):
                ph = PHASE[kind]
                wh = w_hi[:, s, :].rearrange("p (k n) -> p k n", k=KC)
                wl = w_lo[:, s, :].rearrange("p (k n) -> p k n", k=KC)
                tile0 = NT * (u + UNIT0[kind])
                coming = tiles[0] == 0
                first_unit = isinstance(u, int) and u == 0
                order = [(t, kc) for t in tiles for kc in range(KC)]
                if coming and first_unit:
                    order.sort(key=lambda x: x[1])
                n = 0
                for t, kc in order:
                    tok = slice(t * P, (t + 1) * P)
                    if kc == 0 and not (isinstance(tile0, int) and tile0 + t < 2):
                        pe.wait_ge(vlo_done, tile0 + (t - 1))
                    if t == 0 and kc % 2 == 0:
                        pe.wait_ge(lo_done, part_done(ph, u, kc // 2))
                    if first_unit and t == 0:
                        pe.wait_ge(hlo_done, KC * NORM[kind] + kc + 1)
                    for m, (a, b) in enumerate(((h_lo, wh), (h_hi, wl), (h_hi, wh))):
                        ins = pe.matmul(ps[:, PJ[t % 2], 0:UW], a[:, kc, tok], b[:, kc, :],
                                        start=(kc == 0 and m == 0), stop=(kc == KC - 1 and m == 2))
                        n += 1
                        if kc == KC - 1 and m == 2:
                            ins.then_inc(proj_done, 1)
                        if n % 4 == 0:
                            yield

            def run(slabs, k):
                for _ in range(k):
                    next(slabs, None)

            def transposes(bank, blocks, inputs):
                for (c, i) in zip(blocks, inputs):
                    ins = pe.transpose(ps[:, bank, c * P:(c + 1) * P], i, ident[:, :])
                return ins

            def fill_qk(kind, u, c):
                if c == 0:
                    pe.wait_ge(rope_done, u + (UNIT0[kind] + 1))
                    if kind == "B" and not (isinstance(u, int) and u < 2):
                        pe.wait_ge(oln_done, u - 1)
                if not (kind == "A" and u == 0 and c == 0):
                    pe.wait_ge(tlo_done, fill_no(kind, u, c) - 1)
                transposes(TB, range(NT), [qk[:, t, c * P:(c + 1) * P] for t in range(NT)])\
                    .then_inc(tr_done, 1)

            def start_unit0(kind):
                for tiles in ((0, 1), (2, 3)):
                    for _ in projection(kind, 0, 0, tiles):
                        pass
                slabs = projection(kind, 1, 1, (0, 1))
                run(slabs, 6)
                for c in range(QFILLS[kind]):
                    fill_qk(kind, 0, c)
                    run(slabs, 2)
                scores = scores_a if kind == "A" else scores_b
                scores(0, 0)
                scores(0, 1)
                run(slabs, 24)

            def scores_a(u, t):
                if t == 0:
                    pe.wait_ge(tlo_done, fill_no("A", u, 2))
                if NT * u + t >= 2:
                    pe.wait_ge(plo_done, tile_no("A", u, t - 2))
                q = slice(t * P, (t + 1) * P)
                lo = 0 if t else P
                keys = slice((t - 1) * P if t else 0, (t + 1) * P)
                for e in range(2):
                    rows = slice(e * HD, (e + 1) * HD)
                    bank = ps[:, s_bank(t) + e, :].rearrange("p (h k) -> p h k", h=2)
                    pe.matmul(bank[:, :, lo:], mask_q[rows, :],
                              mask_k[rows, lo:].unsqueeze(1).broadcast_to((HD, 2, 2 * P - lo)),
                              start=True, stop=False)
                    for c in range(2):
                        for m, (a, b) in enumerate(((qt_lo, qt_hi), (qt_hi, qt_lo), (qt_hi, qt_hi))):
                            ins = pe.matmul(bank[:, c, lo:], a[rows, c, q], b[rows, 2, keys],
                                            start=False, stop=(c == 1 and m == 2))
                ins.then_inc(s_done, 1)

            def probs_a(u, t):
                pe.wait_ge(p_done, tile_no("A", u, t))
                for kt in (0, 1) if t else (1,):
                    ins = transposes(s_bank(t) + kt, (0, 2, 1, 3),
                                     [prob[:, t % 2, h * 256 + kt * P:h * 256 + (kt + 1) * P]
                                      for h in range(4)])
                ins.then_inc(ptr_done, 1)

            def values_a(u, t):
                pe.wait_ge(plo_done, tile_no("A", u, t))
                if NT * u + t:
                    pe.wait_ge(olo_done, NT * u + t)
                if t == 0:
                    pe.wait_ge(vlo_done, NT * (u + 1))
                for kt in (0, 1) if t else (1,):
                    v = t - 1 + kt
                    ins = hi_lo(ps[:, OBK, :], v_hi[:, u % 2, v, :], v_lo[:, u % 2, v, :],
                                pt_hi[:, kt, :], pt_lo[:, kt, :], start=(kt == 0 or t == 0),
                                stop=(kt == 1))
                ins.then_inc(pv_done, 1)

            def unit_a(u):
                more = u + 1 < UA
                slabs = chain(projection("A", u + 1, (u + 1) % 2, (2, 3)) if more else (),
                              projection("A", u + 2, u % 2, (0, 1)) if u + 2 < UA else ())
                probs_a(u, 0)
                run(slabs, 5)
                values_a(u, 0)
                scores_a(u, 2)
                run(slabs, 3)
                probs_a(u, 1)
                run(slabs, 4)
                values_a(u, 1)
                scores_a(u, 3)
                if more:
                    run(slabs, 1)
                    fill_qk("A", u + 1, 0)
                probs_a(u, 2)
                run(slabs, 2)
                if more:
                    fill_qk("A", u + 1, 1)
                    run(slabs, 1)
                values_a(u, 2)
                if more:
                    run(slabs, 1)
                    fill_qk("A", u + 1, 2)
                    run(slabs, 2)
                    scores_a(u + 1, 0)
                probs_a(u, 3)
                run(slabs, 3)
                values_a(u, 3)
                if more:
                    scores_a(u + 1, 1)
                run(slabs, 24)

            def scores_b(u, t):
                if t == 0:
                    pe.wait_ge(tlo_done, fill_no("B", u, 1))
                pe.wait_ge(plo_done, tile_no("B", u, t - 2))
                q = slice(t * P, (t + 1) * P)
                n = (t + 1) * P
                for e in range(2):
                    rows = slice(e * HD, (e + 1) * HD)
                    bank = ps[:, s_bank(t) + e, :]
                    for m, (a, b) in enumerate(((qt_lo, qt_hi), (qt_hi, qt_lo), (qt_hi, qt_hi))):
                        pe.matmul(bank[:, 0:n], a[rows, 0, q], b[rows, 1, 0:n], start=(m == 0),
                                  stop=False)
                    ins = pe.matmul(bank[:, n - P:n], mask_q[rows, :], mask_k[rows, P:2 * P],
                                    start=False, stop=True)
                ins.then_inc(s_done, 1)

            def probs_b(u, t):
                pe.wait_ge(p_done, tile_no("B", u, t))
                transposes(s_bank(t), range(t + 1), [prob[:, t % 2, k * P:(k + 1) * P] for k in range(t + 1)])\
                    .then_inc(ptr_done, 1)

            def values_b(u, s, t):
                pe.wait_ge(plo_done, tile_no("B", u, t))
                if t == 0:
                    pe.wait_ge(vlo_done, tile_no("B", u, NT - 1))
                    if not (isinstance(u, int) and u == 0):
                        pe.wait_ge(otmp_done, u)
                o = ps[:, OBK, t * P:(t + 1) * P]
                for k in range(t + 1):
                    ins = hi_lo(o, v_hi[:, s, k, :], v_lo[:, s, k, :], pt_hi[:, t % 2, k * P:(k + 1) * P],
                                pt_lo[:, t % 2, k * P:(k + 1) * P], start=(k == 0), stop=(k == t))
                ins.then_inc(pv_done, 1)

            def unit_b(u, s, more=True, more2=True):
                slabs = chain(projection("B", u + 1, 1 - s, (2, 3)) if more else (),
                              projection("B", u + 2, s, (0, 1)) if more2 else ())
                probs_b(u, 0)
                run(slabs, 4)
                values_b(u, s, 0)
                scores_b(u, 2)
                run(slabs, 4)
                probs_b(u, 1)
                run(slabs, 4)
                values_b(u, s, 1)
                scores_b(u, 3)
                if more:
                    run(slabs, 1)
                    fill_qk("B", u + 1, 0)
                probs_b(u, 2)
                run(slabs, 2)
                if more:
                    fill_qk("B", u + 1, 1)
                    run(slabs, 1)
                values_b(u, s, 2)
                if more:
                    run(slabs, 2)
                    scores_b(u + 1, 0)
                probs_b(u, 3)
                run(slabs, 3)
                values_b(u, s, 3)
                if more:
                    scores_b(u + 1, 1)
                run(slabs, 1)
                pe.wait_ge(osq_done, u + 1)
                pe.matmul(ps[:, TB, :], ones_d[:, :], osq[:, :], start=True, stop=True)\
                  .then_inc(oms_done, 1)
                run(slabs, 24)

            osq = sq[:, 0, :]

            start_unit0("A")
            for u in range(UA):
                unit_a(u)

            def out_projection(l):
                ph, norm = ("outA", "outB")[l], NORM["F0"] if l == 0 else NORM["F1"]
                pe.wait_ge(olo_done, NT * UA + UB * l)
                with pe.Fori(0, OB // 2) as r:
                    for s in range(2):
                        pe.wait_ge(lo_done, part_done(ph, r * 2 + s))
                        wh = w_hi[:, s, 0:cols(ph)].rearrange("p (k n) -> p k n", k=KC)
                        wl = w_lo[:, s, 0:cols(ph)].rearrange("p (k n) -> p k n", k=KC)
                        for e in range(ODC):
                            j = ODC * s + e
                            pe.wait_ge(x_ready, r * 4 + (KC * norm + j - 3))
                            for kc in range(KC):
                                c = slice(e * P, (e + 1) * P)
                                ins = hi_lo(ps[:, j, :], wh[:, kc, c], wl[:, kc, c], ot_hi[:, kc, :],
                                            ot_lo[:, kc, :], start=(kc == 0), stop=(kc == KC - 1))
                            ins.then_inc(oproj_done, 1)

            def up_pair(l, r, is_first):
                ph, norm = f"up{l}", NORM["F0"] if l == 0 else NORM["F1"]
                for s in range(2):
                    pe.wait_ge(lo_done, part_done(ph, r * 2 + s))
                    if not is_first:
                        pe.wait_ge(u_done, r * 2 + (FB * l + s - 1))
                    wh = w_hi[:, s, 0:cols(ph)].rearrange("p (k g n) -> p k g n", k=KC, g=2)
                    wl = w_lo[:, s, 0:cols(ph)].rearrange("p (k g n) -> p k g n", k=KC, g=2)
                    order = [(g, kc) for g in range(2) for kc in range(KC)]
                    if is_first and s == 0:
                        order.sort(key=lambda x: x[1])
                    for g, kc in order:
                        if is_first and s == 0 and g == 0:
                            pe.wait_ge(hlo_done, KC * norm + kc + 1)
                        ins = hi_lo(ps[:, 2 * s + g, :], wh[:, kc, g, :], wl[:, kc, g, :],
                                    h_hi[:, kc, :], h_lo[:, kc, :], start=(kc == 0),
                                    stop=(kc == KC - 1))
                    ins.then_inc(up_done, 1)

            def down_pair(l, r, is_first, is_last):
                ph = f"down{l}"
                for s in range(2):
                    pe.wait_ge(lo_done, part_done(ph, r * 2 + s))
                    pe.wait_ge(ulo_done, r * 2 + (FB * l + s + 1))
                    for dc in range(KC):
                        if is_first and s == 0 and dc == 4:
                            pe.wait_ge(u_done, FB * (l + 1))
                        c = slice(dc * P, (dc + 1) * P)
                        ins = hi_lo(ps[:, (4 + dc) % 8, :], w_hi[:, s, c], w_lo[:, s, c],
                                    u_hi[:, s, :], u_lo[:, s, :], start=(is_first and s == 0),
                                    stop=(is_last and s == 1))
                        if is_last and s == 1:
                            ins.then_inc(down_done, 1)
                    if not (is_last and s == 1):
                        ins.then_inc(down_used, 1)

            def feed_forward(l):
                mean_square(NORM["F0"] if l == 0 else NORM["F1"])
                up_pair(l, 0, True)
                with pe.Fori(1, FB // 2) as r:
                    up_pair(l, r, False)
                down_pair(l, 0, True, False)
                with pe.Fori(1, FB // 2 - 1) as r:
                    down_pair(l, r, False, False)
                down_pair(l, FB // 2 - 1, False, True)

            out_projection(0)
            feed_forward(0)

            mean_square(NORM["B"])
            start_unit0("B")
            unit_b(0, 0)
            unit_b(1, 1)
            with pe.Fori(1, UB // 2 - 1) as r:
                for s in range(2):
                    unit_b(r * 2 + s, s)
            unit_b(UB - 2, 0, more2=False)
            unit_b(UB - 1, 1, more=False, more2=False)
            out_projection(1)
            feed_forward(1)

            mean_square(NORM["end"])
            for kc in range(KC):
                pe.wait_ge(y_done, kc + 1)
                if kc == TB:
                    pe.wait_ge(rstd_done, 5)
                for t in range(NT):
                    ins = pe.transpose(ps[:, kc, t * P:(t + 1) * P], htmp[:, kc % 2, t * P:(t + 1) * P],
                                       ident[:, :])
                ins.then_inc(y_tr, 1)

        @block.scalar
        def _(act):
            def high(ph, s, turn, used=None, c=0):
                if c >= parts(ph):
                    return
                n = cols(ph) // parts(ph)
                at = slice(c * n, (c + 1) * n)
                if used is not None and c == 0:
                    wait_used(act, *used)
                if c == 0:
                    act.wait_ge(raw_landed[s], landed(ph, s, turn) if isinstance(turn, int)
                                else turn * (16 * PHASES[ph][3]) + landed(ph, s, 0))
                act.activation(w_hi[:, s, at], raw[:, s, at], ACT.Copy).then_inc(hi_done, 1)

            def high_after(ph, b, c=0):
                if b + 2 < n_blocks(ph):
                    high(ph, b % 2, b // 2 + 1, (ph, b), c)
                elif ph != ORDER[-1]:
                    high(ORDER[ORDER.index(ph) + 1], b % 2, 0, (ph, b), c)

            def square(norm, dc):
                act.wait_ge(x_ready, KC * norm + dc + 1)
                if KC * (norm - 1) + dc >= 2:
                    act.wait_ge(ss_done, KC * (norm - 1) + dc - 1)
                act.activation(sq[:, dc % 2, :], xT[:, dc, :], ACT.Square).then_inc(sq_done, 1)

            def rsqrt(norm):
                act.wait_ge(ms_done, norm + 1)
                act.activation(rstd[:, :], ps[:, TB, :], ACT.Ln, bias=eps[:, :]).then_inc(ln_done, 1)
                act.wait_ge(ln_done, norm + 1)
                act.activation(rstd[:, :], rstd[:, :], ACT.Exp, scale=-0.5).then_inc(rstd_done, 1)

            def high_h(norm, between):
                for kc in range(KC):
                    act.wait_ge(htmp_done, KC * norm + kc + 1)
                    act.activation(h_hi[:, kc, :], htmp[:, kc % 2, :], ACT.Copy).then_inc(hhi_done, 1)
                    between(kc)

            def take(kind, u, s, t):
                n = u * NT + (NT * UNIT0[kind] + t)
                act.wait_ge(proj_done, n + 1)
                bank = ps[:, PJ[t % 2], :]
                if kind == "A":
                    act.activation(qk[:, t, 5 * HD:6 * HD], bank[:, 4 * HD:5 * HD], ACT.Copy)
                    act.activation(qk[:, t, 0:5 * HD], bank[:, 0:5 * HD], ACT.Copy)
                else:
                    act.activation(qk[:, t, 0:2 * P], bank[:, 0:2 * P], ACT.Copy)
                dst, src = values(kind, v_hi, s, t)
                act.activation(dst, src, ACT.Copy).then_inc(proj_out, 1)

            def high_qk(kind, u, c):
                act.wait_ge(tr_done, fill_no(kind, u, c))
                act.activation(qt_hi[:, c, :], ps[:, TB, :], ACT.Copy).then_inc(thi_done, 1)

            def high_p(kind, u, t):
                act.wait_ge(ptr_done, tile_no(kind, u, t))
                act.activation(*probs(kind, pt_hi, t), ACT.Copy).then_inc(phi_done, 1)

            def exps_a(u, t):
                lo = 0 if t else P
                act.wait_ge(nb_done, NT * u + t + 1)
                act.activation(es[:, t, :], sd[:, t, :], ACT.Exp)
                for h in range(4):
                    s = ps[:, s_bank(t) + h // 2, (h % 2) * 256 + lo:(h % 2 + 1) * 256]
                    ins = act.activation(prob[:, t % 2, h * 256 + lo:(h + 1) * 256], s, ACT.Exp,
                                         bias=nb[:, t, h:h + 1], scale=SCALE,
                                         accum_out=rowsum[:, t, h:h + 1])
                ins.then_inc(exp_done, 1)

            def exps_b(u, t):
                n = (t + 1) * P
                act.wait_ge(nb_done, u * NT + (NT * UNIT0["B"] + t + 1))
                for e in range(2):
                    ins = act.activation(prob[:, t % 2, e * T:e * T + n], ps[:, s_bank(t) + e, 0:n],
                                         ACT.Exp, bias=nb[:, t, e:e + 1], scale=SCALE,
                                         accum_out=rowsum[:, t, e:e + 1])
                ins.then_inc(exp_done, 1)

            act.wait_ge(ang_done, 1)
            act.activation(cos16[:, :, 0:HALF], angcos[:, :, :], ACT.Sin)
            act.activation(cos16[:, :, HALF:ROT], angcos[:, :, :], ACT.Sin)
            act.activation(sin16[:, :, 0:HALF], ang[:, :, :], ACT.Sin, scale=-1.0)
            act.activation(sin16[:, :, HALF:ROT], ang[:, :, :], ACT.Sin).then_inc(trig_done, 1)
            act.preload_act_table_set("natural_log_exp_and_others")
            for t in range(NT):
                act.wait_ge(x_landed[t], 16)
                if t:
                    act.wait_ge(x_sq, t)
                act.activation(sq[:, :, :].rearrange("p a b -> p (a b)"), x_tok[:, t, :], ACT.Square,
                               accum_out=x_ss[:, t:t + 1]).then_inc(x_sq, 1)
            act.wait_ge(const_done, CONSTS)
            rsqrt(NORM["A"])
            high("attnA", 0, 0)

            def weights0(kc):
                if kc % 2 and kc < KC - 1:
                    high("attnA", 0, 0, None, kc // 2 + 1)

            high_h(NORM["A"], weights0)
            act.wait_ge(lam_sum, 1)
            act.activation(lam_s[:, 2:4], lam_s[:, 0:2], ACT.Exp).then_inc(lam_exp, 1)

            for t in range(NT):
                take("A", 0, 0, t)
                high("attnA", 1, 0, None, t)

            def first_scores(kind, exps):
                for c in range(QFILLS[kind]):
                    high_qk(kind, 0, c)
                exps(0, 0)
                take(kind, 1, 1, 0)

            def high_out_a(u, t):
                act.wait_ge(pv_done, NT * u + t + 1)
                for e in range(2):
                    dst, src = outputs_a(ot_hi, u, t, e)
                    ins = act.activation(dst, src, ACT.Copy)
                ins.then_inc(ohi_done, 1)

            first_scores("A", exps_a)
            for u in range(UA):
                more, more2 = u + 1 < UA, u + 2 < UA
                high_p("A", u, 0)
                exps_a(u, 1)
                if more:
                    take("A", u + 1, (u + 1) % 2, 1)
                high_after("attnA", u, 0)
                high_out_a(u, 0)
                high_after("attnA", u, 1)
                high_p("A", u, 1)
                if more:
                    take("A", u + 1, (u + 1) % 2, 2)
                exps_a(u, 2)
                if more:
                    take("A", u + 1, (u + 1) % 2, 3)
                high_out_a(u, 1)
                high_after("attnA", u, 2)
                if more:
                    high_qk("A", u + 1, 0)
                high_p("A", u, 2)
                high_after("attnA", u, 3)
                if more:
                    high_qk("A", u + 1, 1)
                exps_a(u, 3)
                high_out_a(u, 2)
                if more:
                    high_qk("A", u + 1, 2)
                high_p("A", u, 3)
                if more2:
                    take("A", u + 2, u % 2, 0)
                if more:
                    exps_a(u + 1, 0)
                high_out_a(u, 3)

            def after_out(l):
                ph, norm = ("outA", "outB")[l], NORM["F0"] if l == 0 else NORM["F1"]
                for b in range(OB):
                    for e in range(ODC):
                        square(norm, ODC * b + e)
                    if b < OB - 1:
                        high_after(ph, b)
                rsqrt(norm)
                high_h(norm, lambda kc: high_after(ph, OB - 1) if kc == 1 else None)

            def high_u(l, s, f):
                act.wait_ge(u_done, f + (FB * l + 1))
                act.activation(u_hi[:, s, :], u_all[:, bass.ds(f, 1), :], ACT.Copy).then_inc(uhi_done, 1)

            def silu(l, s, f):
                act.wait_ge(conv_done, f + (FB * l + 1))
                act.activation(gated[:, s, :], conv[:, s, :], ACT.Silu).then_inc(silu_done, 1)

            def feed_forward(l):
                up, down = f"up{l}", f"down{l}"
                act.preload_act_table_set("silu_and_others")
                with act.Fori(0, FB // 2 - 1) as r:
                    for s in range(2):
                        high(up, s, r + 1, (up, r * 2 + s))
                        silu(l, s, r * 2 + s)
                for s in range(2):
                    high_after(up, FB - 2 + s)
                    silu(l, s, FB - 2 + s)
                    high_u(l, s, s)
                with act.Fori(0, FB // 2 - 1) as r:
                    for s in range(2):
                        wait_used(act, down, r * 2 + s)
                        high_u(l, s, r * 2 + (s + 2))
                        high(down, s, r + 1)
                act.preload_act_table_set("natural_log_exp_and_others")
                norm = NORM["B"] if l == 0 else NORM["end"]
                for dc in range(KC):
                    square(norm, dc)
                    if dc % 2 and dc > 1:
                        high_after(down, FB - 2, dc // 2 - 1)
                rsqrt(norm)
                high_after(down, FB - 2, 3)

            after_out(0)
            feed_forward(0)

            def weights1(kc):
                if kc % 2:
                    high_after("down0", FB - 1, kc // 2)

            high_h(NORM["B"], weights1)

            def unit_b(u, s, more=True, more2=True):
                def weights(c):
                    if isinstance(u, int):
                        high_after("attnB", u, c)
                    else:
                        high("attnB", s, r + 1, ("attnB", u), c)

                high_p("B", u, 0)
                exps_b(u, 1)
                if more:
                    take("B", u + 1, 1 - s, 1)
                weights(0)
                weights(1)
                high_p("B", u, 1)
                if more:
                    take("B", u + 1, 1 - s, 2)
                exps_b(u, 2)
                if more:
                    take("B", u + 1, 1 - s, 3)
                weights(2)
                if more:
                    high_qk("B", u + 1, 0)
                high_p("B", u, 2)
                weights(3)
                if more:
                    high_qk("B", u + 1, 1)
                exps_b(u, 3)
                high_p("B", u, 3)
                if more:
                    exps_b(u + 1, 0)
                act.wait_ge(pv_done, tile_no("B", u, NT - 1))
                act.activation(sq[:, 0, :], ps[:, OBK, :], ACT.Square).then_inc(osq_done, 1)
                if more2:
                    take("B", u + 2, s, 0)
                act.wait_ge(oms_done, u + 1)
                act.activation(rstd[:, :], ps[:, TB, :], ACT.Ln, bias=eps[:, :], scale=float(D // P))\
                   .then_inc(oln_done, 1)
                act.wait_ge(oln_done, u + 1)
                act.activation(rstd[:, :], rstd[:, :], ACT.Exp, scale=-0.5).then_inc(orstd_done, 1)
                act.wait_ge(otmp_done, u + 1)
                act.activation(ot_hi[:, bass.ds(u, 1), :], htmp[:, 0, :], ACT.Copy).then_inc(ohi_done, 1)

            for t in range(NT):
                take("B", 0, 0, t)
            first_scores("B", exps_b)
            with act.Fori(0, UB // 2 - 1) as r:
                for s in range(2):
                    unit_b(r * 2 + s, s)
            unit_b(UB - 2, 0, more2=False)
            unit_b(UB - 1, 1, more=False, more2=False)
            after_out(1)
            feed_forward(1)
            for kc in range(KC):
                act.wait_ge(y_tr, kc + 1)
                act.activation(x_tok[:, :, kc * P:(kc + 1) * P],
                               ps[:, kc, :].rearrange("p (t d) -> p t d", t=NT), ACT.Copy)\
                   .then_inc(y_out, 1)

        @block.vector
        def _(dve):
            own = Chain(dve, dve_self)

            def add_squares(norm, dc):
                n = KC * (norm - 1) + dc
                dve.wait_ge(sq_done, n + 1)
                if dc == 0:
                    dve.tensor_copy(ssacc[:, :], sq[:, 0, :]).then_inc(ss_done, 1)
                    return
                if n:
                    dve.wait_ge(ss_done, n)
                dve.tensor_tensor(ssacc[:, :], ssacc[:, :], sq[:, dc % 2, :], ALU.add)\
                   .then_inc(ss_done, 1)

            def normed(norm, kc, gain, done):
                dve.scalar_tensor_tensor(out=htmp[:, kc % 2, :], in0=xT[:, kc, :], scalar=gain,
                                         in1=rstd[:, :], op0=ALU.mult, op1=ALU.mult).then_inc(done, 1)

            def low_h(norm, l, row):
                dve.wait_ge(rstd_done, norm + 1)
                for kc in range(KC + 1):
                    if kc >= 2 and kc < KC:
                        dve.wait_ge(hlo_done, KC * norm + kc - 1)
                    if kc < KC:
                        normed(norm, kc, vecT[:, l, row + kc:row + kc + 1], htmp_done)
                    if kc >= 1:
                        dve.wait_ge(hhi_done, KC * norm + kc)
                        dve.tensor_tensor(h_lo[:, kc - 1, :], htmp[:, (kc - 1) % 2, :],
                                          h_hi[:, kc - 1, :].bitcast(F32), ALU.subtract)\
                           .then_inc(hlo_done, 1)

            def rope(kind, u):
                nh = 6 if kind == "A" else 4
                x_ = qk[:, :, 0:nh * HD].rearrange("p t (h d) -> p t h d", h=nh)
                c = cos16[:, :, :].unsqueeze(2)
                s = sin16[:, :, :].unsqueeze(2)
                a, b = ropeA[:, :, 0:nh, :], ropeB[:, :, 0:nh, :]
                lo, hi = slice(0, HALF), slice(HALF, ROT)
                dve.wait_ge(proj_out, u * NT + (NT * (UNIT0[kind] + 1)))
                own.mark(dve.tensor_tensor(a, x_[:, :, :, 0:ROT], c.broadcast_to((P, NT, nh, ROT)), ALU.mult))
                own.mark(dve.tensor_tensor(b[:, :, :, lo], x_[:, :, :, hi],
                                           s[:, :, :, lo].broadcast_to((P, NT, nh, HALF)), ALU.mult))
                own.link(dve.tensor_tensor(b[:, :, :, hi], x_[:, :, :, lo],
                                           s[:, :, :, hi].broadcast_to((P, NT, nh, HALF)), ALU.mult))
                dve.tensor_tensor(x_[:, :, :, 0:ROT], a, b, ALU.add).then_inc(rope_done, 1)

            def low_v(kind, u, s, t):
                dve.wait_ge(proj_out, u * NT + (NT * UNIT0[kind] + t + 1))
                dst, src = values(kind, v_lo, s, t)
                dve.tensor_tensor(dst, src, values(kind, v_hi, s, t)[0].bitcast(F32), ALU.subtract)\
                   .then_inc(vlo_done, 1)

            def low_qk(kind, u, c):
                dve.wait_ge(thi_done, fill_no(kind, u, c))
                dve.tensor_tensor(qt_lo[:, c, :], ps[:, TB, :], qt_hi[:, c, :].bitcast(F32),
                                  ALU.subtract).then_inc(tlo_done, 1)

            def low_p(kind, u, t):
                dve.wait_ge(phi_done, tile_no(kind, u, t))
                dst, src = probs(kind, pt_lo, t)
                dve.tensor_tensor(dst, src, probs(kind, pt_hi, t)[0].bitcast(F32), ALU.subtract)\
                   .then_inc(plo_done, 1)

            def maxima_a(u, t):
                lo = 0 if t else P
                s = ps[:, s_bank(t):s_bank(t) + 2, :].rearrange("p b (h k) -> p (b h) k", h=2)
                sink = nsink[:, 4 * u:4 * u + 4]
                dve.wait_ge(s_done, NT * u + t + 1)
                own.link(dve.tensor_reduce(den[:, t, :], s[:, :, lo:], AX.X, ALU.max, negate=True))
                own.link(dve.scalar_tensor_tensor(out=nb[:, t, :], in0=den[:, t, :], scalar=SCALE,
                                                  in1=sink, op0=ALU.mult, op1=ALU.min))
                dve.tensor_tensor(sd[:, t, :], nb[:, t, :], sink, ALU.subtract).then_inc(nb_done, 1)

            def divide_a(u, t):
                lo = 0 if t else P
                dve.wait_ge(exp_done, NT * u + t + 1)
                own.link(dve.tensor_tensor(den[:, t, :], rowsum[:, t, :], es[:, t, :], ALU.add))
                own.link(dve.reciprocal(rden[:, t, :], den[:, t, :]))
                p = prob[:, t % 2, :].rearrange("p (h k) -> p h k", h=4)[:, :, lo:]
                r = rden[:, t, :].unsqueeze(2).broadcast_to((P, 4, 256 - lo))
                dve.tensor_tensor(p, p, r, ALU.mult).then_inc(p_done, 1)

            def maxima_b(u, t):
                n = (t + 1) * P
                dve.wait_ge(s_done, u * NT + (NT * UNIT0["B"] + t + 1))
                own.link(dve.tensor_reduce(den[:, t, 0:2], ps[:, s_bank(t):s_bank(t) + 2, 0:n], AX.X,
                                           ALU.max, negate=True))
                dve.tensor_scalar(nb[:, t, 0:2], den[:, t, 0:2], SCALE, None, ALU.mult)\
                   .then_inc(nb_done, 1)

            def combine_b(u, t):
                n = (t + 1) * P
                dve.wait_ge(exp_done, u * NT + (NT * UNIT0["B"] + t + 1))
                own.link(dve.reciprocal(rden[:, t, 0:2], rowsum[:, t, 0:2]))
                own.link(dve.tensor_scalar(rden[:, t, 2:3], rden[:, t, 1:2], neglam[:, :], None, ALU.mult))
                p0, p1 = prob[:, t % 2, 0:n], prob[:, t % 2, T:T + n]
                own.link(dve.tensor_scalar(p1, p1, rden[:, t, 2:3], None, ALU.mult))
                dve.scalar_tensor_tensor(out=p0, in0=p0, scalar=rden[:, t, 0:1], in1=p1, op0=ALU.mult,
                                         op1=ALU.add).then_inc(p_done, 1)

            dve.wait_ge(pos_landed, 16)
            dve.tensor_copy(pos_f[:, :], pos_i[:, :]).then_inc(pos_done, 1)
            dve.wait_ge(posT_tr, 1)
            dve.tensor_copy(posT[:, :], ps[:, 7, 0:NT]).then_inc(posT_done, 1)

            dve.wait_ge(posT_done, 1)
            dve.wait_ge(const_done, 1 + HALF)
            own.link(dve.tensor_tensor(ang[:, :, :], posT[:, :].unsqueeze(2).broadcast_to((P, NT, HALF)),
                                       invf[:, :].unsqueeze(1).broadcast_to((P, NT, HALF)), ALU.mult))
            own.link(dve.tensor_scalar(turns[:, :, :], ang[:, :, :], 1.0 / (2 * math.pi), ROUND,
                                       ALU.mult, ALU.add))
            own.link(dve.tensor_scalar(turns[:, :, :], turns[:, :, :], ROUND, None, ALU.subtract))
            for part in TWO_PI_PARTS:
                own.link(dve.scalar_tensor_tensor(out=ang[:, :, :], in0=turns[:, :, :], scalar=-part,
                                                  in1=ang[:, :, :], op0=ALU.mult, op1=ALU.add))
            own.link(dve.tensor_scalar(ang[:, :, :], ang[:, :, :], PI_BELOW, -PI_BELOW, ALU.min, ALU.max))
            own.link(dve.tensor_scalar(angneg[:, :, :], ang[:, :, :], -1.0, None, ALU.mult))
            own.link(dve.tensor_tensor(angneg[:, :, :], ang[:, :, :], angneg[:, :, :], ALU.max))
            dve.tensor_scalar(angcos[:, :, :], angneg[:, :, :], -1.0, math.pi / 2, ALU.mult, ALU.add)\
               .then_inc(ang_done, 1)
            dve.wait_ge(ident_done, 1)
            for t in range(NT):
                dve.wait_ge(x_sq, t + 1)
                dve.tensor_scalar(ssacc[:, t * P:(t + 1) * P], ident[:, :], x_ss[:, t:t + 1], None, ALU.mult)\
                   .then_inc(x_diag, 1)
            for kc in range(KC):
                dve.wait_ge(x_tr, kc + 1)
                dve.tensor_copy(xT[:, kc, :], ps[:, kc, :]).then_inc(x_ready, 1)
            dve.wait_ge(vecT_tr, 1)
            own.mark(dve.tensor_copy(vecT[:, 0, 0:R_FINAL], ps[:, 0, 0:R_FINAL]))
            own.link(dve.tensor_copy(vecT[:, 1, :], ps[:, 0, P:P + R_ALL]))
            low_h(NORM["A"], 0, R_ATTN)

            dve.wait_ge(lam_landed, 64)
            for i in range(2):
                ins = dve.tensor_tensor_reduce(lam[:, 2 * i, :], lam[:, 2 * i, :], lam[:, 2 * i + 1, :], 1.0,
                                               0.0, ALU.mult, ALU.add, lam_s[:, i:i + 1])
                if i == 0:
                    own.mark(ins)
            ins.then_inc(lam_sum, 1)
            dve.wait_ge(lam_exp, 1)
            own.link(dve.tensor_tensor(neglam[:, :], lam_s[:, 3:4], lam_s[:, 2:3], ALU.subtract))
            own.link(dve.tensor_scalar(neglam[:, :], neglam[:, :], LAMBDA_INIT, None, ALU.subtract))
            own.link(dve.tensor_scalar(gainB[:, :], vecT[:, 1, R_SUBLN:R_SUBLN + 1], 1.0 - LAMBDA_INIT,
                                       None, ALU.mult))
            dve.wait_ge(sink_landed, 16)
            own.link(dve.tensor_scalar(nsink[:, :].rearrange("p (u e c) -> p u e c", u=UA, e=2),
                                       sink_in[:, :].rearrange("p (u c e) -> p u e c", u=UA, e=2),
                                       -1.0, None, ALU.mult))
            dve.wait_ge(trig_done, 1)

            def first_scores(kind, maxima, divide):
                for t in range(NT):
                    low_v(kind, 0, 0, t)
                rope(kind, 0)
                for c in range(QFILLS[kind]):
                    low_qk(kind, 0, c)
                maxima(0, 0)
                maxima(0, 1)
                divide(0, 0)
                low_v(kind, 1, 1, 0)

            def low_out_a(u, t):
                dve.wait_ge(ohi_done, NT * u + t + 1)
                for e in range(2):
                    dst, src = outputs_a(ot_lo, u, t, e)
                    ins = dve.tensor_tensor(dst, src, outputs_a(ot_hi, u, t, e)[0].bitcast(F32),
                                            ALU.subtract)
                    if e == 0:
                        own.mark(ins)
                ins.then_inc(olo_done, 1)

            first_scores("A", maxima_a, divide_a)
            for u in range(UA):
                more, more2 = u + 1 < UA, u + 2 < UA
                low_p("A", u, 0)
                divide_a(u, 1)
                if more:
                    low_v("A", u + 1, (u + 1) % 2, 1)
                low_out_a(u, 0)
                maxima_a(u, 2)
                low_p("A", u, 1)
                if more:
                    low_v("A", u + 1, (u + 1) % 2, 2)
                divide_a(u, 2)
                if more:
                    low_v("A", u + 1, (u + 1) % 2, 3)
                    rope("A", u + 1)
                low_out_a(u, 1)
                maxima_a(u, 3)
                if more:
                    low_qk("A", u + 1, 0)
                low_p("A", u, 2)
                if more:
                    low_qk("A", u + 1, 1)
                divide_a(u, 3)
                low_out_a(u, 2)
                if more:
                    low_qk("A", u + 1, 2)
                    maxima_a(u + 1, 0)
                low_p("A", u, 3)
                if more2:
                    low_v("A", u + 2, u % 2, 0)
                if more:
                    divide_a(u + 1, 0)
                low_out_a(u, 3)
                if more:
                    maxima_a(u + 1, 1)

            def add_to_stream(norm, dc, done, n, bank):
                if dc < KC:
                    dve.wait_ge(done, n + dc + 1)
                    dve.tensor_tensor(xT[:, dc, :], xT[:, dc, :], ps[:, bank, :], ALU.add)\
                       .then_inc(x_ready, 1)
                if dc >= 1:
                    add_squares(norm, dc - 1)

            def after_out(l):
                norm = NORM["F0"] if l == 0 else NORM["F1"]
                for dc in range(KC + 1):
                    add_to_stream(norm, dc, oproj_done, KC * l, dc % 4)
                low_h(norm, l, R_FFN)

            def low_u(l, s, f):
                dve.wait_ge(uhi_done, f + (FB * l + 1))
                dve.tensor_tensor(u_lo[:, s, :], u_all[:, bass.ds(f, 1), :].rearrange("p a b -> p (a b)"),
                                  u_hi[:, s, :].bitcast(F32), ALU.subtract).then_inc(ulo_done, 1)

            def gate(l, s, f):
                def w(row):
                    return vecT[:, l, bass.ds(f + row, 1)]
                a, g, c = ps[:, 2 * s, :], ps[:, 2 * s + 1, :], conv[:, s, :]
                dve.wait_ge(up_done, f + (FB * l + 1))
                own.link(dve.tensor_scalar(c, a, w(R_CONVW + 2 * FB), w(R_CONVB), ALU.mult, ALU.add))
                own.link(dve.scalar_tensor_tensor(out=c[:, 1:], in0=a[:, 0:T - 1], scalar=w(R_CONVW + FB),
                                                  in1=c[:, 1:], op0=ALU.mult, op1=ALU.add))
                dve.scalar_tensor_tensor(out=c[:, 2:], in0=a[:, 0:T - 2], scalar=w(R_CONVW),
                                         in1=c[:, 2:], op0=ALU.mult, op1=ALU.add).then_inc(conv_done, 1)
                dve.wait_ge(silu_done, f + (FB * l + 1))
                dve.tensor_tensor(u_all[:, bass.ds(f, 1), :].rearrange("p a b -> p (a b)"), gated[:, s, :],
                                  g, ALU.mult).then_inc(u_done, 1)

            def feed_forward(l):
                with dve.Fori(0, FB // 2 - 1) as r:
                    own.enter(r, 4)
                    for s in range(2):
                        gate(l, s, r * 2 + s)
                own.leave(FB // 2 - 1)
                for s in range(2):
                    gate(l, s, FB - 2 + s)
                    low_u(l, s, s)
                with dve.Fori(0, FB // 2 - 1) as r:
                    for s in range(2):
                        low_u(l, s, r * 2 + (s + 2))
                norm = NORM["B"] if l == 0 else NORM["end"]
                for dc in range(KC + 1):
                    add_to_stream(norm, dc, down_done, KC * l, (4 + dc) % 8)

            after_out(0)
            feed_forward(0)
            low_h(NORM["B"], 1, R_ATTN)

            def unit_b(u, s, more=True, more2=True):
                low_p("B", u, 0)
                combine_b(u, 1)
                if more:
                    low_v("B", u + 1, 1 - s, 1)
                maxima_b(u, 2)
                low_p("B", u, 1)
                if more:
                    low_v("B", u + 1, 1 - s, 2)
                combine_b(u, 2)
                if more:
                    low_v("B", u + 1, 1 - s, 3)
                    rope("B", u + 1)
                maxima_b(u, 3)
                if more:
                    low_qk("B", u + 1, 0)
                low_p("B", u, 2)
                if more:
                    low_qk("B", u + 1, 1)
                combine_b(u, 3)
                if more:
                    maxima_b(u + 1, 0)
                low_p("B", u, 3)
                if more:
                    combine_b(u + 1, 0)
                    maxima_b(u + 1, 1)
                if more2:
                    low_v("B", u + 2, s, 0)
                dve.wait_ge(orstd_done, u + 1)
                dve.scalar_tensor_tensor(out=htmp[:, 0, :], in0=ps[:, OBK, :], scalar=gainB[:, :],
                                         in1=rstd[:, :], op0=ALU.mult, op1=ALU.mult).then_inc(otmp_done, 1)
                dve.wait_ge(ohi_done, u + (NT * UA + 1))
                dve.tensor_tensor(ot_lo[:, bass.ds(u, 1), :].rearrange("p a b -> p (a b)"), htmp[:, 0, :],
                                  ot_hi[:, bass.ds(u, 1), :].rearrange("p a b -> p (a b)").bitcast(F32),
                                  ALU.subtract).then_inc(olo_done, 1)

            first_scores("B", maxima_b, combine_b)
            with dve.Fori(0, UB // 2 - 1) as r:
                own.enter(r, PER_UNIT_B * 2)
                for s in range(2):
                    unit_b(r * 2 + s, s)
            own.leave(UB // 2 - 1)
            unit_b(UB - 2, 0, more2=False)
            unit_b(UB - 1, 1, more=False, more2=False)
            after_out(1)
            feed_forward(1)
            dve.wait_ge(rstd_done, NORM["end"] + 1)
            for kc in range(KC):
                if kc >= 2:
                    dve.wait_ge(y_tr, kc - 1)
                normed(NORM["end"], kc, vecT[:, 1, R_FINAL + kc:R_FINAL + kc + 1], y_done)


def inv_freq(i):
    import numpy as np
    return float(np.power(np.float32(THETA), np.float32(-2.0 * i / ROT), dtype=np.float32))


_INS = ["x", "positions", "attn_norm", "ffn_norm", "ffn_w_up", "ffn_conv_w", "ffn_conv_b", "ffn_w_down",
        "a_w_in", "a_sinks", "a_w_out", "b_w_in", "b_lam_q1", "b_lam_k1", "b_lam_q2", "b_lam_k2",
        "b_subln", "b_w_out", "final_norm"]


def kernel(**inputs):
    import numpy as _np
    import concourse.bacc as _bacc
    from concourse import mybir as _mybir
    from concourse.bass_utils import run_bass_kernel_spmd as _run

    nc = _bacc.Bacc("TRN2", target_bir_lowering=False, num_devices=1)
    arrays, args = {}, []
    for name in _INS:
        a = _np.ascontiguousarray(inputs[name])
        arrays[f"in_{name}"] = a
        args.append(nc.dram_tensor(f"in_{name}", a.shape, _mybir.dt.from_np(a.dtype),
                                   kind="ExternalInput").ap())
    args.append(nc.dram_tensor("out_0", (1, T, D), _mybir.dt.float32, kind="ExternalOutput").ap())
    trunk(nc, *args)
    r = _run(nc, [arrays], core_ids=[0])
    return r.results[0]["out_0"]
```

```python
from contextlib import ExitStack
from itertools import chain
import math

import concourse.bass as bass
from concourse import mybir

P = 128
T = 512
NT = T // P
D = 1024
KC = D // P
HD = 64
UW = 384
F = 2816
FB = F // P
CONVW = 3
EPS = 1e-6
NEG = -1e30
SCALE = HD ** -0.5
THETA, ROT = 500000.0, HD // 4
HALF = ROT // 2
LAMBDA_INIT = 0.8 - 0.6 * math.exp(-0.3 * 1)
TWO_PI_PARTS = (6.28125, 0.0019350051879882812, 3.019916050561733e-07)
ROUND = 12582912.0
PI_BELOW = 3.1415925

UA, UB = 4, 8
OB, ODC = 4, 2

PHASES = {}
_first = _landed = _parts = 0
for _name, _n, _cols, _dmas, _cut in (
        ("attnA", UA, KC * UW, 3, 4), ("outA", OB, KC * ODC * P, 1, 4),
        ("up0", FB, KC * 2 * P, 2, 1), ("down0", FB, D, 1, 2),
        ("attnB", UB, KC * UW, 3, 4), ("outB", OB, KC * ODC * P, 1, 4),
        ("up1", FB, KC * 2 * P, 2, 1), ("down1", FB, D, 1, 2)):
    PHASES[_name] = (_first, _n, _cols, _dmas, _landed, _cut, _parts)
    _first += _n
    _landed += 16 * _dmas * (_n // 2)
    _parts += _cut * _n
ORDER = list(PHASES)
PER_UNIT_B = 3 + 4 * 4

R_CONVW, R_CONVB, R_ATTN, R_FFN, R_FINAL, R_SUBLN, R_ALL = 0, 66, 88, 96, 104, 112, 113

CONSTS = 1 + HALF + 4 + 10

ALU = mybir.AluOpType
ACT = mybir.ActivationFunctionType
AX = mybir.AxisListType
F32 = mybir.dt.float32
F32R = mybir.dt.float32r
BF16 = mybir.dt.bfloat16
I32 = mybir.dt.int32


class Chain:

    def __init__(self, eng, sem):
        self.eng, self.sem, self.base, self.k = eng, sem, 0, 0

    def link(self, ins):
        ins.then_inc(self.sem, 1)
        self.k += 1
        self.eng.wait_ge(self.sem, self.base + self.k)

    def mark(self, ins):
        ins.then_inc(self.sem, 1)
        self.k += 1

    def enter(self, r, per, at=0):
        self.start, self.per = self.base + self.k - per * at, per
        self.base, self.k = r * per + self.start, 0

    def leave(self, turns):
        assert self.k == self.per, (self.k, self.per)
        self.base, self.k = self.start + self.per * turns, 0


def trunk(nc, x, positions, attn_norm, ffn_norm, ffn_w_up, ffn_conv_w, ffn_conv_b, ffn_w_down,
          a_w_in, a_sinks, a_w_out, b_w_in, b_lam_q1, b_lam_k1, b_lam_q2, b_lam_k2, b_subln,
          b_w_out, final_norm, out):
    ctx = ExitStack()
    with ctx:
        def sb(name, shape, dt=F32, stack=ctx):
            return stack.enter_context(nc.sbuf_tensor(name, shape, dt))

        def sem(name):
            return ctx.enter_context(nc.semaphore(name))

        xT = sb("xT", [P, KC, T])
        h_hi = sb("h_hi", [P, KC, T], F32R)
        h_lo = sb("h_lo", [P, KC, T], F32R)
        raw = sb("raw", [P, 2, KC * UW])
        w_hi = sb("w_hi", [P, 2, KC * UW], F32R)
        w_lo = sb("w_lo", [P, 2, KC * UW], F32R)
        htmp = sb("htmp", [P, 2, T])
        sq = sb("sq", [P, 2, T])
        rstd = sb("rstd", [P, T])
        rstd_tok = sb("rstd_tok", [P, NT])
        ident = sb("ident", [P, P])
        ones_d = sb("ones_d", [P, P])
        eps = sb("eps", [P, 1])
        mask_q = sb("mask_q", [P, P], BF16)
        mask_k = sb("mask_k", [P, 2 * P], BF16)
        vecT = sb("vecT", [P, 2, R_ALL])
        nsink = sb("nsink", [P, UA * 4])
        lam_s = sb("lam_s", [P, 4])
        neglam = sb("neglam", [P, 1])
        gainB = sb("gainB", [P, 1])
        cos16 = sb("cos16", [P, NT, ROT])
        sin16 = sb("sin16", [P, NT, ROT])
        ropeA = htmp[:, 1, 0:NT * 6 * ROT].rearrange("p (t h d) -> p t h d", t=NT, h=6)
        ropeB = sq[:, 1, 0:NT * 6 * ROT].rearrange("p (t h d) -> p t h d", t=NT, h=6)
        nb = sb("nb", [P, NT, 4])
        sd = sb("sd", [P, NT, 4])
        es = sb("es", [P, NT, 4])
        rowsum = sb("rowsum", [P, NT, 4])
        den = sb("den", [P, NT, 4])
        rden = sb("rden", [P, NT, 4])

        with ExitStack() as st:
            ot_hi = sb("ot_hi", [P, KC, T], F32R, st)
            ot_lo = sb("ot_lo", [P, KC, T], F32R, st)
            qk = sb("qk", [P, NT, UW], F32, st)
            qt_hi = sb("qt_hi", [P, 3, T], F32R, st)
            qt_lo = sb("qt_lo", [P, 3, T], F32R, st)
            v_hi = sb("v_hi", [P, 2, NT, P], F32R, st)
            v_lo = sb("v_lo", [P, 2, NT, P], F32R, st)
            prob = sb("prob", [P, 2, 1024], F32, st)
            pt_hi = sb("pt_hi", [P, 2, T], F32R, st)
            pt_lo = sb("pt_lo", [P, 2, T], F32R, st)
        with ExitStack() as st:
            u_all = sb("u_all", [P, FB, T], F32, st)
            u_hi = sb("u_hi", [P, 2, T], F32R, st)
            u_lo = sb("u_lo", [P, 2, T], F32R, st)
            conv = sb("conv", [P, 2, T], F32, st)
            gated = sb("gated", [P, 2, T], F32, st)
            normed = sb("normed", [P, 2, T], F32, st)
            ssacc = sb("ssacc", [P, T], F32, st)
        with ExitStack() as st:
            x_tok = sb("x_tok", [P, NT, D], F32, st)
            grow = sb("grow", [KC, P], F32, st)
            vrow = sb("vrow", [P, 2, P], F32, st)
            pos_i = sb("pos_i", [NT, P], I32, st)
            pos_f = sb("pos_f", [NT, P], F32, st)
            posT = sb("posT", [P, NT], F32, st)
            x_ss = sb("x_ss", [P, NT], F32, st)
            invf = sb("invf", [P, HALF], F32, st)
            ang = sb("ang", [P, NT, HALF], F32, st)
            turns = sb("turns", [P, NT, HALF], F32, st)
            angneg = sb("angneg", [P, NT, HALF], F32, st)
            lam = sb("lam", [P, 4, HD], F32, st)
            sink_in = sb("sink_in", [P, UA * 4], F32, st)
            angcos = sb("angcos", [P, NT, HALF], F32, st)
            y_feat = sb("y_feat", [P, KC, T], F32, st)

        ps = ctx.enter_context(nc.psum_tensor("ps", [P, 8, T], F32))
        PJ, TB, OBK = (0, 1), 6, 7

        OUT_BANKS = ((0, 1, TB, 3), (0, 1, 2, 3))
        OUT_AHEAD = (6, 7)

        def s_bank(t):
            return 2 + 2 * (t % 2)

        x_landed = [sem(f"x_landed{t}") for t in range(NT)]
        vec_landed = sem("vec_landed")
        sink_landed = sem("sink_landed")
        lam_landed = sem("lam_landed")
        pos_landed = sem("pos_landed")
        raw_landed = [sem("raw_landed0"), sem("raw_landed1")]
        hi_done = sem("hi_done")
        lo_done = sem("lo_done")
        const_done = sem("const_done")
        ident_done = sem("ident_done")
        pos_done = sem("pos_done")
        posT_tr = sem("posT_tr")
        posT_done = sem("posT_done")
        ang_done = sem("ang_done")
        trig_done = sem("trig_done")
        vecT_tr = sem("vecT_tr")
        vecT_done = sem("vecT_done")
        lam_sum = sem("lam_sum")
        lam_exp = sem("lam_exp")
        x_tr = sem("x_tr")
        x_sq = sem("x_sq")
        x_ready = sem("x_ready")
        sq_done = sem("sq_done")
        ss_done = sem("ss_done")
        ms_done = sem("ms_done")
        ln_done = sem("ln_done")
        rstd_done = sem("rstd_done")
        hhi_done = sem("hhi_done")
        hlo_done = sem("hlo_done")
        proj_done = sem("proj_done")
        proj_out = sem("proj_out")
        rope_done = sem("rope_done")
        vlo_done = sem("vlo_done")
        tr_done = sem("tr_done")
        thi_done = sem("thi_done")
        tlo_done = sem("tlo_done")
        ptr_done = sem("ptr_done")
        phi_done = sem("phi_done")
        plo_done = sem("plo_done")
        s_done = sem("s_done")
        nb_done = sem("nb_done")
        exp_done = sem("exp_done")
        p_done = sem("p_done")
        pv_done = sem("pv_done")
        ohi_done = sem("ohi_done")
        olo_done = sem("olo_done")
        osq_done = sem("osq_done")
        oms_done = sem("oms_done")
        oln_done = sem("oln_done")
        orstd_done = sem("orstd_done")
        otmp_done = sem("otmp_done")
        oproj_done = sem("oproj_done")
        up_done = sem("up_done")
        conv_done = sem("conv_done")
        silu_done = sem("silu_done")
        u_done = sem("u_done")
        uhi_done = sem("uhi_done")
        ulo_done = sem("ulo_done")
        down_used = sem("down_used")
        down_done = sem("down_done")
        y_done = sem("y_done")
        y_tr = sem("y_tr")
        y_act = sem("y_act")
        y_dve = sem("y_dve")
        gain_landed = sem("gain_landed")
        half_landed = sem("half_landed")
        stored = sem("stored")
        dve_self = sem("dve_self")

        def qk_bank(u, c):
            return (TB, 2, 3)[c] if isinstance(u, int) and u == 0 else TB

        def pj(u, t):
            return t if isinstance(u, int) and u == 0 else PJ[t % 2]

        def values(kind, dst, s, t, bank):
            src = ps[:, bank, 2 * P:UW]
            if kind == "B":
                return dst[:, s, t, :], src
            return (dst[:, s, t, :].rearrange("p (c d) -> p c d", c=2),
                    src[:, HD:].unsqueeze(1).broadcast_to((P, 2, HD)))

        def probs(kind, dst, t):
            if kind == "B":
                n = (t + 1) * P
                return dst[:, t % 2, 0:n], ps[:, s_bank(t), 0:n]
            if t == 0:
                return dst[:, 1, :], ps[:, s_bank(t) + 1, :]
            return dst[:, :, :], ps[:, s_bank(t):s_bank(t) + 2, :]

        def outputs_a(dst, u, t, e):
            rows = slice(e * HD, (e + 1) * HD)
            src = ps[:, OBK, :].rearrange("p (c e q) -> p c e q", c=2, e=2)
            return dst[rows, 2 * u:2 * u + 2, t * P:(t + 1) * P], src[rows, :, e, :]

        block = ctx.enter_context(nc.Block())

        def first(ph):
            return PHASES[ph][0]

        def n_blocks(ph):
            return PHASES[ph][1]

        def landed(ph, s, turn):
            return PHASES[ph][4] + 16 * PHASES[ph][3] * (turn + 1)

        def cols(ph):
            return PHASES[ph][2]

        def parts(ph):
            return PHASES[ph][5]

        def part_done(ph, i, c=None):
            n = parts(ph)
            return i * n + (PHASES[ph][6] + (n if c is None else c + 1))

        UNIT0 = {"A": 0, "B": UA}
        QFILLS = {"A": 3, "B": 2}
        FILL0 = {"A": 0, "B": UA * 3}
        NORM = {"A": 0, "F0": 1, "B": 2, "F1": 3, "end": 4}
        PHASE = {"A": "attnA", "B": "attnB"}

        def fill_no(kind, u, c):
            return u * QFILLS[kind] + (FILL0[kind] + c + 1)

        def tile_no(kind, u, t):
            return u * NT + (NT * UNIT0[kind] + t + 1)

        def layer(ph):
            return 0 if first(ph) < first("attnB") else 1

        def wait_used(eng, ph, i):
            l = layer(ph)
            if ph[:4] == "attn":
                eng.wait_ge(proj_done, i * NT + (NT * (UNIT0[ph[4]] + 1)))
            elif ph[:3] == "out":
                eng.wait_ge(oproj_done, i * ODC + (KC * l + ODC))
            elif ph[:2] == "up":
                eng.wait_ge(up_done, i + (FB * l + 1))
            elif isinstance(i, int) and i == FB - 1:
                eng.wait_ge(down_done, KC * (l + 1))
            else:
                eng.wait_ge(down_used, i + ((FB - 1) * l + 1))

        @block.sync
        def _(sp):
            xv = x.rearrange("b (t p) d -> p (b t) d", p=P)
            sp.dma_start(pos_i[:, :], positions.rearrange("b (t p) -> (b t) p", p=P))\
              .then_inc(pos_landed, 16)
            sp.dma_start(grow[:, :], attn_norm[0].rearrange("(k p) -> k p", p=P))\
              .then_inc(gain_landed, 16)
            for t in range(NT):
                sp.dma_start(x_tok[:, t, :], xv[:, t, :]).then_inc(x_landed[t], 16)

            def load_attn(ph, s, i, chunks, signal):
                w, qw, kvw = (a_w_in, 256, 64) if ph == "attnA" else (b_w_in, P, P)
                wv = w[0].rearrange("(k p) n -> p k n", p=P)
                rv = raw[:, s, :].rearrange("p (k n) -> p k n", k=KC)
                sp.dma_start(rv[:, chunks, 0:qw], wv[:, chunks, bass.ds(i * qw, qw)]).then_inc(signal, 16)
                for side in range(2):
                    at = qw + side * kvw
                    sp.dma_start(rv[:, chunks, at:at + kvw],
                                 wv[:, chunks, bass.ds(i * kvw + (D if side == 0 else v_at(ph)), kvw)])\
                      .then_inc(signal, 16)

            def load(ph, s, turn, wait):
                i = 2 * turn + s
                if wait == "own":
                    sp.wait_ge(lo_done, part_done(ph, i - 2))
                elif wait == "before":
                    q = ORDER[ORDER.index(ph) - 1]
                    sp.wait_ge(lo_done, part_done(q, n_blocks(q) - 2 + s))
                if ph[:4] == "attn":
                    load_attn(ph, s, i, slice(0, KC), raw_landed[s])
                elif ph[:3] == "out":
                    w = a_w_out if ph == "outA" else b_w_out
                    wv = w[0].rearrange("(k p) n -> p k n", p=P)
                    rv = raw[:, s, 0:cols(ph)].rearrange("p (k n) -> p k n", k=KC)
                    sp.dma_start(rv, wv[:, :, bass.ds(i * ODC * P, ODC * P)])\
                      .then_inc(raw_landed[s], 16)
                elif ph[:2] == "up":
                    wv = ffn_w_up[int(ph[2])].rearrange("(k p) n -> p k n", p=P)
                    rv = raw[:, s, 0:cols(ph)].rearrange("p (k g n) -> p k g n", k=KC, g=2)
                    for g in range(2):
                        sp.dma_start(rv[:, :, g, :], wv[:, :, bass.ds(i * P + g * F, P)])\
                          .then_inc(raw_landed[s], 16)
                else:
                    wv = ffn_w_down[int(ph[4])].rearrange("(f p) n -> p f n", p=P)
                    sp.dma_start(raw[:, s, 0:D], wv[:, bass.ds(i, 1), :])\
                      .then_inc(raw_landed[s], 16)

            def v_at(ph):
                return D + 256 if ph == "attnA" else 2 * D

            def vectors(l):
                n = CONVW * FB
                sp.dma_start(vrow[R_CONVW:R_CONVW + n, l, :],
                             ffn_conv_w[l].rearrange("c (f p) -> (c f) p", p=P)).then_inc(vec_landed, 16)
                sp.dma_start(vrow[R_CONVB:R_CONVB + FB, l, :],
                             ffn_conv_b[l].rearrange("(f p) -> f p", p=P)).then_inc(vec_landed, 16)
                sp.dma_start(vrow[R_ATTN:R_ATTN + KC, l, :],
                             attn_norm[l].rearrange("(f p) -> f p", p=P)).then_inc(vec_landed, 16)
                sp.dma_start(vrow[R_FFN:R_FFN + KC, l, :],
                             ffn_norm[l].rearrange("(f p) -> f p", p=P)).then_inc(vec_landed, 16)

            load_attn("attnA", 0, 0, slice(0, KC // 2), half_landed)
            load_attn("attnA", 0, 0, slice(KC // 2, KC), raw_landed[0])
            load("attnA", 1, 0, None)
            vectors(0)
            vectors(1)
            sp.dma_start(vrow[R_FINAL:R_FINAL + KC, 1, :],
                         final_norm.rearrange("(f p) -> f p", p=P)).then_inc(vec_landed, 16)
            sp.dma_start(vrow[R_SUBLN:R_SUBLN + 1, 1, :], b_subln).then_inc(vec_landed, 16)
            sp.dma_start(sink_in[:, :], a_sinks.partition_broadcast(P)).then_inc(sink_landed, 16)
            for i, v in enumerate((b_lam_q1, b_lam_k1, b_lam_q2, b_lam_k2)):
                sp.dma_start(lam[:, i, :], v.partition_broadcast(P)).then_inc(lam_landed, 16)

            for ph in ORDER:
                for s in range(2):
                    if ph != ORDER[0]:
                        load(ph, s, 0, "before")
                if n_blocks(ph) == 4:
                    for s in range(2):
                        load(ph, s, 1, "own")
                else:
                    with sp.Fori(1, n_blocks(ph) // 2) as r:
                        for s in range(2):
                            load(ph, s, r, "own")

            ov = out.rearrange("b (t p) d -> p (b t) d", p=P)
            half = D // 2
            for b in range(2 * NT):
                sp.wait_ge(y_dve if b % 2 else y_act, b // 2 + 1)
                at = slice(b // NT * half, (b // NT + 1) * half)
                sp.dma_start(ov[:, b % NT, at], x_tok[:, b % NT, at]).then_inc(stored, 16)
            sp.wait_ge(stored, 16 * 2 * NT)

        @block.gpsimd
        def _(pool):
            pool.memset(ident[:, :], 0.0).then_inc(const_done, 1)
            pool.wait_ge(const_done, 1)
            pool.affine_select(out=ident[:, :], in_=ident[:, :], compare_op=ALU.not_equal, fill=1.0,
                               base=0, pattern=[[-1, P]], channel_multiplier=1).then_inc(ident_done, 1)
            for i in range(HALF):
                pool.memset(invf[:, i:i + 1], inv_freq(i)).then_inc(const_done, 1)
            pool.memset(ones_d[:, :], 1.0 / D).then_inc(const_done, 1)
            pool.memset(eps[:, :], EPS).then_inc(const_done, 1)
            pool.memset(mask_q[:, :], 0.0).then_inc(const_done, 1)
            pool.memset(mask_k[:, :], 0.0).then_inc(const_done, 1)
            pool.wait_ge(const_done, 1 + HALF + 4)
            for row in (0, HD):
                pool.memset(mask_q[row:row + 1, 0:HD], 1.0).then_inc(const_done, 1)
                pool.memset(mask_q[row + 32:row + 33, HD:P], 1.0).then_inc(const_done, 1)
                pool.memset(mask_k[row:row + 1, 0:HD], NEG).then_inc(const_done, 1)
                pool.memset(mask_k[row:row + 1, 3 * HD:4 * HD], NEG).then_inc(const_done, 1)
                pool.memset(mask_k[row + 32:row + 33, 0:2 * HD], NEG).then_inc(const_done, 1)
            pool.wait_ge(const_done, CONSTS)

            def low(ph, s, i):
                n = cols(ph) // parts(ph)
                for c in range(parts(ph)):
                    at = slice(c * n, (c + 1) * n)
                    pool.wait_ge(hi_done, part_done(ph, i, c))
                    pool.tensor_tensor(w_lo[:, s, at], raw[:, s, at], w_hi[:, s, at].bitcast(F32),
                                       ALU.subtract).then_inc(lo_done, 1)

            for ph in ORDER:
                with pool.Fori(0, n_blocks(ph) // 2) as r:
                    for s in range(2):
                        low(ph, s, r * 2 + s)

        @block.tensor
        def _(pe):
            def hi_lo(out_, a_hi, a_lo, b_hi, b_lo, start, stop):
                pe.matmul(out_, a_lo, b_hi, start=start, stop=False)
                pe.matmul(out_, a_hi, b_lo, start=False, stop=False)
                return pe.matmul(out_, a_hi, b_hi, start=False, stop=stop)

            pe.wait_ge(ident_done, 1)
            pe.wait_ge(pos_done, 1)
            pe.transpose(ps[:, 7, 0:NT], pos_f[:, :], ident[0:NT, 0:NT]).then_inc(posT_tr, 1)
            pe.wait_ge(gain_landed, 16)
            pe.transpose(ps[:, 6, 0:KC], grow[:, :], ident[0:KC, 0:KC]).then_inc(posT_tr, 1)
            for t in range(NT):
                pe.wait_ge(x_landed[t], 16)
                for kc in range(KC):
                    if t == 0 and kc == 6:
                        pe.wait_ge(posT_done, 2)
                    ins = pe.transpose(ps[:, kc, t * P:(t + 1) * P], x_tok[:, t, kc * P:(kc + 1) * P],
                                       ident[:, :])
                    if t == NT - 1:
                        ins.then_inc(x_tr, 1)
            pe.wait_ge(const_done, CONSTS)

            def little_vectors():
                pe.wait_ge(vec_landed, 16 * 10)
                pe.transpose(ps[:, TB, 0:R_FINAL], vrow[0:R_FINAL, 0, :], ident[0:R_FINAL, 0:R_FINAL])
                pe.transpose(ps[:, TB, P:P + R_ALL], vrow[0:R_ALL, 1, :],
                             ident[0:R_ALL, 0:R_ALL]).then_inc(vecT_tr, 1)

            def mean_square(norm):
                pe.wait_ge(ss_done, KC * norm)
                pe.matmul(ps[:, TB, :], ones_d[:, :], ssacc[:, :], start=True, stop=True)\
                  .then_inc(ms_done, 1)

            def mean_square_tok(norm):
                pe.wait_ge(ss_done, KC * norm)
                for t in range(NT):
                    ins = pe.matmul(ps[:, OBK, t:t + 1], ssacc[:, t * P:(t + 1) * P], ones_d[:, 0:1],
                                    start=True, stop=True)
                ins.then_inc(ms_done, 1)

            def projection(kind, u, s, tiles):
                ph = PHASE[kind]
                wh = w_hi[:, s, :].rearrange("p (k n) -> p k n", k=KC)
                wl = w_lo[:, s, :].rearrange("p (k n) -> p k n", k=KC)
                tile0 = NT * (u + UNIT0[kind])
                coming = tiles[0] == 0
                first_unit = isinstance(u, int) and u == 0
                order = [(t, kc) for t in tiles for kc in range(KC)]
                if coming and first_unit:
                    order.sort(key=lambda x: x[1])
                n = 0
                for t, kc in order:
                    tok = slice(t * P, (t + 1) * P)
                    if kc == 0 and not first_unit:
                        unit1 = isinstance(u, int) and u == 1 and t < 2
                        pe.wait_ge(vlo_done, tile0 + (t - NT + 1 if unit1 else t - 1))
                    if t == 0 and kc % 2 == 0:
                        pe.wait_ge(lo_done, part_done(ph, u, kc // 2))
                    if first_unit and t == 0:
                        pe.wait_ge(hlo_done, KC * NORM[kind] + kc + 1)
                    for m, (a, b) in enumerate(((h_lo, wh), (h_hi, wl), (h_hi, wh))):
                        ins = pe.matmul(ps[:, pj(u, t), 0:UW], a[:, kc, tok], b[:, kc, :],
                                        start=(kc == 0 and m == 0), stop=(kc == KC - 1 and m == 2))
                        n += 1
                        if kc == KC - 1 and m == 2:
                            ins.then_inc(proj_done, 1)
                        if n % 4 == 0:
                            yield

            def run(slabs, k):
                for _ in range(k):
                    next(slabs, None)

            def transposes(bank, blocks, inputs):
                for (c, i) in zip(blocks, inputs):
                    ins = pe.transpose(ps[:, bank, c * P:(c + 1) * P], i, ident[:, :])
                return ins

            def fill_qk(kind, u, c):
                if c == 0:
                    pe.wait_ge(rope_done, u + (UNIT0[kind] + 1))
                    if kind == "B" and not (isinstance(u, int) and u < 2):
                        pe.wait_ge(oln_done, u - 1)
                if not (isinstance(u, int) and u == 0):
                    pe.wait_ge(tlo_done, fill_no(kind, u, c) - 1)
                transposes(qk_bank(u, c), range(NT), [qk[:, t, c * P:(c + 1) * P] for t in range(NT)])\
                    .then_inc(tr_done, 1)

            def start_unit0(kind):
                slabs = chain(projection(kind, 0, 0, (0, 1)), projection(kind, 0, 0, (2, 3)))
                run(slabs, 12 + 8)
                if kind == "B":
                    mean_square_tok(NORM["B"])
                run(slabs, 4)
                slabs = projection(kind, 1, 1, (0, 1))
                if kind == "A":
                    run(slabs, 3)
                    little_vectors()
                    run(slabs, 3)
                    pe.wait_ge(vecT_done, 2)
                else:
                    run(slabs, 6)
                for c in range(QFILLS[kind]):
                    fill_qk(kind, 0, c)
                run(slabs, 3)
                scores = scores_a if kind == "A" else scores_b
                scores(0, 0)
                scores(0, 1)
                run(slabs, 24)

            def scores_a(u, t):
                if t == 0:
                    pe.wait_ge(tlo_done, fill_no("A", u, 2))
                if NT * u + t >= 2:
                    pe.wait_ge(plo_done, tile_no("A", u, t - 2))
                q = slice(t * P, (t + 1) * P)
                lo = 0 if t else P
                keys = slice((t - 1) * P if t else 0, (t + 1) * P)
                for e in range(2):
                    rows = slice(e * HD, (e + 1) * HD)
                    bank = ps[:, s_bank(t) + e, :].rearrange("p (h k) -> p h k", h=2)
                    pe.matmul(bank[:, :, lo:], mask_q[rows, :],
                              mask_k[rows, lo:].unsqueeze(1).broadcast_to((HD, 2, 2 * P - lo)),
                              start=True, stop=False)
                    for c in range(2):
                        for m, (a, b) in enumerate(((qt_lo, qt_hi), (qt_hi, qt_lo), (qt_hi, qt_hi))):
                            ins = pe.matmul(bank[:, c, lo:], a[rows, c, q], b[rows, 2, keys],
                                            start=False, stop=(c == 1 and m == 2))
                ins.then_inc(s_done, 1)

            def probs_a(u, t):
                pe.wait_ge(p_done, tile_no("A", u, t))
                for kt in (0, 1) if t else (1,):
                    ins = transposes(s_bank(t) + kt, (0, 2, 1, 3),
                                     [prob[:, t % 2, h * 256 + kt * P:h * 256 + (kt + 1) * P]
                                      for h in range(4)])
                ins.then_inc(ptr_done, 1)

            def values_a(u, t):
                pe.wait_ge(plo_done, tile_no("A", u, t))
                if NT * u + t:
                    pe.wait_ge(olo_done, NT * u + t)
                if t == 0:
                    pe.wait_ge(vlo_done, NT * (u + 1))
                for kt in (0, 1) if t else (1,):
                    v = t - 1 + kt
                    ins = hi_lo(ps[:, OBK, :], v_hi[:, u % 2, v, :], v_lo[:, u % 2, v, :],
                                pt_hi[:, kt, :], pt_lo[:, kt, :], start=(kt == 0 or t == 0),
                                stop=(kt == 1))
                ins.then_inc(pv_done, 1)

            def unit_a(u):
                more = u + 1 < UA
                if u + 2 < UA:
                    ahead = projection("A", u + 2, u % 2, (0, 1))
                elif more:
                    ahead = out_ahead(0, (0, 1), range(4))
                else:
                    ahead = chain(out_ahead(0, (2,), range(6)), out_ahead(0, (0, 1), range(4, 6)),
                                  out_ahead(0, (3,), range(6)))
                slabs = chain(projection("A", u + 1, (u + 1) % 2, (2, 3)) if more else (), ahead)
                n = (4, 3, 5, 2, 2, 2, 1, 1, 4) if u + 2 < UA else (4, 3, 5, 1, 1, 1, 1, 1, 3) if more \
                    else (3, 0, 3, 0, 3, 0, 1, 0, 4)
                probs_a(u, 0)
                run(slabs, n[0])
                values_a(u, 0)
                scores_a(u, 2)
                run(slabs, n[1])
                probs_a(u, 1)
                run(slabs, n[2])
                values_a(u, 1)
                scores_a(u, 3)
                if more:
                    run(slabs, n[3])
                    fill_qk("A", u + 1, 0)
                probs_a(u, 2)
                run(slabs, n[4])
                if more:
                    fill_qk("A", u + 1, 1)
                    run(slabs, n[5])
                if more:
                    fill_qk("A", u + 1, 2)
                values_a(u, 2)
                run(slabs, n[6])
                if more:
                    run(slabs, n[7])
                    scores_a(u + 1, 0)
                probs_a(u, 3)
                run(slabs, n[8])
                values_a(u, 3)
                if more:
                    scores_a(u + 1, 1)
                run(slabs, 24)

            def scores_b(u, t):
                if t == 0:
                    pe.wait_ge(tlo_done, fill_no("B", u, 1))
                pe.wait_ge(plo_done, tile_no("B", u, t - 2))
                q = slice(t * P, (t + 1) * P)
                n = (t + 1) * P
                for e in range(2):
                    rows = slice(e * HD, (e + 1) * HD)
                    bank = ps[:, s_bank(t) + e, :]
                    for m, (a, b) in enumerate(((qt_lo, qt_hi), (qt_hi, qt_lo), (qt_hi, qt_hi))):
                        pe.matmul(bank[:, 0:n], a[rows, 0, q], b[rows, 1, 0:n], start=(m == 0),
                                  stop=False)
                    ins = pe.matmul(bank[:, n - P:n], mask_q[rows, :], mask_k[rows, P:2 * P],
                                    start=False, stop=True)
                ins.then_inc(s_done, 1)

            def probs_b(u, t):
                pe.wait_ge(p_done, tile_no("B", u, t))
                transposes(s_bank(t), range(t + 1), [prob[:, t % 2, k * P:(k + 1) * P] for k in range(t + 1)])\
                    .then_inc(ptr_done, 1)

            def values_b(u, s, pair):
                t = 2 * pair + 1
                pe.wait_ge(plo_done, tile_no("B", u, t))
                if pair == 0:
                    pe.wait_ge(vlo_done, tile_no("B", u, NT - 1))
                    if not (isinstance(u, int) and u == 0):
                        pe.wait_ge(otmp_done, u)
                both = ps[:, OBK, (t - 1) * P:(t + 1) * P].rearrange("p (a q) -> p a q", a=2)
                passes = [(v, pt, k) for k in range(t) for v, pt in ((v_lo, pt_hi), (v_hi, pt_lo),
                                                                     (v_hi, pt_hi))]
                for i, (v, pt, k) in enumerate(passes):
                    ins = pe.matmul(both, v[:, s, k, :], pt[:, :, k * P:(k + 1) * P], start=(i == 0),
                                    stop=(i == len(passes) - 1))
                    if i == 0:
                        own = slice(t * P, (t + 1) * P)
                        for v, pt in ((v_lo, pt_hi), (v_hi, pt_lo), (v_hi, pt_hi)):
                            pe.matmul(ps[:, OBK, own], v[:, s, t, :], pt[:, 1, own], start=False, stop=False)
                ins.then_inc(pv_done, 2)

            def unit_b(u, s, more=True, more2=True):
                if more2:
                    ahead = projection("B", u + 2, s, (0, 1))
                elif more:
                    ahead = out_ahead(1, (0, 1), range(3))
                else:
                    ahead = chain(out_ahead(1, (0, 1), range(3, 7)), out_ahead(1, (3,), range(7)),
                                  out_ahead(1, (2,), range(7)))
                slabs = chain(projection("B", u + 1, 1 - s, (2, 3)) if more else (), ahead)
                n = (4, 4, 4, 2, 2, 1, 3, 3, 1) if more2 else (4, 4, 4, 1, 1, 1, 2, 1, 0) if more else \
                    (4, 2, 2, 0, 4, 0, 0, 4, 1)
                probs_b(u, 0)
                run(slabs, n[0])
                scores_b(u, 2)
                run(slabs, n[1])
                probs_b(u, 1)
                run(slabs, n[2])
                values_b(u, s, 0)
                scores_b(u, 3)
                if more:
                    run(slabs, n[3])
                    fill_qk("B", u + 1, 0)
                probs_b(u, 2)
                run(slabs, n[4])
                if more:
                    fill_qk("B", u + 1, 1)
                    run(slabs, n[5] + n[6])
                    scores_b(u + 1, 0)
                probs_b(u, 3)
                run(slabs, n[7])
                values_b(u, s, 1)
                if more:
                    scores_b(u + 1, 1)
                run(slabs, n[8])
                pe.wait_ge(osq_done, u + 1)
                pe.matmul(ps[:, TB, :], ones_d[:, :], osq[:, :], start=True, stop=True)\
                  .then_inc(oms_done, 1)
                run(slabs, 24)

            def out_products(l, dc, chunks):
                ph, s = ("outA", "outB")[l], dc // ODC % 2
                wh = w_hi[:, s, 0:cols(ph)].rearrange("p (k n) -> p k n", k=KC)
                wl = w_lo[:, s, 0:cols(ph)].rearrange("p (k n) -> p k n", k=KC)
                c = slice(dc % ODC * P, (dc % ODC + 1) * P)
                for kc in chunks:
                    ins = hi_lo(ps[:, OUT_BANKS[l][dc % 4], :], wh[:, kc, c], wl[:, kc, c],
                                ot_hi[:, kc, :], ot_lo[:, kc, :], start=(kc == 0), stop=(kc == KC - 1))
                if kc == KC - 1:
                    ins.then_inc(oproj_done, 1)

            def out_ahead(l, dcs, chunks):
                ph = ("outA", "outB")[l]
                for kc in chunks:
                    for dc in dcs:
                        pe.wait_ge(lo_done, part_done(ph, dc // ODC, kc * parts(ph) // KC))
                        if kc == 0:
                            last = ("AB"[l], (UA, UB)[l] - 1)
                            if dc < 2:
                                pe.wait_ge(vlo_done, tile_no(*last, NT - 1))
                            elif dc == 2 and l == 1 or dc == 3 and l == 0:
                                pe.wait_ge(plo_done, tile_no(*last, 2))
                            elif dc == 3:
                                pe.wait_ge(exp_done, tile_no(*last, 2))
                        pe.wait_ge(olo_done, NT * (kc // 2 + 1) if l == 0 else NT * UA + kc + 1)
                        out_products(l, dc, (kc,))
                        yield

            def out_projection(l):
                pe.wait_ge(olo_done, NT * UA + UB * l)
                norm = NORM["F0"] if l == 0 else NORM["F1"]
                for dc in range(KC):
                    if dc >= 4:
                        pe.wait_ge(x_ready, KC * norm + dc - 3)
                    ahead = OUT_AHEAD[l] if dc < 4 else 0
                    ph = ("outA", "outB")[l]
                    for c in range(parts(ph)):
                        n = KC // parts(ph)
                        rows = range(max(ahead, c * n), (c + 1) * n)
                        if rows:
                            pe.wait_ge(lo_done, part_done(ph, dc // ODC, c))
                            out_products(l, dc, rows)

            osq = sq[:, 0, :]

            start_unit0("A")
            for u in range(UA):
                unit_a(u)

            def up_pair(l, r, is_first):
                ph, norm = f"up{l}", NORM["F0"] if l == 0 else NORM["F1"]
                for s in range(2):
                    pe.wait_ge(lo_done, part_done(ph, r * 2 + s))
                    if not is_first:
                        pe.wait_ge(u_done, r * 2 + (FB * l + s - 1))
                    wh = w_hi[:, s, 0:cols(ph)].rearrange("p (k g n) -> p k g n", k=KC, g=2)
                    wl = w_lo[:, s, 0:cols(ph)].rearrange("p (k g n) -> p k g n", k=KC, g=2)
                    if is_first:
                        pe.wait_ge(x_ready, KC * norm + (6 if s == 0 else KC))
                    order = [(g, kc) for g in range(2) for kc in range(KC)]
                    if is_first and s == 0:
                        order.sort(key=lambda x: x[1])
                    for g, kc in order:
                        if is_first and s == 0 and g == 0:
                            pe.wait_ge(hlo_done, KC * norm + kc + 1)
                        ins = hi_lo(ps[:, 2 * s + g, :], wh[:, kc, g, :], wl[:, kc, g, :],
                                    h_hi[:, kc, :], h_lo[:, kc, :], start=(kc == 0),
                                    stop=(kc == KC - 1))
                    ins.then_inc(up_done, 1)
                    if is_first and s == 0:
                        mean_square(norm)

            def down_pair(l, r, is_first, is_last):
                ph = f"down{l}"
                order = [(s, dc) for s in range(2) for dc in range(KC)]
                if is_first:
                    order = [(0, dc) for dc in [*range(4, KC), *range(4)]] + order[KC:]
                if is_last:
                    h = KC // 2
                    order = order[:h] + [(1 - k, dc + h * k) for dc in range(h) for k in range(2)] + order[-h:]
                begun = set()
                for s, dc in order:
                    part = dc * parts(ph) // KC
                    if (s, part) not in begun:
                        pe.wait_ge(lo_done, part_done(ph, r * 2 + s, part))
                        if not begun & {(s, 0), (s, 1)}:
                            pe.wait_ge(ulo_done, r * 2 + (FB * l + s + 1))
                        begun.add((s, part))
                    if is_first and s == 0 and dc in (0, 2):
                        pe.wait_ge(u_done, FB * (l + 1) - (1 if dc == 0 else 0))
                    c = slice(dc * P, (dc + 1) * P)
                    ins = hi_lo(ps[:, dc, :], w_hi[:, s, c], w_lo[:, s, c],
                                u_hi[:, s, :], u_lo[:, s, :], start=(is_first and s == 0),
                                stop=(is_last and s == 1))
                    if is_last and s == 1:
                        ins.then_inc(down_done, 1)
                    elif dc == (3 if is_first and s == 0 else KC - 1):
                        ins.then_inc(down_used, 1)

            def feed_forward(l):
                up_pair(l, 0, True)
                with pe.Fori(1, FB // 2) as r:
                    up_pair(l, r, False)
                down_pair(l, 0, True, False)
                with pe.Fori(1, FB // 2 - 1) as r:
                    down_pair(l, r, False, False)
                down_pair(l, FB // 2 - 1, False, True)

            out_projection(0)
            feed_forward(0)

            start_unit0("B")
            unit_b(0, 0)
            unit_b(1, 1)
            with pe.Fori(1, UB // 2 - 1) as r:
                for s in range(2):
                    unit_b(r * 2 + s, s)
            unit_b(UB - 2, 0, more2=False)
            unit_b(UB - 1, 1, more=False, more2=False)
            out_projection(1)
            feed_forward(1)

            def back(dc, tiles):
                for t in tiles:
                    at = slice(dc % 4 * P, (dc % 4 + 1) * P)
                    ins = pe.transpose(ps[:, dc // 4 * NT + t, at],
                                       y_feat[:, dc, t * P:(t + 1) * P], ident[:, :])
                    if dc % 4 == 3:
                        ins.then_inc(y_tr, 1)

            pe.wait_ge(x_ready, KC * NORM["end"] + 4)
            for dc in range(4):
                pe.wait_ge(y_done, dc + 1)
                back(dc, range(NT))
            pe.wait_ge(x_ready, KC * NORM["end"] + 7)
            for dc in range(4, 7):
                pe.wait_ge(y_done, dc + 1)
                back(dc, range(3))
            pe.wait_ge(y_done, KC)
            back(7, range(3))
            mean_square_tok(NORM["end"])
            pe.wait_ge(ln_done, NORM["end"] + 1)
            for dc in range(4, KC):
                back(dc, (3,))

        @block.scalar
        def _(act):
            def high(ph, s, turn, used=None, c=0, wait=None):
                if c >= parts(ph):
                    return
                n = cols(ph) // parts(ph)
                at = slice(c * n, (c + 1) * n)
                if used is not None and c == 0:
                    wait_used(act, *used)
                if c == 0 if wait is None else wait:
                    act.wait_ge(raw_landed[s], landed(ph, s, turn) if isinstance(turn, int)
                                else turn * (16 * PHASES[ph][3]) + landed(ph, s, 0))
                act.activation(w_hi[:, s, at], raw[:, s, at], ACT.Copy).then_inc(hi_done, 1)

            def high_after(ph, b, c=0):
                if b + 2 < n_blocks(ph):
                    high(ph, b % 2, b // 2 + 1, (ph, b), c)
                elif ph != ORDER[-1]:
                    high(ORDER[ORDER.index(ph) + 1], b % 2, 0, (ph, b), c)

            def high_whole(ph, b):
                for c in range(4):
                    high_after(ph, b, c)

            def gained(norm, dc, gain):
                act.wait_ge(x_ready, KC * norm + dc + 1)
                dst, done = (y_feat, y_done) if norm == NORM["end"] else (h_hi, hhi_done)
                act.activation(dst[:, dc, :], xT[:, dc, :], ACT.Copy, scale=gain).then_inc(done, 1)

            def square(norm, dc):
                if KC * (norm - 1) + dc >= 2:
                    act.wait_ge(ss_done, KC * (norm - 1) + dc - 1)
                act.activation(sq[:, dc % 2, :], xT[:, dc, :], ACT.Square).then_inc(sq_done, 1)

            def rsqrt(norm, dst, src, scale=1.0):
                if norm != NORM["A"]:
                    act.wait_ge(ms_done, norm)
                act.activation(dst, src, ACT.Ln, bias=eps[:, :], scale=scale).then_inc(ln_done, 1)
                act.wait_ge(ln_done, norm + 1)
                act.activation(dst, dst, ACT.Exp, scale=-0.5).then_inc(rstd_done, 1)

            def take(kind, u, s, t):
                n = u * NT + (NT * UNIT0[kind] + t)
                if isinstance(u, int) and u == 0 and t == 0:
                    act.wait_ge(rstd_done, NORM[kind] + 1)
                act.wait_ge(proj_done, n + 1)
                b = pj(u, t)
                bank, scale = ps[:, b, :], rstd_tok[:, t:t + 1]
                if kind == "A":
                    act.activation(qk[:, t, 5 * HD:6 * HD], bank[:, 4 * HD:5 * HD], ACT.Copy, scale=scale)
                    act.activation(qk[:, t, 0:5 * HD], bank[:, 0:5 * HD], ACT.Copy, scale=scale)
                else:
                    act.activation(qk[:, t, 0:2 * P], bank[:, 0:2 * P], ACT.Copy, scale=scale)
                dst, src = values(kind, v_hi, s, t, b)
                act.activation(dst, src, ACT.Copy, scale=scale).then_inc(proj_out, 1)

            def high_qk(kind, u, c):
                act.wait_ge(tr_done, fill_no(kind, u, c))
                act.activation(qt_hi[:, c, :], ps[:, qk_bank(u, c), :], ACT.Copy).then_inc(thi_done, 1)

            def high_p(kind, u, t):
                act.wait_ge(ptr_done, tile_no(kind, u, t))
                act.activation(*probs(kind, pt_hi, t), ACT.Copy).then_inc(phi_done, 1)

            def exps_a(u, t):
                lo = 0 if t else P
                act.wait_ge(nb_done, NT * u + t + 1)
                act.activation(es[:, t, :], sd[:, t, :], ACT.Exp)
                for h in range(4):
                    s = ps[:, s_bank(t) + h // 2, (h % 2) * 256 + lo:(h % 2 + 1) * 256]
                    ins = act.activation(prob[:, t % 2, h * 256 + lo:(h + 1) * 256], s, ACT.Exp,
                                         bias=nb[:, t, h:h + 1], scale=SCALE,
                                         accum_out=rowsum[:, t, h:h + 1])
                ins.then_inc(exp_done, 1)

            def exps_b(u, t):
                n = (t + 1) * P
                act.wait_ge(nb_done, u * NT + (NT * UNIT0["B"] + t + 1))
                for e in range(2):
                    ins = act.activation(prob[:, t % 2, e * T:e * T + n], ps[:, s_bank(t) + e, 0:n],
                                         ACT.Exp, bias=nb[:, t, e:e + 1], scale=SCALE,
                                         accum_out=rowsum[:, t, e:e + 1])
                ins.then_inc(exp_done, 1)

            act.wait_ge(ang_done, 1)
            act.activation(cos16[:, :, 0:HALF], angcos[:, :, :], ACT.Sin)
            act.activation(cos16[:, :, HALF:ROT], angcos[:, :, :], ACT.Sin)
            act.activation(sin16[:, :, 0:HALF], ang[:, :, :], ACT.Sin, scale=-1.0)
            act.activation(sin16[:, :, HALF:ROT], ang[:, :, :], ACT.Sin).then_inc(trig_done, 1)
            act.preload_act_table_set("natural_log_exp_and_others")

            def square_tokens(t):
                act.wait_ge(x_landed[t], 16)
                if t:
                    act.wait_ge(x_sq, t)
                act.activation(sq[:, :, :].rearrange("p a b -> p (a b)"), x_tok[:, t, :], ACT.Square,
                               accum_out=x_ss[:, t:t + 1]).then_inc(x_sq, 1)

            square_tokens(0)
            square_tokens(1)
            for kc in range(KC):
                gained(NORM["A"], kc, vecT[:, 0, R_ATTN + kc:R_ATTN + kc + 1])
                if kc == 0:
                    act.wait_ge(half_landed, 16 * 3)
                if kc < 4:
                    high("attnA", 0, 0, None, kc, wait=(kc == 2))
            square_tokens(2)
            square_tokens(3)
            act.wait_ge(const_done, CONSTS)
            act.wait_ge(x_sq, NT)
            rsqrt(NORM["A"], rstd_tok[:, :], x_ss[:, :], 1.0 / D)

            high("attnA", 1, 0, None, 0)
            for t in range(NT):
                take("A", 0, 0, t)
                if t < NT - 1:
                    high("attnA", 1, 0, None, t + 1)

            def first_scores(kind, exps):
                for c in range(QFILLS[kind]):
                    high_qk(kind, 0, c)
                exps(0, 0)
                take(kind, 1, 1, 0)
                if kind == "A":
                    act.wait_ge(lam_sum, 1)
                    act.activation(lam_s[:, 2:4], lam_s[:, 0:2], ACT.Exp).then_inc(lam_exp, 1)

            def high_out_a(u, t):
                act.wait_ge(pv_done, NT * u + t + 1)
                for e in range(2):
                    dst, src = outputs_a(ot_hi, u, t, e)
                    ins = act.activation(dst, src, ACT.Copy)
                ins.then_inc(ohi_done, 1)

            def weights(u, c):
                if u < UA - 1:
                    high_after("attnA", u, c)

            first_scores("A", exps_a)
            for u in range(UA):
                more, more2 = u + 1 < UA, u + 2 < UA
                high_p("A", u, 0)
                exps_a(u, 1)
                if more:
                    take("A", u + 1, (u + 1) % 2, 1)
                weights(u, 0)
                high_out_a(u, 0)
                weights(u, 1)
                high_p("A", u, 1)
                if more:
                    take("A", u + 1, (u + 1) % 2, 2)
                weights(u, 2)
                exps_a(u, 2)
                if more:
                    take("A", u + 1, (u + 1) % 2, 3)
                high_out_a(u, 1)
                weights(u, 3)
                if more:
                    high_qk("A", u + 1, 0)
                high_p("A", u, 2)
                if more:
                    high_qk("A", u + 1, 1)
                exps_a(u, 3)
                if more:
                    high_qk("A", u + 1, 2)
                if u == UA - 2:
                    high_whole("attnA", UA - 1)
                high_out_a(u, 2)
                high_p("A", u, 3)
                if more2:
                    take("A", u + 2, u % 2, 0)
                if more:
                    exps_a(u + 1, 0)
                high_out_a(u, 3)

            def after_out(l):
                ph, norm = ("outA", "outB")[l], NORM["F0"] if l == 0 else NORM["F1"]
                for b in range(OB):
                    for e in range(ODC):
                        dc = ODC * b + e
                        gained(norm, dc, vecT[:, l, R_FFN + dc:R_FFN + dc + 1])
                        square(norm, dc)
                        for c in range(2):
                            high_after(ph, b, 2 * e + c)
                rsqrt(norm, rstd[:, :], ps[:, TB, :])

            def high_u(l, s, f):
                act.wait_ge(u_done, f + (FB * l + 1))
                act.activation(u_hi[:, s, :], u_all[:, bass.ds(f, 1), :], ACT.Copy).then_inc(uhi_done, 1)

            def silu(l, s, f):
                act.wait_ge(conv_done, f + (FB * l + 1))
                act.activation(gated[:, s, :], conv[:, s, :], ACT.Silu).then_inc(silu_done, 1)

            def feed_forward(l):
                up, down = f"up{l}", f"down{l}"
                act.preload_act_table_set("silu_and_others")
                with act.Fori(0, FB // 2 - 1) as r:
                    for s in range(2):
                        high(up, s, r + 1, (up, r * 2 + s))
                        silu(l, s, r * 2 + s)
                for s in range(2):
                    high_whole(up, FB - 2 + s)
                    silu(l, s, FB - 2 + s)
                    high_u(l, s, s)
                with act.Fori(0, FB // 2 - 1) as r:
                    for s in range(2):
                        wait_used(act, down, r * 2 + s)
                        high_u(l, s, r * 2 + (s + 2))
                        for c in range(parts(down)):
                            high(down, s, r + 1, None, c)
                for dc in range(KC):
                    if l == 0:
                        gained(NORM["B"], dc, vecT[:, 1, R_ATTN + dc:R_ATTN + dc + 1])
                        if 3 <= dc < 7:
                            high_after(down, FB - 2, dc - 3)
                    else:
                        gained(NORM["end"], dc, vecT[:, 1, R_FINAL + dc:R_FINAL + dc + 1])
                        square(NORM["end"], dc)
                if l == 0:
                    for dc in range(KC):
                        square(NORM["B"], dc)
                    high_whole(down, FB - 1)
                act.preload_act_table_set("natural_log_exp_and_others")
                rsqrt(NORM["B"] if l == 0 else NORM["end"], rstd_tok[:, :], ps[:, OBK, 0:NT])

            after_out(0)
            feed_forward(0)

            def rsqrt_head(u):
                act.wait_ge(oms_done, u + 1)
                act.activation(rstd[:, :], ps[:, TB, :], ACT.Ln, bias=eps[:, :], scale=float(D // P))\
                   .then_inc(oln_done, 1)
                act.wait_ge(oln_done, u + 1)
                act.activation(rstd[:, :], rstd[:, :], ACT.Exp, scale=-0.5).then_inc(orstd_done, 1)

            def high_out_b(u):
                act.wait_ge(otmp_done, u + 1)
                act.activation(ot_hi[:, bass.ds(u, 1), :], htmp[:, 0, :], ACT.Copy).then_inc(ohi_done, 1)

            def unit_b(u, s, more=True, more2=True):
                before = not (isinstance(u, int) and u == 0)

                def weights(c):
                    if isinstance(u, int) and u == UB - 1:
                        return
                    if isinstance(u, int):
                        high_after("attnB", u, c)
                    else:
                        high("attnB", s, r + 1, ("attnB", u), c)

                high_p("B", u, 0)
                if before:
                    rsqrt_head(u - 1)
                exps_b(u, 1)
                if more:
                    take("B", u + 1, 1 - s, 1)
                if before:
                    high_out_b(u - 1)
                weights(0)
                weights(1)
                high_p("B", u, 1)
                if more:
                    take("B", u + 1, 1 - s, 2)
                weights(2)
                exps_b(u, 2)
                if more:
                    take("B", u + 1, 1 - s, 3)
                weights(3)
                if more:
                    high_qk("B", u + 1, 0)
                high_p("B", u, 2)
                exps_b(u, 3)
                if more:
                    high_qk("B", u + 1, 1)
                high_p("B", u, 3)
                if more:
                    exps_b(u + 1, 0)
                if isinstance(u, int) and u == UB - 2:
                    high_whole("attnB", UB - 1)
                act.wait_ge(pv_done, tile_no("B", u, NT - 1))
                act.activation(sq[:, 0, :], ps[:, OBK, :], ACT.Square).then_inc(osq_done, 1)
                if more2:
                    take("B", u + 2, s, 0)

            for t in range(NT):
                take("B", 0, 0, t)
            first_scores("B", exps_b)
            unit_b(0, 0)
            unit_b(1, 1)
            with act.Fori(1, UB // 2 - 1) as r:
                for s in range(2):
                    unit_b(r * 2 + s, s)
            unit_b(UB - 2, 0, more2=False)
            unit_b(UB - 1, 1, more=False, more2=False)
            rsqrt_head(UB - 1)
            high_out_b(UB - 1)
            after_out(1)
            feed_forward(1)
            act.wait_ge(rstd_done, NORM["end"] + 1)
            for b in range(0, 2 * NT, 2):
                act.wait_ge(y_tr, b + 1)
                act.activation(x_tok[:, b % NT, b // NT * (D // 2):(b // NT + 1) * (D // 2)], ps[:, b, :],
                               ACT.Copy, scale=rstd_tok[:, b % NT:b % NT + 1]).then_inc(y_act, 1)

        @block.vector
        def _(dve):
            own = Chain(dve, dve_self)

            def add_squares(norm, dc):
                n = KC * (norm - 1) + dc
                dve.wait_ge(sq_done, n + 1)
                if dc == 0:
                    dve.tensor_copy(ssacc[:, :], sq[:, 0, :]).then_inc(ss_done, 1)
                    return
                if n:
                    dve.wait_ge(ss_done, n)
                dve.tensor_tensor(ssacc[:, :], ssacc[:, :], sq[:, dc % 2, :], ALU.add)\
                   .then_inc(ss_done, 1)

            def low_h(norm, kc, gain):
                dve.wait_ge(hhi_done, KC * norm + kc + 1)
                dve.scalar_tensor_tensor(out=h_lo[:, kc, :], in0=xT[:, kc, :], scalar=gain,
                                         in1=h_hi[:, kc, :].bitcast(F32), op0=ALU.mult,
                                         op1=ALU.subtract).then_inc(hlo_done, 1)

            def rope(kind, u):
                nh = 6 if kind == "A" else 4
                x_ = qk[:, :, 0:nh * HD].rearrange("p t (h d) -> p t h d", h=nh)
                c = cos16[:, :, :].unsqueeze(2)
                s = sin16[:, :, :].unsqueeze(2)
                a, b = ropeA[:, :, 0:nh, :], ropeB[:, :, 0:nh, :]
                lo, hi = slice(0, HALF), slice(HALF, ROT)
                dve.wait_ge(proj_out, u * NT + (NT * (UNIT0[kind] + 1)))
                own.mark(dve.tensor_tensor(a, x_[:, :, :, 0:ROT], c.broadcast_to((P, NT, nh, ROT)), ALU.mult))
                own.mark(dve.tensor_tensor(b[:, :, :, lo], x_[:, :, :, hi],
                                           s[:, :, :, lo].broadcast_to((P, NT, nh, HALF)), ALU.mult))
                own.link(dve.tensor_tensor(b[:, :, :, hi], x_[:, :, :, lo],
                                           s[:, :, :, hi].broadcast_to((P, NT, nh, HALF)), ALU.mult))
                dve.tensor_tensor(x_[:, :, :, 0:ROT], a, b, ALU.add).then_inc(rope_done, 1)

            def low_v(kind, u, s, t):
                dve.wait_ge(proj_out, u * NT + (NT * UNIT0[kind] + t + 1))
                b = pj(u, t)
                dst, src = values(kind, v_lo, s, t, b)
                dve.scalar_tensor_tensor(out=dst, in0=src, scalar=rstd_tok[:, t:t + 1],
                                         in1=values(kind, v_hi, s, t, b)[0].bitcast(F32), op0=ALU.mult,
                                         op1=ALU.subtract).then_inc(vlo_done, 1)

            def low_qk(kind, u, c):
                dve.wait_ge(thi_done, fill_no(kind, u, c))
                dve.tensor_tensor(qt_lo[:, c, :], ps[:, qk_bank(u, c), :], qt_hi[:, c, :].bitcast(F32),
                                  ALU.subtract).then_inc(tlo_done, 1)

            def low_p(kind, u, t):
                dve.wait_ge(phi_done, tile_no(kind, u, t))
                dst, src = probs(kind, pt_lo, t)
                dve.tensor_tensor(dst, src, probs(kind, pt_hi, t)[0].bitcast(F32), ALU.subtract)\
                   .then_inc(plo_done, 1)

            def maxima_a(u, t):
                lo = 0 if t else P
                s = ps[:, s_bank(t):s_bank(t) + 2, :].rearrange("p b (h k) -> p (b h) k", h=2)
                sink = nsink[:, 4 * u:4 * u + 4]
                dve.wait_ge(s_done, NT * u + t + 1)
                own.link(dve.tensor_reduce(den[:, t, :], s[:, :, lo:], AX.X, ALU.max, negate=True))
                own.link(dve.scalar_tensor_tensor(out=nb[:, t, :], in0=den[:, t, :], scalar=SCALE,
                                                  in1=sink, op0=ALU.mult, op1=ALU.min))
                dve.tensor_tensor(sd[:, t, :], nb[:, t, :], sink, ALU.subtract).then_inc(nb_done, 1)

            def divide_a(u, t):
                lo = 0 if t else P
                dve.wait_ge(exp_done, NT * u + t + 1)
                own.link(dve.tensor_tensor(den[:, t, :], rowsum[:, t, :], es[:, t, :], ALU.add))
                own.link(dve.reciprocal(rden[:, t, :], den[:, t, :]))
                p = prob[:, t % 2, :].rearrange("p (h k) -> p h k", h=4)[:, :, lo:]
                r = rden[:, t, :].unsqueeze(2).broadcast_to((P, 4, 256 - lo))
                dve.tensor_tensor(p, p, r, ALU.mult).then_inc(p_done, 1)

            def maxima_b(u, t):
                n = (t + 1) * P
                dve.wait_ge(s_done, u * NT + (NT * UNIT0["B"] + t + 1))
                own.link(dve.tensor_reduce(den[:, t, 0:2], ps[:, s_bank(t):s_bank(t) + 2, 0:n], AX.X,
                                           ALU.max, negate=True))
                dve.tensor_scalar(nb[:, t, 0:2], den[:, t, 0:2], SCALE, None, ALU.mult)\
                   .then_inc(nb_done, 1)

            def combine_b(u, t):
                n = (t + 1) * P
                dve.wait_ge(exp_done, u * NT + (NT * UNIT0["B"] + t + 1))
                own.link(dve.reciprocal(rden[:, t, 0:2], rowsum[:, t, 0:2]))
                own.link(dve.tensor_scalar(rden[:, t, 2:3], rden[:, t, 1:2], neglam[:, :], None, ALU.mult))
                p0, p1 = prob[:, t % 2, 0:n], prob[:, t % 2, T:T + n]
                own.link(dve.tensor_scalar(p1, p1, rden[:, t, 2:3], None, ALU.mult))
                dve.scalar_tensor_tensor(out=p0, in0=p0, scalar=rden[:, t, 0:1], in1=p1, op0=ALU.mult,
                                         op1=ALU.add).then_inc(p_done, 1)

            dve.wait_ge(pos_landed, 16)
            dve.tensor_copy(pos_f[:, :], pos_i[:, :]).then_inc(pos_done, 1)
            dve.wait_ge(posT_tr, 1)
            dve.tensor_copy(posT[:, :], ps[:, 7, 0:NT]).then_inc(posT_done, 1)

            dve.wait_ge(posT_done, 1)
            dve.wait_ge(const_done, 1 + HALF)
            own.link(dve.tensor_tensor(ang[:, :, :], posT[:, :].unsqueeze(2).broadcast_to((P, NT, HALF)),
                                       invf[:, :].unsqueeze(1).broadcast_to((P, NT, HALF)), ALU.mult))
            own.link(dve.tensor_scalar(turns[:, :, :], ang[:, :, :], 1.0 / (2 * math.pi), ROUND,
                                       ALU.mult, ALU.add))
            own.link(dve.tensor_scalar(turns[:, :, :], turns[:, :, :], ROUND, None, ALU.subtract))
            for part in TWO_PI_PARTS:
                own.link(dve.scalar_tensor_tensor(out=ang[:, :, :], in0=turns[:, :, :], scalar=-part,
                                                  in1=ang[:, :, :], op0=ALU.mult, op1=ALU.add))
            own.link(dve.tensor_scalar(ang[:, :, :], ang[:, :, :], PI_BELOW, -PI_BELOW, ALU.min, ALU.max))
            own.link(dve.tensor_scalar(angneg[:, :, :], ang[:, :, :], -1.0, None, ALU.mult))
            own.link(dve.tensor_tensor(angneg[:, :, :], ang[:, :, :], angneg[:, :, :], ALU.max))
            dve.tensor_scalar(angcos[:, :, :], angneg[:, :, :], -1.0, math.pi / 2, ALU.mult, ALU.add)\
               .then_inc(ang_done, 1)
            dve.wait_ge(posT_tr, 2)
            dve.tensor_copy(vecT[:, 0, R_ATTN:R_ATTN + KC], ps[:, 6, 0:KC]).then_inc(posT_done, 1)
            dve.wait_ge(posT_done, 2)
            for kc in range(KC + 2):
                if kc < KC:
                    dve.wait_ge(x_tr, kc + 1)
                    dve.tensor_copy(xT[:, kc, :], ps[:, kc, :]).then_inc(x_ready, 1)
                if kc >= 2:
                    low_h(NORM["A"], kc - 2, vecT[:, 0, R_ATTN + kc - 2:R_ATTN + kc - 1])

            def little_vectors():
                dve.wait_ge(vecT_tr, 1)
                dve.tensor_copy(vecT[:, 0, 0:R_ATTN], ps[:, TB, 0:R_ATTN])
                dve.tensor_copy(vecT[:, 0, R_FFN:R_FINAL], ps[:, TB, R_FFN:R_FINAL]).then_inc(vecT_done, 1)
                dve.tensor_copy(vecT[:, 1, :], ps[:, TB, P:P + R_ALL]).then_inc(vecT_done, 1)
                dve.wait_ge(sink_landed, 16)
                own.link(dve.tensor_scalar(nsink[:, :].rearrange("p (u e c) -> p u e c", u=UA, e=2),
                                           sink_in[:, :].rearrange("p (u c e) -> p u e c", u=UA, e=2),
                                           -1.0, None, ALU.mult))

            def lambda_sums():
                dve.wait_ge(lam_landed, 64)
                for i in range(2):
                    ins = dve.tensor_tensor_reduce(lam[:, 2 * i, :], lam[:, 2 * i, :], lam[:, 2 * i + 1, :],
                                                   1.0, 0.0, ALU.mult, ALU.add, lam_s[:, i:i + 1])
                    if i == 0:
                        own.mark(ins)
                ins.then_inc(lam_sum, 1)

            def lambda_of_sums():
                dve.wait_ge(lam_exp, 1)
                own.link(dve.tensor_tensor(neglam[:, :], lam_s[:, 3:4], lam_s[:, 2:3], ALU.subtract))
                own.link(dve.tensor_scalar(neglam[:, :], neglam[:, :], LAMBDA_INIT, None, ALU.subtract))
                own.link(dve.tensor_scalar(gainB[:, :], vecT[:, 1, R_SUBLN:R_SUBLN + 1], 1.0 - LAMBDA_INIT,
                                           None, ALU.mult))

            def first_scores(kind, maxima, divide):
                for t in range(NT):
                    low_v(kind, 0, 0, t)
                if kind == "A":
                    dve.wait_ge(trig_done, 1)
                rope(kind, 0)
                if kind == "A":
                    little_vectors()
                for c in range(QFILLS[kind]):
                    low_qk(kind, 0, c)
                maxima(0, 0)
                maxima(0, 1)
                if kind == "A":
                    lambda_sums()
                divide(0, 0)
                low_v(kind, 1, 1, 0)
                if kind == "A":
                    lambda_of_sums()

            def low_out_a(u, t):
                dve.wait_ge(ohi_done, NT * u + t + 1)
                for e in range(2):
                    dst, src = outputs_a(ot_lo, u, t, e)
                    ins = dve.tensor_tensor(dst, src, outputs_a(ot_hi, u, t, e)[0].bitcast(F32),
                                            ALU.subtract)
                    if e == 0:
                        own.mark(ins)
                ins.then_inc(olo_done, 1)

            first_scores("A", maxima_a, divide_a)
            for u in range(UA):
                more, more2 = u + 1 < UA, u + 2 < UA
                low_p("A", u, 0)
                divide_a(u, 1)
                if more:
                    low_v("A", u + 1, (u + 1) % 2, 1)
                low_out_a(u, 0)
                maxima_a(u, 2)
                low_p("A", u, 1)
                if more:
                    low_v("A", u + 1, (u + 1) % 2, 2)
                divide_a(u, 2)
                if more:
                    low_v("A", u + 1, (u + 1) % 2, 3)
                    rope("A", u + 1)
                low_out_a(u, 1)
                maxima_a(u, 3)
                if more:
                    low_qk("A", u + 1, 0)
                low_p("A", u, 2)
                if more:
                    low_qk("A", u + 1, 1)
                divide_a(u, 3)
                if more:
                    low_qk("A", u + 1, 2)
                low_out_a(u, 2)
                if more:
                    maxima_a(u + 1, 0)
                low_p("A", u, 3)
                if more2:
                    low_v("A", u + 2, u % 2, 0)
                if more:
                    divide_a(u + 1, 0)
                low_out_a(u, 3)
                if more:
                    maxima_a(u + 1, 1)

            def add_to_stream(norm, done, n, banks, gain):
                late = KC + 1 if norm == NORM["B"] else 2 if gain else 1
                for dc in range(KC + late):
                    if dc < KC:
                        dve.wait_ge(done, n + dc + 1)
                        dve.tensor_tensor(xT[:, dc, :], xT[:, dc, :], ps[:, banks[dc % len(banks)], :],
                                          ALU.add).then_inc(x_ready, 1)
                    if gain and 1 <= dc <= KC:
                        low_h(norm, dc - 1, vecT[:, gain[0], gain[1] + dc - 1:gain[1] + dc])
                    if dc >= late:
                        add_squares(norm, dc - late)

            def after_out(l):
                add_to_stream(NORM["F0"] if l == 0 else NORM["F1"], oproj_done, KC * l, OUT_BANKS[l],
                              (l, R_FFN))

            def low_u(l, s, f):
                dve.wait_ge(uhi_done, f + (FB * l + 1))
                dve.tensor_tensor(u_lo[:, s, :], u_all[:, bass.ds(f, 1), :].rearrange("p a b -> p (a b)"),
                                  u_hi[:, s, :].bitcast(F32), ALU.subtract).then_inc(ulo_done, 1)

            def gate(l, s, f):
                def w(row):
                    return vecT[:, l, bass.ds(f + row, 1)]
                a, c = normed[:, s, :], conv[:, s, :]
                dve.wait_ge(up_done, f + (FB * l + 1))
                own.link(dve.tensor_tensor(a, ps[:, 2 * s, :], rstd[:, :], ALU.mult))
                own.link(dve.tensor_scalar(c, a, w(R_CONVW + 2 * FB), w(R_CONVB), ALU.mult, ALU.add))
                own.link(dve.scalar_tensor_tensor(out=c[:, 1:], in0=a[:, 0:T - 1], scalar=w(R_CONVW + FB),
                                                  in1=c[:, 1:], op0=ALU.mult, op1=ALU.add))
                dve.scalar_tensor_tensor(out=c[:, 2:], in0=a[:, 0:T - 2], scalar=w(R_CONVW),
                                         in1=c[:, 2:], op0=ALU.mult, op1=ALU.add).then_inc(conv_done, 1)
                dve.wait_ge(conv_done, f + (FB * l + 1))
                own.link(dve.tensor_tensor(a, ps[:, 2 * s + 1, :], rstd[:, :], ALU.mult))
                dve.wait_ge(silu_done, f + (FB * l + 1))
                dve.tensor_tensor(u_all[:, bass.ds(f, 1), :].rearrange("p a b -> p (a b)"), gated[:, s, :],
                                  a, ALU.mult).then_inc(u_done, 1)

            def feed_forward(l):
                dve.wait_ge(rstd_done, (NORM["F0"] if l == 0 else NORM["F1"]) + 1)
                with dve.Fori(0, FB // 2 - 1) as r:
                    own.enter(r, 8)
                    for s in range(2):
                        gate(l, s, r * 2 + s)
                own.leave(FB // 2 - 1)
                for s in range(2):
                    gate(l, s, FB - 2 + s)
                    low_u(l, s, s)
                with dve.Fori(0, FB // 2 - 1) as r:
                    for s in range(2):
                        low_u(l, s, r * 2 + (s + 2))
                if l == 0:
                    add_to_stream(NORM["B"], down_done, 0, range(KC), (1, R_ATTN))
                else:
                    add_to_stream(NORM["end"], down_done, KC, range(KC), None)

            after_out(0)
            feed_forward(0)

            def norm_head(u):
                dve.wait_ge(orstd_done, u + 1)
                dve.scalar_tensor_tensor(out=htmp[:, 0, :], in0=ps[:, OBK, :], scalar=gainB[:, :],
                                         in1=rstd[:, :], op0=ALU.mult, op1=ALU.mult).then_inc(otmp_done, 1)

            def low_out_b(u):
                dve.wait_ge(ohi_done, u + (NT * UA + 1))
                dve.tensor_tensor(ot_lo[:, bass.ds(u, 1), :].rearrange("p a b -> p (a b)"), htmp[:, 0, :],
                                  ot_hi[:, bass.ds(u, 1), :].rearrange("p a b -> p (a b)").bitcast(F32),
                                  ALU.subtract).then_inc(olo_done, 1)

            def unit_b(u, s, more=True, more2=True):
                before = not (isinstance(u, int) and u == 0)
                low_p("B", u, 0)
                if before:
                    norm_head(u - 1)
                combine_b(u, 1)
                if more:
                    low_v("B", u + 1, 1 - s, 1)
                if before:
                    low_out_b(u - 1)
                maxima_b(u, 2)
                low_p("B", u, 1)
                if more:
                    low_v("B", u + 1, 1 - s, 2)
                combine_b(u, 2)
                if more:
                    low_v("B", u + 1, 1 - s, 3)
                    rope("B", u + 1)
                maxima_b(u, 3)
                if more:
                    low_qk("B", u + 1, 0)
                low_p("B", u, 2)
                if more:
                    low_qk("B", u + 1, 1)
                combine_b(u, 3)
                if more:
                    maxima_b(u + 1, 0)
                low_p("B", u, 3)
                if more:
                    combine_b(u + 1, 0)
                    maxima_b(u + 1, 1)
                if more2:
                    low_v("B", u + 2, s, 0)

            first_scores("B", maxima_b, combine_b)
            unit_b(0, 0)
            unit_b(1, 1)
            with dve.Fori(1, UB // 2 - 1) as r:
                own.enter(r, PER_UNIT_B * 2, 1)
                for s in range(2):
                    unit_b(r * 2 + s, s)
            own.leave(UB // 2 - 1)
            unit_b(UB - 2, 0, more2=False)
            unit_b(UB - 1, 1, more=False, more2=False)
            norm_head(UB - 1)
            low_out_b(UB - 1)
            after_out(1)
            feed_forward(1)
            dve.wait_ge(rstd_done, NORM["end"] + 1)
            for b in range(1, 2 * NT, 2):
                dve.wait_ge(y_tr, b + 1)
                dve.tensor_scalar(x_tok[:, b % NT, b // NT * (D // 2):(b // NT + 1) * (D // 2)], ps[:, b, :],
                                  rstd_tok[:, b % NT:b % NT + 1], None, ALU.mult).then_inc(y_dve, 1)


def inv_freq(i):
    import numpy as np
    return float(np.power(np.float32(THETA), np.float32(-2.0 * i / ROT), dtype=np.float32))


_INS = ["x", "positions", "attn_norm", "ffn_norm", "ffn_w_up", "ffn_conv_w", "ffn_conv_b", "ffn_w_down",
        "a_w_in", "a_sinks", "a_w_out", "b_w_in", "b_lam_q1", "b_lam_k1", "b_lam_q2", "b_lam_k2",
        "b_subln", "b_w_out", "final_norm"]


def kernel(**inputs):
    import numpy as _np
    import concourse.bacc as _bacc
    from concourse import mybir as _mybir
    from concourse.bass_utils import run_bass_kernel_spmd as _run

    nc = _bacc.Bacc("TRN2", target_bir_lowering=False, num_devices=1)
    arrays, args = {}, []
    for name in _INS:
        a = _np.ascontiguousarray(inputs[name])
        arrays[f"in_{name}"] = a
        args.append(nc.dram_tensor(f"in_{name}", a.shape, _mybir.dt.from_np(a.dtype),
                                   kind="ExternalInput").ap())
    args.append(nc.dram_tensor("out_0", (1, T, D), _mybir.dt.float32, kind="ExternalOutput").ap())
    trunk(nc, *args)
    r = _run(nc, [arrays], core_ids=[0])
    return r.results[0]["out_0"]
```
